# Optimizing a Trainium2 kernel written in Bass

```python
import math
import jax, jax.numpy as jnp
from jax import lax
import numpy as np

D_MODEL = 1024
BATCH = 1
SEQ = 512
DEPTH = 2

CHUNK = 64
PLE_DIM = 256
N_BRANCH = 4
BRANCH_WIDTH = 512
S5_GROUPS = 32
S5_GROUP_CH = 16
S5_WIDTH = S5_GROUPS * S5_GROUP_CH
S5_STATE = 64
SWA_Q_HEADS = 8
SWA_KV_HEADS = 2
SWA_HEAD_DIM = 64
SWA_WIDTH = SWA_Q_HEADS * SWA_HEAD_DIM
SWA_WINDOW = 128
SWA_WIN_CHUNKS = SWA_WINDOW // CHUNK
GLA_HEADS = 4
GLA_DK = 64
GLA_DV = 128
GLA_WIDTH = GLA_HEADS * GLA_DV
GLA_GATE_RANK = 16
GLA_GATE_TAU = 16.0
MLA_HEADS = 4
MLA_Q_LORA = 256
MLA_KV_LORA = 128
MLA_NOPE = 128
MLA_ROPE = 64
MLA_V = 128
MLA_WIDTH = MLA_HEADS * MLA_V
MLA_Q_BLOCK = 128
ROPE_THETA = 10000.0
N_EXPERTS = 64
TOP_K = 8
EXPERT_FF = 256
SHARED_FF = 256
ROUTED_SCALE = 2.5
MOE_BLOCK = 128
DN_ALPHA = (2 * DEPTH) ** 0.25
DN_BETA = (8 * DEPTH) ** -0.25
LN_EPS = 1e-5
RMS_EPS = 1e-6
NEG_INF = -1e30

IN_SIZES = (
    S5_WIDTH,
    SWA_Q_HEADS * SWA_HEAD_DIM,
    SWA_KV_HEADS * SWA_HEAD_DIM,
    SWA_KV_HEADS * SWA_HEAD_DIM,
    GLA_HEADS * GLA_DK,
    GLA_HEADS * GLA_DK,
    GLA_HEADS * GLA_DV,
    GLA_HEADS * GLA_DV,
    GLA_GATE_RANK,
    MLA_Q_LORA,
    MLA_KV_LORA,
    MLA_ROPE,
    N_BRANCH * D_MODEL,
)
N_IN = sum(IN_SIZES)

kernel_name = 'hybrid_s5_swa_gla_mla_moe_deepnorm'

def _layer_norm(x, g, b):
    xf = x.astype(jnp.float32)
    mu = xf.mean(-1, keepdims=True)
    var = jnp.mean(jnp.square(xf - mu), -1, keepdims=True)
    y = (xf - mu) * lax.rsqrt(var + LN_EPS) * g.astype(jnp.float32) + b.astype(jnp.float32)
    return y.astype(x.dtype)

def _rms_norm(x, g):
    xf = x.astype(jnp.float32)
    y = xf * lax.rsqrt(jnp.mean(jnp.square(xf), -1, keepdims=True) + RMS_EPS) * g.astype(jnp.float32)
    return y.astype(x.dtype)

def _alibi_slopes(n_heads):
    return 2.0 ** (-8.0 * jnp.arange(1, n_heads + 1, dtype=jnp.float32) / n_heads)

def _rope(x, pos):
    half = x.shape[-1] // 2
    inv = ROPE_THETA ** (-jnp.arange(half, dtype=jnp.float32) / half)
    ang = pos.astype(jnp.float32)[:, None] * inv
    cos = jnp.cos(ang)[:, None, :]
    sin = jnp.sin(ang)[:, None, :]
    xf = x.astype(jnp.float32)
    x1, x2 = xf[..., :half], xf[..., half:]
    return jnp.concatenate([x1 * cos - x2 * sin, x1 * sin + x2 * cos], -1).astype(x.dtype)

def _s5_mixer(u, a_re, a_im, log_dt, b_re, b_im, c_re, c_im, d_skip, w_glu):
    f32 = jnp.float32
    bsz, seq, _ = u.shape
    ug = u.astype(f32).reshape(bsz, seq, S5_GROUPS, S5_GROUP_CH)
    lam = lax.complex(a_re.astype(f32), a_im.astype(f32))
    dt = jnp.exp(log_dt.astype(f32))[:, None]
    lam_bar = jnp.exp(lam * dt)
    b_c = lax.complex(b_re.astype(f32), b_im.astype(f32))
    b_bar = ((lam_bar - 1.0) / lam)[..., None] * b_c
    c_c = lax.complex(c_re.astype(f32), c_im.astype(f32))
    bu = jnp.einsum('bsgc,gpc->bsgp', ug.astype(jnp.complex64), b_bar)
    a_seq = jnp.broadcast_to(lam_bar, bu.shape)

    def combine(left, right):
        a_l, b_l = left
        a_r, b_r = right
        return a_l * a_r, a_r * b_l + b_r

    _, states = lax.associative_scan(combine, (a_seq, bu), axis=1)
    y = jnp.einsum('bsgp,gcp->bsgc', states, c_c).real + d_skip.astype(f32) * ug
    y = jax.nn.gelu(y.reshape(bsz, seq, S5_WIDTH)).astype(u.dtype)
    return y * jax.nn.sigmoid(y @ w_glu)

def _swa_mixer(q, k, v, sinks):
    f32 = jnp.float32
    bsz, seq, _ = q.shape
    n_chunks = seq // CHUNK
    rep = SWA_Q_HEADS // SWA_KV_HEADS
    band = SWA_WIN_CHUNKS * CHUNK
    qc = q.reshape(bsz, n_chunks, CHUNK, SWA_KV_HEADS, rep, SWA_HEAD_DIM)
    kc = k.reshape(bsz, n_chunks, CHUNK, SWA_KV_HEADS, SWA_HEAD_DIM)
    vc = v.reshape(bsz, n_chunks, CHUNK, SWA_KV_HEADS, SWA_HEAD_DIM)
    pad = ((0, 0), (SWA_WIN_CHUNKS - 1, 0), (0, 0), (0, 0), (0, 0))
    kp = jnp.pad(kc, pad)
    vp = jnp.pad(vc, pad)
    kb = jnp.concatenate([kp[:, j:j + n_chunks] for j in range(SWA_WIN_CHUNKS)], axis=2)
    vb = jnp.concatenate([vp[:, j:j + n_chunks] for j in range(SWA_WIN_CHUNKS)], axis=2)
    scores = jnp.einsum('bcqgrd,bckgd->bgrcqk', qc, kb, preferred_element_type=f32) * (SWA_HEAD_DIM ** -0.5)
    qi = jnp.arange(CHUNK)[:, None]
    kj = jnp.arange(band)[None, :]
    dist = jnp.abs(qi - kj + (SWA_WIN_CHUNKS - 1) * CHUNK).astype(f32)
    slopes = _alibi_slopes(SWA_Q_HEADS).reshape(SWA_KV_HEADS, rep)
    scores = scores - slopes[:, :, None, None, None] * dist
    key_chunk = jnp.arange(n_chunks)[:, None] + kj // CHUNK - (SWA_WIN_CHUNKS - 1)
    scores = jnp.where((key_chunk >= 0)[:, None, :], scores, NEG_INF)
    sink = sinks.astype(f32).reshape(SWA_KV_HEADS, rep)[:, :, None, None, None]
    m = jnp.maximum(scores.max(-1, keepdims=True), sink)
    pr = jnp.exp(scores - m)
    denom = pr.sum(-1, keepdims=True) + jnp.exp(sink - m)
    out = jnp.einsum('bgrcqk,bckgd->bcqgrd', (pr / denom).astype(v.dtype), vb)
    return out.reshape(bsz, seq, SWA_WIDTH)

def _gla_mixer(q, k, v, g_out, g_lr, w_lr2, b_lr, norm_g):
    f32 = jnp.float32
    bsz, seq, _ = q.shape
    n_chunks = seq // CHUNK
    shp = (bsz, n_chunks, CHUNK, GLA_HEADS, -1)
    qc = q.astype(f32).reshape(shp) * (GLA_DK ** -0.5)
    kc = k.astype(f32).reshape(shp)
    vc = v.astype(f32).reshape(shp)
    log_a = jax.nn.log_sigmoid((g_lr @ w_lr2 + b_lr).astype(f32)) / GLA_GATE_TAU
    bcum = jnp.cumsum(log_a.reshape(shp), axis=2)
    b_last = bcum[:, :, -1:]
    q_dec = qc * jnp.exp(bcum)
    k_inv = kc * jnp.exp(-bcum)
    causal = jnp.tril(jnp.ones((CHUNK, CHUNK), dtype=bool))
    att = jnp.where(causal, jnp.einsum('bcqhk,bcshk->bchqs', q_dec, k_inv), 0.0)
    o_intra = jnp.einsum('bchqs,bcshv->bcqhv', att, vc)
    chunk_kv = jnp.einsum('bcshk,bcshv->bchkv', kc * jnp.exp(b_last - bcum), vc)
    chunk_decay = jnp.exp(b_last[:, :, 0])

    def step(state, inp):
        dec, kv = inp
        return dec[..., None] * state + kv, state

    init = jnp.zeros((bsz, GLA_HEADS, GLA_DK, GLA_DV), f32)
    _, s_prev = lax.scan(step, init, (jnp.moveaxis(chunk_decay, 1, 0), jnp.moveaxis(chunk_kv, 1, 0)))
    s_prev = jnp.moveaxis(s_prev, 0, 1)
    o = o_intra + jnp.einsum('bcqhk,bchkv->bcqhv', q_dec, s_prev)
    mu = o.mean(-1, keepdims=True)
    var = jnp.mean(jnp.square(o - mu), -1, keepdims=True)
    o = ((o - mu) * lax.rsqrt(var + LN_EPS)).reshape(bsz, seq, GLA_WIDTH) * norm_g.astype(f32)
    return (o * jax.nn.silu(g_out.astype(f32))).astype(q.dtype)

def _mla_mixer(q_down, kv_down, k_rope, q_norm_g, w_uq, kv_norm_g, w_ukv):
    f32 = jnp.float32
    bsz, seq, _ = q_down.shape
    pos = jnp.arange(seq)
    q = (_rms_norm(q_down, q_norm_g) @ w_uq).reshape(bsz, seq, MLA_HEADS, MLA_NOPE + MLA_ROPE)
    kv = (_rms_norm(kv_down, kv_norm_g) @ w_ukv).reshape(bsz, seq, MLA_HEADS, MLA_NOPE + MLA_V)
    q_pe = _rope(q[..., MLA_NOPE:], pos)
    k_pe = _rope(k_rope[:, :, None, :], pos)
    qh = jnp.concatenate([q[..., :MLA_NOPE], q_pe], -1)
    kh = jnp.concatenate([kv[..., :MLA_NOPE], jnp.broadcast_to(k_pe, (bsz, seq, MLA_HEADS, MLA_ROPE))], -1)
    vh = kv[..., MLA_NOPE:]
    scale = (MLA_NOPE + MLA_ROPE) ** -0.5
    n_blocks = seq // MLA_Q_BLOCK
    q_blocks = jnp.moveaxis(qh.reshape(bsz, n_blocks, MLA_Q_BLOCK, MLA_HEADS, -1), 1, 0)
    key_chunk = pos // CHUNK

    def attend(args):
        qb, blk = args
        q_chunk = (blk * MLA_Q_BLOCK + jnp.arange(MLA_Q_BLOCK)) // CHUNK
        allowed = key_chunk[None, :] <= q_chunk[:, None]
        s = jnp.einsum('bqhd,bkhd->bhqk', qb, kh, preferred_element_type=f32) * scale
        pr = jax.nn.softmax(jnp.where(allowed, s, NEG_INF), axis=-1).astype(vh.dtype)
        return jnp.einsum('bhqk,bkhd->bqhd', pr, vh)

    out = lax.map(attend, (q_blocks, jnp.arange(n_blocks)))
    return jnp.moveaxis(out, 0, 1).reshape(bsz, seq, MLA_WIDTH)

def _routed_experts(x2d, top_idx, top_w, w_gate, w_up, w_down):
    n_tok, d = x2d.shape
    n_assign = n_tok * TOP_K
    n_pad = n_assign + N_EXPERTS * MOE_BLOCK
    n_blocks = n_pad // MOE_BLOCK
    e_flat = top_idx.reshape(-1)
    order = jnp.argsort(e_flat)
    e_sorted = e_flat[order]
    counts = jnp.bincount(e_flat, length=N_EXPERTS)
    padded = (counts + MOE_BLOCK - 1) // MOE_BLOCK * MOE_BLOCK
    pad_end = jnp.cumsum(padded)
    pad_start = pad_end - padded
    grp_start = jnp.cumsum(counts) - counts
    dest = pad_start[e_sorted] + jnp.arange(n_assign) - grp_start[e_sorted]
    row_tok = jnp.zeros((n_pad,), jnp.int32).at[dest].set((order // TOP_K).astype(jnp.int32))
    row_w = jnp.zeros((n_pad,), top_w.dtype).at[dest].set(top_w.reshape(-1)[order])
    block_e = jnp.minimum(jnp.searchsorted(pad_end, jnp.arange(n_blocks) * MOE_BLOCK, side='right'), N_EXPERTS - 1)

    def expert_block(args):
        toks, wts, e = args
        xs = x2d[toks]
        h = jax.nn.silu(xs @ w_gate[e]) * (xs @ w_up[e])
        return (h @ w_down[e]) * wts[:, None]

    yb = lax.map(expert_block, (row_tok.reshape(n_blocks, MOE_BLOCK), row_w.reshape(n_blocks, MOE_BLOCK), block_e))
    return jax.ops.segment_sum(yb.reshape(n_pad, d), row_tok, num_segments=n_tok)

def _moe(x2d, router_w, router_bias, w_gate, w_up, w_down, sh_gate, sh_up, sh_down):
    f32 = jnp.float32
    scores = jax.nn.sigmoid(jnp.dot(x2d, router_w, preferred_element_type=f32))
    _, top_idx = lax.top_k(scores + router_bias.astype(f32), TOP_K)
    top_s = jnp.take_along_axis(scores, top_idx, axis=-1)
    top_w = (top_s / top_s.sum(-1, keepdims=True) * ROUTED_SCALE).astype(x2d.dtype)
    routed = _routed_experts(x2d, top_idx, top_w, w_gate, w_up, w_down)
    shared = (jax.nn.silu(x2d @ sh_gate) * (x2d @ sh_up)) @ sh_down
    return routed + shared

def setup_inputs(seed: int = 0) -> dict:
    key = jax.random.key(seed)
    keys = iter(list(jax.random.split(key, 40)))
    f32 = jnp.float32
    L = DEPTH
    D = D_MODEL

    def nrm(shape, scale):
        return jax.random.normal(next(keys), shape, f32) * scale

    def gain(shape):
        return 1.0 + nrm(shape, 0.02)

    inv_sqrt2 = 0.5 ** 0.5
    return {
        'x': nrm((BATCH, SEQ, D), 1.0),
        'p': nrm((DEPTH, BATCH, SEQ, PLE_DIM), 1.0),
        'w_in': nrm((L, D, N_IN), D ** -0.5),
        's5_a_re': -0.5 + nrm((L, S5_GROUPS, S5_STATE), 0.01),
        's5_a_im': jnp.pi * jnp.arange(S5_STATE, dtype=f32) + nrm((L, S5_GROUPS, S5_STATE), 0.01),
        's5_log_dt': jax.random.uniform(next(keys), (L, S5_GROUPS), f32, math.log(1e-3), math.log(1e-1)),
        's5_b_re': nrm((L, S5_GROUPS, S5_STATE, S5_GROUP_CH), inv_sqrt2 * S5_GROUP_CH ** -0.5),
        's5_b_im': nrm((L, S5_GROUPS, S5_STATE, S5_GROUP_CH), inv_sqrt2 * S5_GROUP_CH ** -0.5),
        's5_c_re': nrm((L, S5_GROUPS, S5_GROUP_CH, S5_STATE), inv_sqrt2 * S5_STATE ** -0.5),
        's5_c_im': nrm((L, S5_GROUPS, S5_GROUP_CH, S5_STATE), inv_sqrt2 * S5_STATE ** -0.5),
        's5_d': nrm((L, S5_GROUPS, S5_GROUP_CH), 1.0),
        's5_w_glu': nrm((L, S5_WIDTH, S5_WIDTH), S5_WIDTH ** -0.5),
        'swa_sinks': nrm((L, SWA_Q_HEADS), 1.0),
        'gla_w_lr2': nrm((L, GLA_GATE_RANK, GLA_HEADS * GLA_DK), GLA_GATE_RANK ** -0.5),
        'gla_b_lr': nrm((L, GLA_HEADS * GLA_DK), 0.1),
        'gla_norm_g': gain((L, GLA_WIDTH)),
        'mla_q_norm_g': gain((L, MLA_Q_LORA)),
        'mla_w_uq': nrm((L, MLA_Q_LORA, MLA_HEADS * (MLA_NOPE + MLA_ROPE)), MLA_Q_LORA ** -0.5),
        'mla_kv_norm_g': gain((L, MLA_KV_LORA)),
        'mla_w_ukv': nrm((L, MLA_KV_LORA, MLA_HEADS * (MLA_NOPE + MLA_V)), MLA_KV_LORA ** -0.5),
        'w_branch': nrm((L, N_BRANCH, BRANCH_WIDTH, D), BRANCH_WIDTH ** -0.5),
        'w_out': nrm((L, D, D), DN_BETA * D ** -0.5),
        'ln1_g': gain((L, D)),
        'ln1_b': nrm((L, D), 0.02),
        'router_w': nrm((L, D, N_EXPERTS), D ** -0.5),
        'router_bias': nrm((L, N_EXPERTS), 0.01),
        'exp_w_gate': nrm((L, N_EXPERTS, D, EXPERT_FF), D ** -0.5),
        'exp_w_up': nrm((L, N_EXPERTS, D, EXPERT_FF), D ** -0.5),
        'exp_w_down': nrm((L, N_EXPERTS, EXPERT_FF, D), DN_BETA * EXPERT_FF ** -0.5),
        'sh_w_gate': nrm((L, D, SHARED_FF), D ** -0.5),
        'sh_w_up': nrm((L, D, SHARED_FF), D ** -0.5),
        'sh_w_down': nrm((L, SHARED_FF, D), DN_BETA * SHARED_FF ** -0.5),
        'ple_w': nrm((L, PLE_DIM, D), DN_BETA * PLE_DIM ** -0.5),
        'ple_gate_w': nrm((L, D, D), D ** -0.5),
        'ln2_g': gain((L, D)),
        'ln2_b': nrm((L, D), 0.02),
    }

def reference(x, p, w_in, s5_a_re, s5_a_im, s5_log_dt, s5_b_re, s5_b_im, s5_c_re, s5_c_im, s5_d, s5_w_glu,
              swa_sinks, gla_w_lr2, gla_b_lr, gla_norm_g, mla_q_norm_g, mla_w_uq, mla_kv_norm_g, mla_w_ukv,
              w_branch, w_out, ln1_g, ln1_b, router_w, router_bias, exp_w_gate, exp_w_up, exp_w_down,
              sh_w_gate, sh_w_up, sh_w_down, ple_w, ple_gate_w, ln2_g, ln2_b):
    bsz, seq, d = x.shape
    split_at = np.cumsum(IN_SIZES)[:-1].tolist()
    for i in range(DEPTH):
        (a_u, b_q, b_k, b_v, c_q, c_k, c_v, c_g, c_lr, d_qd, d_kvd, d_kr, gate_logits) = jnp.split(
            x @ w_in[i], split_at, axis=-1)
        o_a = _s5_mixer(a_u, s5_a_re[i], s5_a_im[i], s5_log_dt[i], s5_b_re[i], s5_b_im[i],
                        s5_c_re[i], s5_c_im[i], s5_d[i], s5_w_glu[i])
        o_b = _swa_mixer(b_q, b_k, b_v, swa_sinks[i])
        o_c = _gla_mixer(c_q, c_k, c_v, c_g, c_lr, gla_w_lr2[i], gla_b_lr[i], gla_norm_g[i])
        o_d = _mla_mixer(d_qd, d_kvd, d_kr, mla_q_norm_g[i], mla_w_uq[i], mla_kv_norm_g[i], mla_w_ukv[i])
        branches = jnp.stack([o_a, o_b, o_c, o_d], axis=2)
        proj = jnp.einsum('bsnw,nwd->bsnd', branches, w_branch[i])
        gates = jax.nn.sigmoid(gate_logits.reshape(bsz, seq, N_BRANCH, d))
        mix = jnp.sum(gates * proj, axis=2) @ w_out[i]
        x = _layer_norm(DN_ALPHA * x + mix, ln1_g[i], ln1_b[i])
        ffn = _moe(x.reshape(-1, d), router_w[i], router_bias[i], exp_w_gate[i], exp_w_up[i], exp_w_down[i],
                   sh_w_gate[i], sh_w_up[i], sh_w_down[i]).reshape(bsz, seq, d)
        ple = jax.nn.sigmoid(x @ ple_gate_w[i]) * (p[i] @ ple_w[i])
        x = _layer_norm(DN_ALPHA * x + ffn + ple, ln2_g[i], ln2_b[i])
    return x


_drawn_inputs = setup_inputs


def setup_inputs(seed=0):
    import zlib

    import numpy as np

    out = dict(_drawn_inputs(seed))
    spreads = {}
    factors = {'s5_a_re': 8.0,
     's5_b_re': 3.465,
     's5_b_im': 3.146,
     's5_c_re': 3.18,
     's5_c_im': 3.014,
     'gla_norm_g': 3.583,
     'mla_q_norm_g': 6.567,
     'mla_kv_norm_g': 6.612}
    for name, (base, spread) in spreads.items():
        noise = np.random.default_rng([zlib.crc32(name.encode()), seed]).standard_normal(out[name].shape)
        drawn = base * np.exp(spread * noise) if base else spread * noise
        out[name] = __import__('jax').numpy.asarray(drawn.astype(out[name].dtype))
    for name, factor in factors.items():
        out[name] = (out[name] * factor).astype(out[name].dtype)
    return out
```

```python
from contextlib import ExitStack

import concourse.bass as bass
from concourse import mybir

F32 = mybir.dt.float32
I32 = mybir.dt.int32
ALU = mybir.AluOpType
ACT = mybir.ActivationFunctionType
AX = mybir.AxisListType

P = 128
CHUNK = 64
S5_GROUP_CH = 16
SWA_HEADS, SWA_KV, SWA_DIM = 8, 2, 64
GLA_HEADS, GLA_DK, GLA_DV = 4, 64, 128
GLA_TAU = 16.0
MLA_HEADS, MLA_NOPE, MLA_ROPE, MLA_V = 4, 128, 64, 128
MLA_SCALE = (MLA_NOPE + MLA_ROPE) ** -0.5
ROPE_THETA = 10000.0
TOP_K = 8
ROUTED_SCALE = 2.5
LN_EPS, RMS_EPS = 1e-5, 1e-6
MASKED = -1e30
TWO_PI = 6.283185307179586
PI_CLIP = 3.1415925

COL_U, COL_Q, COL_K, COL_CQ, COL_CV, COL_CG, COL_LR, COL_KVD, COL_GATE = (
    0, 512, 1024, 1280, 1792, 2304, 2816, 3088, 3280)
WSLOTS, WCOLS = 5, 272
BLK = 256
EXPERT_RING = 4
SLOTS = 128


def shape_constants():
    import numpy as np
    f = np.float32
    seq, n_exp = 512, 64
    tok = np.arange(seq)
    p = np.arange(P)
    half = MLA_ROPE // 2
    inv = f(ROPE_THETA) ** (-np.arange(half, dtype=f) / f(half))
    ang = tok.astype(f)[None, :] * inv.astype(f)[p % half][:, None]
    sign = np.where(p % MLA_ROPE < half, -1.0, 1.0)[:, None]
    partner = np.where(p % MLA_ROPE < half, p + half, p - half)
    swap = np.zeros((P, P), f)
    swap[partner, p] = 1
    slopes = 2.0 ** (-8.0 * np.arange(1, SWA_HEADS + 1) / SWA_HEADS)
    kk = np.arange(2 * P)
    dist = np.abs(p[:, None] - (kk[None, :] - P))
    qc, kc = p // CHUNK, kk // CHUNK - 2
    seen = (kc[None, :] == qc[:, None]) | (kc[None, :] == qc[:, None] - 1)
    alibi = np.where(seen[:, None, :], -slopes[None, :, None] * dist[:, None, :], MASKED)
    causal = (p[:, None] <= p[None, :]) & (p[:, None] // CHUNK == p[None, :] // CHUNK)
    return {
        "ident": np.eye(P, dtype=f),
        "centre": (np.eye(P) - 1.0 / P).astype(f),
        "half_swap": swap,
        "rope_cos": np.cos(ang).astype(f),
        "rope_sin": (sign * np.sin(ang)).astype(f),
        "alibi": alibi.astype(f),
        "gla_causal": np.ascontiguousarray(np.broadcast_to(causal[:, None, :], (P, 4, P))).astype(np.int32),
        "chunk_keep": np.broadcast_to((tok % CHUNK != 0), (P, seq)).astype(f),
        "before": (p[:, None] < p[None, :]).astype(f),
        "expert_code": np.broadcast_to(np.arange(1, n_exp + 1), (P, n_exp)).astype(f),
        "token_id": (np.arange(4)[None, :] * P + p[:, None]).astype(np.int32),
        "no_token": np.zeros((P, 256), np.int32),
    }


class Count:

    def __init__(self):
        self.counts, self.latest = {}, None

    def __call__(self, ins, sem):
        self.counts[sem.num] = self.counts.get(sem.num, 0) + 1
        self.latest = (sem, self.counts[sem.num])


class Ring:

    def __init__(self, banks, keys):
        self.banks = banks
        self.number = {k: n for n, k in enumerate(keys)}
        assert len(self.number) == len(keys)

    def bank(self, key):
        return self.banks[self.number[key] % len(self.banks)]

    def nth(self, key):
        return self.number[key] + 1

    def reused(self, key):
        return self.number[key] >= len(self.banks)

    def last_user(self, key):
        return self.number[key] - len(self.banks) + 1


class Region:

    def __init__(self, tensor, words, at=0):
        self.t, self.words, self.at = tensor, words, at

    def take(self, *dims):
        n = 1
        for d in dims:
            n *= d
        assert self.at + n <= self.words, (self.at, n, self.words)
        ap = self.t[:, self.at:self.at + n]
        self.at += n
        if len(dims) == 2:
            return ap.rearrange("p (a b) -> p a b", a=dims[0])
        if len(dims) == 3:
            return ap.rearrange("p (a b c) -> p a b c", a=dims[0], b=dims[1])
        if len(dims) == 4:
            return ap.rearrange("p (a b c d) -> p a b c d", a=dims[0], b=dims[1], c=dims[2])
        return ap


def col(ap, *shape):
    return ap.unsqueeze(len(ap.shape)).to_broadcast(shape)


BRANCH_ORDER = (3, 2, 1, 0)


def mixer_plan():
    steps = [("xt", k) for k in range(8)]
    steps += [("lr",), ("qd", 0), ("qd", 1), ("kvd",), ("rq",), ("kr",), ("rk",), ("krs",), ("q", 0)]
    steps += [("mqn", h) for h in range(4)] + [("mkn", h) for h in range(4)]
    steps += [("mqr", 0), ("mqr", 1), ("mv", 0), ("mqs", 0), ("mqs", 1)] + [("mv", i) for i in range(1, 4)]
    fill = [("q", j) for j in range(1, 4)] + [("k",), ("v",)] + [("u", t) for t in range(4)] + [("cg", t) for t in range(4)]
    fill += [("cq", 0), ("cq", 1)]
    units = [(i, h) for i in range(4) for h in range(4)]
    for n, u in enumerate(units):
        steps += [("ms", *u), ("mn", *u)]
        if n < 14:
            steps.append(fill.pop(0))
        if n:
            steps.append(("mp", *units[n - 1]))
        if n > 1:
            steps.append(("mo", *units[n - 2]))
    steps += [fill.pop(0), ("mp", *units[-1]), ("mo", *units[-2]), ("ck", 0), ("mo", *units[-1]), ("lg",), ("ck", 1)]
    steps += [("cv", i) for i in range(4)]
    halves = [s for n in BRANCH_ORDER for dt in range(8) for s in (("gate", n, dt), ("mix", n, dt))]
    last = BRANCH_ORDER[-1]
    halves[-16:] = [("gate", last, 0)] + [s for dt in range(7) for s in (("gate", last, dt + 1), ("mix", last, dt))] + [("mix", last, 7)]

    def mix(count):
        nonlocal halves
        taken, halves = halves[:count], halves[count:]
        return taken

    steps += [("ggate",)] + mix(3) + [("gdecay",)] + mix(2) + [("krt", 0), ("krt", 1)] + mix(1)
    steps += [("kv", 0), ("kv", 1), ("gstate", 0), ("gstate", 1), ("att", 0), ("att", 1)] + mix(1)
    for h in (0, 2):
        steps += [("go", h)] + mix(1) + [("go", h + 1), ("gc", h)] + mix(1) + [("gc", h + 1), ("gv", h)]
        if h == 0:
            steps += [("att", 2), ("att", 3)]
        steps += mix(1) + [("gv", h + 1), ("gout", h)] + mix(1) + [("gout", h + 1)]
    steps += mix(1)
    units = [(i, g, jp) for i in range(4) for g in range(2) for jp in range(2)]
    for n, u in enumerate(units):
        steps += [("ss", *u), ("sn", *u)]
        if n % 8 != 7:
            steps += mix(1)
        if n:
            steps.append(("sp", *units[n - 1]))
        if n > 1:
            steps.append(("so", *units[n - 2]))
        if n == 2:
            steps.append(("s5_prep",))
        if n == 6:
            steps.append(("s5_mats_prep",))
    steps += mix(1) + [("sp", *units[-1]), ("so", *units[-2])] + [("s5_mats", 0), ("s5_mats", 1), ("so", *units[-1]), ("swa_end",)]
    steps += [("s5_mats", 2), ("s5_mats", 3)]
    for i in range(16):
        steps.append(("bu", i))
        steps += mix(1)
        if i:
            steps.append(("y", i - 1))
    steps += mix(1) + [("y", 15)] + mix(1) + [("gelu",), ("glu", 0), ("glu", 1), ("glu", 2), ("glu", 3)] + mix(1) + [("glu_end",)]
    steps += mix(len(halves)) + [("ln_load",)]
    steps += [s for i in range(4) for s in (("wo", i, 0), ("wo", i, 1), ("ln1", i))]
    return steps


def mixer_banks(steps):
    by_act, by_dve = [], []
    for s in steps:
        kind = s[0]
        if kind == "xt":
            (by_act if s[1] % 2 else by_dve).append(s)
        elif kind in ("lr", "qd", "kvd", "kr", "rq", "rk", "mqn", "mkn", "mv", "q", "k", "v", "u", "cg", "cq", "ck",
                      "cv", "ms", "mo", "krt", "go", "gc", "gv", "so", "glu", "wo", "mp", "sp", "mqr", "gate"):
            by_act.append(s)
        elif kind in ("krs", "mqs", "att", "ss", "mix"):
            by_dve.append(s)
        elif kind == "lg":
            by_dve += [("lg", 0), ("lg", 1)]
        elif kind == "kv":
            by_dve += [("kv", s[1], 1), ("kv", s[1], 0)]
        elif kind == "s5_mats":
            by_act += [("mat", s[1], m) for m in range(4)]
        elif kind == "bu":
            by_dve += [("bu", s[1], 0), ("bu", s[1], 1)]
    return by_act, by_dve


def step_blocks(step):
    kind, a = step[0], step[1:]
    if kind in ("lr", "qd"):
        return [("in", COL_LR, 272)]
    if kind in ("kvd", "kr"):
        return [("in", COL_KVD, 256)]
    if kind in ("q", "u", "cg", "cq", "ck"):
        start = {"q": COL_Q, "u": COL_U, "cg": COL_CG, "cq": COL_CQ, "ck": COL_CQ + BLK}[kind]
        return [("in", start + (a[0] // 2 * BLK if kind in ("q", "u", "cg") else 0), BLK)]
    if kind in ("k", "v"):
        return [("in", COL_K, BLK)]
    if kind == "cv":
        return [("in", COL_CV, BLK), ("in", COL_CV + BLK, BLK)]
    if kind == "gate":
        return [("in", COL_GATE + a[0] * 1024 + a[1] // 2 * BLK, BLK)]
    if kind == "mix":
        return [("branch", a[0], a[1] // 4 * 512)]
    if kind == "glu":
        return [("glu", a[0] // 2 * BLK, BLK)]
    if kind == "wo":
        return [("out", (2 * a[1] + c) * BLK, BLK) for c in range(2)]
    return []


def weight_blocks(plan):
    last = {}
    for step in plan:
        for b in step_blocks(step):
            last[b] = step
    return [(*b, step) for b, step in last.items()]




def build_mixers(nc, ctx, T, layer, W, keep, sem):
    alpha = T["alpha"]
    plan = mixer_plan()
    keys_act, keys_dve = mixer_banks(plan)
    blocks = weight_blocks(plan)
    last_block_use = [b[3] for b in blocks]

    def sb(name, shape, dt=F32):
        return ctx.enter_context(nc.sbuf_tensor(name, shape, dt))

    x, ident, ones, eps = keep["x"], keep["ident"], keep["ones"], keep["eps"]
    centre, half_swap = keep["centre"], keep["half_swap"]
    cos_t, sin_t = keep["rope_cos"], keep["rope_sin"]
    xT = sb("xT", [P, 8, 512])
    mixT = sb("mixT", [P, 8 * 512])
    wring = sb("wring", [P, WSLOTS, 8 * WCOLS])
    uT = sb("uT", [P, 4, 512])
    qT = sb("qT", [P, 4, 512])
    cgT = sb("cgT", [P, 4, 512])
    odT = sb("odT", [P, 4, 512])
    kT = sb("kT", [P, 512])
    v_nat = sb("v_nat", [P, 4, 128])
    lrT = sb("lrT", [16, 512])
    small = sb("small", [P, 384])
    s5keep = sb("s5keep", [P, 3 * 1024])
    work = sb("work", [P, 12032])
    thm = sb("thm", [P, 2, 512])

    sm = Region(small, 384)
    b_lr, gla_g, q_g, kv_g, s5_d = sm.take(2), sm.take(4), sm.take(2), sm.take(1), sm.take(4)
    sinks = sm.take(8)
    mx, nmx, rsum, rinv = sm.take(2, 8), sm.take(2, 8), sm.take(2, 8), sm.take(2, 8)
    esink = sm.take(2, 8)
    decay = sm.take(2, 8)
    stats, mv, rstd = sm.take(12), sm.take(2), sm.take(1)
    phase = sm.take(16)
    s5_are, s5_aim, s5_ldt, s5_th, s5_r = sm.take(16), sm.take(16), sm.take(16), sm.take(16), sm.take(16)
    s5_fr, s5_fi, s5_c, s5_s = sm.take(16), sm.take(16), sm.take(16), sm.take(16)
    s5_a, s5_b, s5_n, s5_m, s5_den = sm.take(16), sm.take(16), sm.take(16), sm.take(16), sm.take(16)
    s5_turns = sb("s5_turns", [P, 16], I32)
    rope_tmp = s5keep[:, 0:512]
    w_lr2 = sb("w_lr2", [16, 256])

    ml = Region(mixT, 4096)
    w_uq, w_ukv, ml_t1, ml_t2 = ml.take(2, 768), ml.take(1024), ml.take(2, 512), ml.take(512)
    mx_all = mixT[:, :].rearrange("p (a b) -> p a b", a=8)
    rm = Region(work, 12032)
    qd, kvd, kr = rm.take(2, 512), rm.take(512), rm.take(512)
    qn, qr, kn, vm = rm.take(4, 512), rm.take(2, 512), rm.take(4, 512), rm.take(4, 512)
    mP, mPT = rm.take(2, 512), rm.take(2, 4, 128)
    rg = Region(work, 12032)
    cq, ck, cv = rg.take(2, 512), rg.take(2, 512), rg.take(4, 512)
    bcum, gtmp = rg.take(2, 512), rg.take(2, 512)
    krem, kremN = rg.take(2, 512), rg.take(4, 2, 128)
    gstate = rg.take(2, 7, 128)
    attT = rg.take(2, 512)
    oT, osq = krem, gtmp
    rs = Region(work, 12032)
    alibi = rs.take(8, 256)
    sS, sP, sPT = rs.take(2, 512), rs.take(2, 512), rs.take(2, 4, 128)
    s5_at = rs.at
    rp = Region(work, 12032, s5_at)
    bre, bim, cre, cim = rp.take(16, 16), rp.take(16, 16), rp.take(4, 128), rp.take(4, 128)
    bxr, bxi = rp.take(16, 32), rp.take(16, 32)
    pt1, pt2 = rp.take(512), rp.take(512)
    rk = Region(work, 12032, s5_at + 2048 + 1024 + 512)
    er, ei = rk.take(2, 512), rk.take(2, 512)
    rt = Region(work, s5_at)
    t1, t2, t3, t4 = rt.take(512), rt.take(512), rt.take(512), rt.take(512)
    zr, zi = rt.take(512), rt.take(512)
    sr, si = rt.take(2, 512), rt.take(2, 512)
    e1, e2 = rk.take(512), rk.take(512)
    glu_gate = Region(work, 12032).take(4, 512)
    b_prod = er.rearrange("p a b -> p (a b)").rearrange("p (a b c) -> p a b c", a=4, b=16)
    kp = Region(s5keep, 3072)
    btr, bti, cxr, cxi = kp.take(4, 128), kp.take(4, 128), kp.take(16, 32), kp.take(16, 32)
    jr, ji = kp.take(16, 32), kp.take(16, 32)
    kr_, ki_ = sb("s5_kr", [P, 16, 16]), sb("s5_ki", [P, 16, 16])
    rl = Region(work, 12032)
    ln_g, ln_b, ln_y = rl.take(1024), rl.take(1024), rl.take(2, 1024)

    pa = [ctx.enter_context(nc.psum_tensor(f"act_bank{n}", [P, 512], F32)) for n in range(3)]
    pv = [ctx.enter_context(nc.psum_tensor(f"dve_bank{n}", [P, 512], F32)) for n in range(4)]
    y_bank = ctx.enter_context(nc.psum_tensor("y_bank", [P, 512], F32))
    A, V = Ring(pa, keys_act), Ring(pv, keys_dve)
    act_bank_full, act_bank_copied = sem("act_bank_full"), sem("act_bank_copied")
    dve_bank_full, dve_bank_copied = sem("dve_bank_full"), sem("dve_bank_copied")

    slot_loaded = [sem(f"weights_in_slot{n}") for n in range(WSLOTS)]
    params_in, consts_in, alibi_in, s5_in, ln_in, x1_out = (
        sem(n) for n in ("params_in", "consts_in", "alibi_in", "s5_params_in", "ln_rows_in", "x1_stored"))
    dve_done, act_done, pool_done = sem("dve_done"), sem("act_done"), sem("pool_done")
    max_ready, exp_done, probs_ready = sem("mla_max_ready"), sem("mla_exp_done"), sem("mla_probs_ready")
    win_ready, win_exp, win_probs = sem("win_scores_ready"), sem("win_exp_done"), sem("win_probs_ready")
    normed = sem("latents_normed")
    rope_ready = sem("rope_ready")
    mla_done, gla_done, swa_done = sem("mla_done"), sem("gla_done"), sem("swa_done")
    gabs, gsoft, gcum, gexp, gdec_ready, gstate_ready, gout_ready = (
        sem(n) for n in ("gla_abs_ready", "gla_softplus_ready", "gla_cum_ready", "gla_exps_ready",
                         "gla_decayed", "gla_state_ready", "gla_out_ready"))
    gvar = sem("gla_sd_ready")
    s5_ang, s5_sin, s5_pool, s5_bx, s5_state, y_step, y_taken, gelu_done, glu_ready, mix_used = (
        sem(n) for n in ("s5_angle_ready", "s5_sincos_ready", "s5_tables_ready", "s5_bx_ready", "s5_state_ready",
                         "s5_y_step", "s5_y_taken", "s5_gelu_done", "s5_glu_ready", "gate_used"))
    s5_table, s5_table_used, s5_lam = sem("s5_table_ready"), sem("s5_table_used"), sem("s5_lam_ready")
    ln_var, ln_sd, ln_done = sem("ln_var_ready"), sem("ln_sd_ready"), sem("ln1_tile_ready")

    arrival, at = {}, [0] * WSLOTS
    for n, b in enumerate(blocks):
        loads = 4 if b[0] == "in" and COL_Q <= b[1] < COL_K else 2 if b[:2] in (("branch", 1), ("in", COL_KVD)) else 1
        at[n % WSLOTS] += 16 * loads
        arrival[b[:3]] = (n % WSLOTS, at[n % WSLOTS])

    def weights(eng, kind, c0, width):
        slot, value = arrival[kind, c0, width]
        eng.wait_ge(slot_loaded[slot], value)
        k = 8 if kind in ("in", "out") else 4
        w = 512 if kind == "branch" else width
        return wring[:, slot, 0:k * w].rearrange("p (k n) -> p k n", k=k)

    def toks(i, n=P):
        return slice(i * n, i * n + n)

    block = ctx.enter_context(nc.Block())

    @block.sync
    def _(eng):
        w_in = W["w_in"][layer].rearrange("(p k) n -> p k n", p=P)
        w_out = W["w_out"][layer].rearrange("(k p) n -> p k n", p=P)
        w_glu = W["s5_w_glu"][layer].rearrange("(k p) n -> p k n", p=P)
        for n, (kind, c0, width, _) in enumerate(blocks):
            slot = n % WSLOTS
            if n >= WSLOTS:
                user = last_block_use[n - WSLOTS]
                if user[0] == "mix":
                    eng.wait_ge(dve_bank_full, V.nth(user))
                else:
                    eng.wait_ge(act_bank_full, A.nth(user))
            k = 8 if kind in ("in", "out") else 4
            w = 512 if kind == "branch" else width
            dst = wring[:, slot, 0:k * w].rearrange("p (k n) -> p k n", k=k)
            done = slot_loaded[slot]
            if kind == "in" and COL_Q <= c0 < COL_K:
                for j in range(2):
                    for g in range(2):
                        c = COL_Q + g * 256 + (c0 - COL_Q) // 2 + j * 64
                        o = (2 * j + g) * 64
                        eng.dma_start(dst[:, :, o:o + 64], w_in[:, :, c:c + 64]).then_inc(done, 16)
            elif kind == "in" and c0 == COL_KVD:
                eng.dma_start(dst[:, :, 0:192], w_in[:, :, c0:c0 + 192]).then_inc(done, 16)
                eng.dma_start(dst[:, :, 192:256], w_in[:, :, c0 + P:c0 + 192]).then_inc(done, 16)
            elif kind == "in":
                eng.dma_start(dst, w_in[:, :, c0:c0 + width]).then_inc(done, 16)
            elif kind == "out":
                eng.dma_start(dst, w_out[:, :, c0:c0 + width]).then_inc(done, 16)
            elif kind == "glu":
                eng.dma_start(dst, w_glu[:, :, c0:c0 + width]).then_inc(done, 16)
            else:
                wb = W["w_branch"][layer, c0]
                cols = slice(width, width + 512)
                if c0 == 1:
                    rows = wb.rearrange("(g j d) n -> g d j n", g=2, j=4)
                    for g in range(2):
                        eng.dma_start(dst[64 * g:64 * g + 64], rows[g][:, :, cols]).then_inc(done, 16)
                else:
                    eng.dma_start(dst, wb.rearrange("(k p) n -> p k n", p=P)[:, :, cols]).then_inc(done, 16)

    @block.gpsimd
    def _(eng):
        pool = Count()

        def load(dst, src, done):
            eng.dma_start(dst, src, allow_slow_non_contiguous=True).then_inc(done, 16)

        load(w_lr2[:, :], W["gla_w_lr2"][layer], params_in)
        load(b_lr, W["gla_b_lr"][layer].rearrange("(t p) -> p t", p=P), params_in)
        load(gla_g, W["gla_norm_g"][layer].rearrange("(t p) -> p t", p=P), params_in)
        load(q_g, W["mla_q_norm_g"][layer].rearrange("(t p) -> p t", p=P), params_in)
        load(kv_g, W["mla_kv_norm_g"][layer].rearrange("(t p) -> p t", p=P), params_in)
        for k in range(2):
            src = W["mla_w_uq"][layer, k * P:(k + 1) * P, :].rearrange("p (h n) -> p h n", h=4)
            load(w_uq[:, k, 0:512].rearrange("p (h n) -> p h n", h=4), src[:, :, 0:P], params_in)
            load(w_uq[:, k, 512:768].rearrange("p (h n) -> p h n", h=4), src[:, :, P:P + 64], params_in)
        load(w_ukv, W["mla_w_ukv"][layer], params_in)
        load(s5_d, W["s5_d"][layer].rearrange("(t g) c -> (g c) t", t=4), params_in)
        load(sinks, W["swa_sinks"][layer].partition_broadcast(P), params_in)
        load(s5_are, W["s5_a_re"][layer].rearrange("(t g) p -> (g p) t", g=2), params_in)
        load(s5_aim, W["s5_a_im"][layer].rearrange("(t g) p -> (g p) t", g=2), params_in)
        for g in range(2):
            src = W["s5_log_dt"][layer].rearrange("(t g) -> g t", g=2)[g]
            load(s5_ldt[64 * g:64 * g + 64], src.partition_broadcast(64), params_in)

        def s5_prep():
            eng.wait_ge(gout_ready, 4)
            load(alibi, T["alibi"], alibi_in)
            for dst, name in ((bre, "s5_b_re"), (bim, "s5_b_im")):
                src = W[name][layer].rearrange("(t g) p c -> (g p) t c", g=2)
                load(dst, src, s5_in)
            for dst, name in ((cre, "s5_c_re"), (cim, "s5_c_im")):
                src = W[name][layer].rearrange("(t g) c p -> (g c) t p", t=4)
                for half in range(2):
                    load(dst[:, :, 64 * half:64 * half + 64], src, s5_in)
            eng.wait_ge(s5_sin, 2)
            eng.wait_ge(s5_lam, 1)
            g = eng
            pr, pi = s5_c, s5_s
            ta = pt1.rearrange("p (a b) -> p a b", a=16)
            tb = pt2.rearrange("p (a b) -> p a b", a=16)
            for tr, ti, size in ((jr, ji, 32), (kr_, ki_, 16)):
                pool(g.memset(tr[:, :, 0:1], 1.0).then_inc(pool_done, 1), pool_done)
                pool(g.memset(ti[:, :, 0:1], 0.0).then_inc(pool_done, 1), pool_done)
                m = 1
                while m < size:
                    eng.wait_ge(*pool.latest)
                    shape = (P, 16, m)
                    bpr, bpi = col(pr, *shape), col(pi, *shape)
                    pool(g.tensor_tensor(ta[:, :, 0:m], tr[:, :, 0:m], bpr, ALU.mult).then_inc(pool_done, 1), pool_done)
                    pool(g.tensor_tensor(tb[:, :, 0:m], ti[:, :, 0:m], bpi, ALU.mult).then_inc(pool_done, 1), pool_done)
                    eng.wait_ge(*pool.latest)
                    pool(g.tensor_tensor(tr[:, :, m:2 * m], ta[:, :, 0:m], tb[:, :, 0:m], ALU.subtract).then_inc(pool_done, 1), pool_done)
                    eng.wait_ge(*pool.latest)
                    pool(g.tensor_tensor(ta[:, :, 0:m], tr[:, :, 0:m], bpi, ALU.mult).then_inc(pool_done, 1), pool_done)
                    pool(g.tensor_tensor(tb[:, :, 0:m], ti[:, :, 0:m], bpr, ALU.mult).then_inc(pool_done, 1), pool_done)
                    eng.wait_ge(*pool.latest)
                    pool(g.tensor_tensor(ti[:, :, m:2 * m], ta[:, :, 0:m], tb[:, :, 0:m], ALU.add).then_inc(pool_done, 1), pool_done)
                    eng.wait_ge(*pool.latest)
                    pool(g.tensor_tensor(ta[:, :, 0], pr, pr, ALU.mult).then_inc(pool_done, 1), pool_done)
                    pool(g.tensor_tensor(tb[:, :, 0], pi, pi, ALU.mult).then_inc(pool_done, 1), pool_done)
                    pool(g.tensor_tensor(ta[:, :, 1], pr, pi, ALU.mult).then_inc(pool_done, 1), pool_done)
                    eng.wait_ge(*pool.latest)
                    pool(g.tensor_tensor(pr, ta[:, :, 0], tb[:, :, 0], ALU.subtract).then_inc(pool_done, 1), pool_done)
                    pool(g.tensor_tensor(pi, ta[:, :, 1], ta[:, :, 1], ALU.add).then_inc(pool_done, 1), pool_done)
                    m *= 2
            eng.wait_ge(*pool.latest)

        def s5_time(i):
            if i == 0:
                eng.wait_ge(swa_done, 1)
                eng.wait_ge(s5_bx, 1)
            if i >= 2:
                eng.wait_ge(s5_table_used, i - 1)
            shape = (P, 16, 32)
            k_r, k_i = kr_[:, i, :].unsqueeze(2).to_broadcast(shape), ki_[:, i, :].unsqueeze(2).to_broadcast(shape)
            j_r, j_i = jr[:, i, :].unsqueeze(1).to_broadcast(shape), ji[:, i, :].unsqueeze(1).to_broadcast(shape)
            e_r, e_i = (e[:, i % 2, :].rearrange("p (c j) -> p c j", c=16) for e in (er, ei))
            a, b = (e.rearrange("p (c j) -> p c j", c=16) for e in (e1, e2))
            for x1, y1, x2, y2, op, out in ((k_r, j_r, k_i, j_i, ALU.subtract, e_r), (k_r, j_i, k_i, j_r, ALU.add, e_i)):
                if pool.latest:
                    eng.wait_ge(*pool.latest)
                pool(eng.tensor_tensor(a, x1, y1, ALU.mult).then_inc(pool_done, 1), pool_done)
                pool(eng.tensor_tensor(b, x2, y2, ALU.mult).then_inc(pool_done, 1), pool_done)
                eng.wait_ge(*pool.latest)
                pool(eng.tensor_tensor(out, a, b, op).then_inc(s5_table if op == ALU.add else pool_done, 1), s5_table if op == ALU.add else pool_done)

        for step in plan:
            if step[0] == "s5_prep":
                s5_prep()
            elif step[0] == "bu":
                s5_time(step[1])
            elif step[0] == "ln_load":
                eng.wait_ge(glu_ready, 1)
                load(ln_g, W["ln1_g"][layer].partition_broadcast(P), ln_in)
                load(ln_b, W["ln1_b"][layer].partition_broadcast(P), ln_in)
            elif step[0] == "ln1":
                i = step[1]
                eng.wait_ge(ln_done, i + 1)
                load(T["x1_dram"][toks(i), :], x[:, i, :], x1_out)
        eng.wait_ge(x1_out, 64)

    @block.scalar
    def _(eng):
        act = Count()
        mix_no = [0]

        def copy_out(step, dst, scale=None):
            eng.wait_ge(act_bank_full, A.nth(step))
            b = A.bank(step)
            src = b[0:dst.shape[0], :]
            if len(dst.shape) == 3:
                src = src.rearrange("p (a b) -> p a b", a=dst.shape[1])
            if scale is None:
                act(eng.copy(dst, src).then_inc(act_bank_copied, 1), act_bank_copied)
            else:
                act(eng.mul(dst, src, scale).then_inc(act_bank_copied, 1), act_bank_copied)

        def squares(step, dst, sq):
            eng.wait_ge(act_bank_full, A.nth(step))
            b = A.bank(step)
            act(eng.activation(sq, b[:, :], ACT.Square).then_inc(act_done, 1), act_done)
            act(eng.copy(dst, b[:, :]).then_inc(act_bank_copied, 1), act_bank_copied)

        def root(step, dst, n, e):
            eng.wait_ge(act_bank_full, A.nth(step))
            b = A.bank(step)
            act(eng.activation(dst, b[:, :], ACT.Sqrt, bias=eps[:, e:e + 1], scale=1.0 / n).then_inc(act_bank_copied, 1), act_bank_copied)

        for step in plan:
            kind, a = step[0], step[1:]
            if kind == "xt" and step in A.number:
                copy_out(step, xT[:, a[0], :])
            elif kind == "lr":
                copy_out(step, lrT[:, :])
            elif kind == "qd":
                squares(step, qd[:, a[0], :], ml_t1[:, a[0], :])
            elif kind == "kvd":
                squares(step, kvd, ml_t2)
            elif kind == "kr":
                copy_out(step, kr)
            elif kind == "rq":
                root(step, thm[:, 0, :], 256, 1)
            elif kind == "rk":
                root(step, thm[:, 1, :], 128, 1)
            elif kind == "mqn":
                copy_out(step, qn[:, a[0], :])
            elif kind == "mkn":
                copy_out(step, kn[:, a[0], :])
            elif kind == "mqr":
                copy_out(step, qr[:, a[0], :])
            elif kind == "mv":
                copy_out(step, vm[:, a[0], :])
            elif kind == "q":
                copy_out(step, qT[:, a[0], :], SWA_DIM ** -0.5)
            elif kind == "k":
                copy_out(step, kT[:, :])
            elif kind == "v":
                copy_out(step, v_nat[:, :, :])
            elif kind == "u":
                copy_out(step, uT[:, a[0], :])
            elif kind == "cg":
                eng.wait_ge(act_bank_full, A.nth(step))
                b = A.bank(step)
                act(eng.activation(cgT[:, a[0], :], b[:, :], ACT.Silu).then_inc(act_bank_copied, 1), act_bank_copied)
            elif kind == "cq":
                copy_out(step, cq[:, a[0], :], GLA_DK ** -0.5)
            elif kind == "ck":
                copy_out(step, ck[:, a[0], :])
            elif kind == "cv":
                copy_out(step, cv[:, a[0], :])
            elif kind == "ms":
                i, h = a
                u, n = 4 * i + h, P * (i + 1)
                eng.wait_ge(max_ready, u + 1)
                b = A.bank(step)
                act(eng.activation(mP[:, u % 2, 0:n], b[:, 0:n], ACT.Exp, bias=nmx[:, u % 2, 0:1], scale=MLA_SCALE,
                                   accum_out=rsum[:, u % 2, 0:1]).then_inc(act_bank_copied, 1), act_bank_copied)
            elif kind == "mp":
                i, h = a
                u, n = 4 * i + h, P * (i + 1)
                eng.wait_ge(act_bank_full, A.nth(step))
                b = A.bank(step)
                act(eng.copy(mPT[:, u % 2, 0:i + 1, :], b[:, 0:n].rearrange("p (a b) -> p a b", b=P)).then_inc(act_bank_copied, 1), act_bank_copied)
            elif kind == "mo":
                i, h = a
                eng.wait_ge(act_bank_full, A.nth(step))
                b = A.bank(step)
                act(eng.copy(odT[:, h, toks(i)], b[:, 0:P]).then_inc(act_bank_copied, 1), act_bank_copied)
            elif kind == "ggate":
                eng.wait_ge(gabs, 1)
                act(eng.activation(bcum, bcum, ACT.Exp, scale=-1.0).then_inc(act_done, 1), act_done)
                eng.wait_ge(*act.latest)
                act(eng.activation(krem, bcum, ACT.Ln, bias=1.0).then_inc(gsoft, 1), gsoft)
            elif kind == "gdecay":
                eng.wait_ge(gcum, 1)
                act(eng.activation(krem, bcum, ACT.Exp, scale=1.0 / GLA_TAU).then_inc(act_done, 1), act_done)
                act(eng.activation(kremN, bcum, ACT.Exp, scale=-1.0 / GLA_TAU).then_inc(act_done, 1), act_done)
                last = bcum.rearrange("p t (c s) -> p t c s", s=CHUNK)[:, :, :, CHUNK - 1]
                act(eng.activation(decay, last, ACT.Exp, scale=1.0 / GLA_TAU).then_inc(act_done, 1), act_done)
                act(eng.activation(gtmp, gtmp, ACT.Exp, scale=1.0 / GLA_TAU).then_inc(gexp, 1), gexp)
            elif kind == "krt":
                eng.wait_ge(act_bank_full, A.nth(step))
                b = A.bank(step)
                act(eng.copy(kremN[:, 2 * a[0]:2 * a[0] + 2, :, :].rearrange("p a b c -> p (a b c)"), b[:, :]).then_inc(act_bank_copied, 1), act_bank_copied)
            elif kind == "go":
                h = a[0]
                if h >= 2:
                    eng.wait_ge(gout_ready, h - 1)
                copy_out(step, oT[:, h % 2, :])
            elif kind == "gc":
                squares(step, oT[:, a[0] % 2, :], osq[:, a[0] % 2, :])
            elif kind == "gv":
                root(step, osq[:, a[0] % 2, :], P, 0)
            elif kind == "gate":
                m = mix_no[0]
                mix_no[0] += 1
                if m >= 2:
                    eng.wait_ge(mix_used, m - 1)
                eng.wait_ge(act_bank_full, A.nth(step))
                b = A.bank(step)
                act(eng.activation(thm[:, m % 2, :], b[:, :], ACT.Tanh, scale=0.5).then_inc(act_bank_copied, 1), act_bank_copied)
            elif kind == "s5_prep":
                eng.wait_ge(params_in, 16 * 16)
                act(eng.activation(s5_ldt, s5_ldt, ACT.Exp).then_inc(s5_sin, 1), s5_sin)
                eng.wait_ge(s5_ang, 1)
                act(eng.activation(s5_r, s5_a, ACT.Exp).then_inc(act_done, 1), act_done)
                eng.wait_ge(s5_ang, 2)
                act(eng.activation(s5_s, phase, ACT.Sin).then_inc(act_done, 1), act_done)
                act(eng.activation(s5_c, s5_b, ACT.Sin, bias=eps[:, 2:3], scale=-1.0).then_inc(s5_sin, 1), s5_sin)
            elif kind == "ss":
                i, g, jp = a
                u = 4 * i + 2 * g + jp
                w = P if i == 0 else 2 * P
                eng.wait_ge(win_ready, u + 1)
                for j in range(2):
                    act(eng.activation(sP[:, u % 2, j * w:(j + 1) * w], sS[:, u % 2, j * w:(j + 1) * w], ACT.Exp,
                                       bias=nmx[:, u % 2, j:j + 1], accum_out=rsum[:, u % 2, j:j + 1]).then_inc(act_done, 1), act_done)
                act(eng.activation(esink[:, u % 2, 0:2], esink[:, u % 2, 0:2], ACT.Exp).then_inc(win_exp, 1), win_exp)
            elif kind == "sp":
                i, g, jp = a
                u = 4 * i + 2 * g + jp
                w = 2 * P if i == 0 else 4 * P
                eng.wait_ge(act_bank_full, A.nth(step))
                b = A.bank(step)
                act(eng.copy(sPT[:, u % 2, 0:w // P, :], b[:, 0:w].rearrange("p (a b) -> p a b", b=P)).then_inc(act_bank_copied, 1), act_bank_copied)
            elif kind == "so":
                i, g, jp = a
                eng.wait_ge(act_bank_full, A.nth(step))
                b = A.bank(step)
                rows = slice(64 * g, 64 * g + 64)
                act(eng.copy(qT[rows, 2 * jp:2 * jp + 2, toks(i)], b[rows, 0:2 * P].rearrange("p (a b) -> p a b", b=P)).then_inc(act_bank_copied, 1),
                    act_bank_copied)
            elif kind == "s5_mats":
                Tt = a[0]
                for m, dst in ((0, btr), (1, bti)):
                    eng.wait_ge(act_bank_full, A.nth(("mat", Tt, m)))
                    b = A.bank(("mat", Tt, m))
                    act(eng.copy(dst[:, Tt, :], b[:, 0:P]).then_inc(act_bank_copied, 1), act_bank_copied)
                for m, dst, sign in ((2, cxr, 1.0), (3, cxi, -1.0)):
                    eng.wait_ge(act_bank_full, A.nth(("mat", Tt, m)))
                    b = A.bank(("mat", Tt, m))
                    for hf in range(2):
                        rows, cols = slice(64 * hf, 64 * hf + 64), slice(16 * hf, 16 * hf + 16)
                        act(eng.mul(dst[rows, 4 * Tt:4 * Tt + 4, cols],
                                    b[rows, 0:P].rearrange("p (i n) -> p i n", n=32)[:, :, cols], sign).then_inc(act_bank_copied if hf else act_done, 1),
                            act_bank_copied if hf else act_done)
            elif kind == "gelu":
                eng.wait_ge(y_taken, 4)
                act(eng.activation(uT[:, :, :], uT[:, :, :], ACT.Gelu_apprx_tanh).then_inc(gelu_done, 1), gelu_done)
            elif kind == "glu":
                eng.wait_ge(act_bank_full, A.nth(step))
                b = A.bank(step)
                act(eng.activation(glu_gate[:, a[0], :], b[:, :], ACT.Sigmoid).then_inc(act_bank_copied, 1), act_bank_copied)
            elif kind == "wo":
                i, half = a
                if i >= 2:
                    eng.wait_ge(ln_done, i - 1)
                elif half == 0 and i == 0:
                    eng.wait_ge(glu_ready, 1)
                eng.wait_ge(act_bank_full, A.nth(step))
                b = A.bank(step)
                act(eng.mul(ln_y[:, i % 2, 512 * half:512 * half + 512], b[:, :], 0.5).then_inc(act_bank_copied, 1), act_bank_copied)
            elif kind == "ln1":
                eng.wait_ge(ln_var, a[0] + 1)
                act(eng.activation(rstd, mv[:, 1:2], ACT.Sqrt, bias=eps[:, 0:1]).then_inc(ln_sd, 1), ln_sd)

    @block.vector
    def _(eng):
        dve = Count()
        mix_no = [0]
        tt, ts, stt = eng.tensor_tensor, eng.tensor_scalar, eng.scalar_tensor_tensor

        def norm_latent(parts, rms, gains):
            dve(eng.reciprocal(rms, rms).then_inc(dve_done, 1), dve_done)
            eng.wait_ge(*dve.latest)
            for n, (t, g) in enumerate(zip(parts, gains)):
                dve(stt(t, t, g, rms, ALU.mult, ALU.mult).then_inc(normed if n == len(parts) - 1 else dve_done, 1), normed if n == len(parts) - 1 else dve_done)

        def rope(step, t, tmp):
            eng.wait_ge(dve_bank_full, V.nth(step))
            b = V.bank(step)
            dve(tt(tmp, b[:, :], sin_t[:, :], ALU.mult).then_inc(dve_bank_copied, 1), dve_bank_copied)
            dve(tt(t, t, cos_t[:, :], ALU.mult).then_inc(dve_done, 1), dve_done)
            eng.wait_ge(*dve.latest)
            dve(tt(t, t, tmp, ALU.add).then_inc(rope_ready, 1), rope_ready)

        for step in plan:
            kind, a = step[0], step[1:]
            if dve.latest:
                eng.wait_ge(*dve.latest)
            if kind == "xt" and step in V.number:
                eng.wait_ge(dve_bank_full, V.nth(step))
                b = V.bank(step)
                dve(eng.tensor_copy(xT[:, a[0], :], b[:, :]).then_inc(dve_bank_copied, 1), dve_bank_copied)
            elif kind == "krs":
                rope(step, kr, rope_tmp)
            elif kind == "rq":
                eng.wait_ge(params_in, 16 * 16)
                eng.wait_ge(act_bank_copied, A.nth(step))
                norm_latent([qd[:, 0, :], qd[:, 1, :]], thm[:, 0, :], [q_g[:, 0:1], q_g[:, 1:2]])
            elif kind == "rk":
                eng.wait_ge(act_bank_copied, A.nth(step))
                norm_latent([kvd], thm[:, 1, :], [kv_g[:, 0:1]])
            elif kind == "mqs":
                rope(step, qr[:, a[0], :], rope_tmp)
            elif kind == "ms":
                i, h = a
                u, n = 4 * i + h, P * (i + 1)
                eng.wait_ge(act_bank_full, A.nth(step))
                b = A.bank(step)
                dve(eng.memset(b[0:64, n - 64:n], MASKED).then_inc(dve_done, 1), dve_done)
                eng.wait_ge(*dve.latest)
                dve(eng.reduce_max(mx[:, u % 2, 0:1], b[:, 0:n], AX.X).then_inc(dve_done, 1), dve_done)
                eng.wait_ge(*dve.latest)
                dve(ts(nmx[:, u % 2, 0:1], mx[:, u % 2, 0:1], -MLA_SCALE, None, ALU.mult).then_inc(max_ready, 1), max_ready)
            elif kind == "mn":
                i, h = a
                u, n = 4 * i + h, P * (i + 1)
                eng.wait_ge(act_bank_copied, A.nth(("ms", i, h)))
                dve(eng.reciprocal(rinv[:, u % 2, 0:1], rsum[:, u % 2, 0:1]).then_inc(dve_done, 1), dve_done)
                eng.wait_ge(*dve.latest)
                dve(ts(mP[:, u % 2, 0:n], mP[:, u % 2, 0:n], rinv[:, u % 2, 0:1], None, ALU.mult).then_inc(probs_ready, 1), probs_ready)
            elif kind == "lg":
                for t in range(2):
                    eng.wait_ge(dve_bank_full, V.nth(("lg", t)))
                    b = V.bank(("lg", t))
                    dve(ts(gtmp[:, t, :], b[:, :], b_lr[:, t:t + 1], None, ALU.add).then_inc(dve_bank_copied, 1), dve_bank_copied)
                eng.wait_ge(*dve.latest)
                dve(stt(bcum, gtmp, -1.0, gtmp, ALU.mult, ALU.max).then_inc(gabs, 1), gabs)
                dve(eng.memset(attT, 0.0).then_inc(dve_done, 1), dve_done)
            elif kind == "ggate":
                eng.wait_ge(gsoft, 1)
                dve(stt(gtmp, gtmp, 0.0, krem, ALU.min, ALU.subtract).then_inc(dve_done, 1), dve_done)
                eng.wait_ge(*dve.latest)
                for t in range(2):
                    dve(eng.tensor_tensor_scan(bcum[:, t, :], keep["chunk_keep"][:, :], gtmp[:, t, :], 0.0, ALU.mult, ALU.add).then_inc(dve_done, 1), dve_done)
                eng.wait_ge(*dve.latest)
                bc = bcum.rearrange("p t (c s) -> p (t c) s", s=CHUNK)
                last = bc[:, :, CHUNK - 1:CHUNK].to_broadcast((P, 16, CHUNK))
                dve(tt(gtmp.rearrange("p t (c s) -> p (t c) s", s=CHUNK), last, bc, ALU.subtract).then_inc(gcum, 1), gcum)
            elif kind == "gdecay":
                eng.wait_ge(gexp, 1)
                eng.wait_ge(act_bank_copied, A.nth(("ck", 1)))
                dve(tt(gtmp, gtmp, ck, ALU.mult).then_inc(dve_done, 1), dve_done)
                dve(tt(cq, cq, krem, ALU.mult).then_inc(dve_done, 1), dve_done)
                eng.wait_ge(*dve.latest)
                dve(tt(ck, ck, kremN.rearrange("p a b c -> p (a b) c").rearrange("p (t a) c -> p t (a c)", t=2), ALU.mult).then_inc(gdec_ready, 1), gdec_ready)
            elif kind == "gstate":
                t = a[0]
                eng.wait_ge(dve_bank_full, V.nth(("kv", t, 0)))
                for c in range(7):
                    kv = V.bank(("kv", t, c % 2))[:, (c // 2) * P:(c // 2 + 1) * P]
                    if c == 0:
                        dve(eng.tensor_copy(gstate[:, t, 0, :], kv).then_inc(dve_done, 1), dve_done)
                    else:
                        eng.wait_ge(*dve.latest)
                        dve(stt(gstate[:, t, c, :], gstate[:, t, c - 1, :], decay[:, t, c:c + 1], kv, ALU.mult, ALU.add).then_inc(dve_bank_copied if c >= 5 else dve_done, 1), dve_bank_copied if c >= 5 else dve_done)
            elif kind == "att":
                h = a[0]
                if h >= 2:
                    eng.wait_ge(act_bank_full, A.nth(("go", h - 2)))
                eng.wait_ge(dve_bank_full, V.nth(step))
                b = V.bank(step)
                dve(eng.copy_predicated(attT[:, h % 2, :].rearrange("p (a b) -> p a b", a=4), keep["gla_causal"][:, :, :],
                                        b[:, :].rearrange("p (a b) -> p a b", a=4)).then_inc(dve_bank_copied, 1), dve_bank_copied)
            elif kind == "gout":
                h = a[0]
                eng.wait_ge(act_bank_copied, A.nth(("gv", h)))
                o, sd = oT[:, h % 2, :], osq[:, h % 2, :]
                dve(eng.reciprocal(sd, sd).then_inc(dve_done, 1), dve_done)
                eng.wait_ge(*dve.latest)
                dve(stt(o, o, gla_g[:, h:h + 1], sd, ALU.mult, ALU.mult).then_inc(dve_done, 1), dve_done)
                eng.wait_ge(*dve.latest)
                dve(tt(cgT[:, h, :], cgT[:, h, :], o, ALU.mult).then_inc(gout_ready, 1), gout_ready)
            elif kind == "mix":
                m = mix_no[0]
                mix_no[0] += 1
                n, dt = a
                eng.wait_ge(dve_bank_full, V.nth(step))
                b = V.bank(step)
                eng.wait_ge(act_bank_copied, A.nth(("gate", n, dt)))
                dve(stt(thm[:, m % 2, :], thm[:, m % 2, :], 1.0, b[:, :], ALU.add, ALU.mult).then_inc(dve_bank_copied, 1), dve_bank_copied)
                eng.wait_ge(*dve.latest)
                if m < 8:
                    dve(eng.tensor_copy(mx_all[:, dt, :], thm[:, m % 2, :]).then_inc(mix_used, 1), mix_used)
                else:
                    dve(tt(mx_all[:, dt, :], mx_all[:, dt, :], thm[:, m % 2, :], ALU.add).then_inc(mix_used, 1), mix_used)
            elif kind == "s5_prep":
                eng.wait_ge(s5_sin, 1)
                dve(tt(s5_a, s5_are, s5_ldt, ALU.mult).then_inc(s5_ang, 1), s5_ang)
                dve(tt(s5_th, s5_aim, s5_ldt, ALU.mult).then_inc(dve_done, 1), dve_done)
                eng.wait_ge(*dve.latest)
                dve(ts(s5_turns[:, :], s5_th, 1.0 / TWO_PI, None, ALU.mult).then_inc(dve_done, 1), dve_done)
                eng.wait_ge(*dve.latest)
                dve(eng.tensor_copy(s5_m, s5_turns[:, :]).then_inc(dve_done, 1), dve_done)
                eng.wait_ge(*dve.latest)
                dve(stt(s5_th, s5_m, -6.28125, s5_th, ALU.mult, ALU.add).then_inc(dve_done, 1), dve_done)
                eng.wait_ge(*dve.latest)
                dve(stt(s5_th, s5_m, -(TWO_PI - 6.28125), s5_th, ALU.mult, ALU.add).then_inc(dve_done, 1), dve_done)
                eng.wait_ge(*dve.latest)
                dve(ts(phase, s5_th, PI_CLIP, -PI_CLIP, ALU.min, ALU.max).then_inc(dve_done, 1), dve_done)
                eng.wait_ge(*dve.latest)
                dve(stt(s5_b, phase, -1.0, phase, ALU.mult, ALU.max).then_inc(s5_ang, 1), s5_ang)
            elif kind == "s5_mats_prep":
                dve(tt(s5_n, s5_are, s5_are, ALU.mult).then_inc(dve_done, 1), dve_done)
                dve(tt(s5_m, s5_aim, s5_aim, ALU.mult).then_inc(dve_done, 1), dve_done)
                eng.wait_ge(*dve.latest)
                dve(tt(s5_n, s5_n, s5_m, ALU.add).then_inc(dve_done, 1), dve_done)
                eng.wait_ge(*dve.latest)
                dve(eng.reciprocal(s5_den, s5_n).then_inc(dve_done, 1), dve_done)
                eng.wait_ge(s5_sin, 2)
                dve(tt(s5_fr, s5_r, s5_c, ALU.mult).then_inc(dve_done, 1), dve_done)
                dve(tt(s5_fi, s5_r, s5_s, ALU.mult).then_inc(s5_lam, 1), s5_lam)
                eng.wait_ge(*dve.latest)
                dve(ts(s5_fr, s5_fr, -1.0, None, ALU.add).then_inc(dve_done, 1), dve_done)
                eng.wait_ge(*dve.latest)
                dve(tt(s5_m, s5_fr, s5_are, ALU.mult).then_inc(dve_done, 1), dve_done)
                dve(tt(s5_n, s5_fi, s5_aim, ALU.mult).then_inc(dve_done, 1), dve_done)
                dve(tt(s5_a, s5_fi, s5_are, ALU.mult).then_inc(dve_done, 1), dve_done)
                dve(tt(s5_b, s5_fr, s5_aim, ALU.mult).then_inc(dve_done, 1), dve_done)
                eng.wait_ge(*dve.latest)
                dve(tt(s5_m, s5_m, s5_n, ALU.add).then_inc(dve_done, 1), dve_done)
                dve(tt(s5_a, s5_a, s5_b, ALU.subtract).then_inc(dve_done, 1), dve_done)
                eng.wait_ge(*dve.latest)
                dve(tt(s5_fr, s5_m, s5_den, ALU.mult).then_inc(dve_done, 1), dve_done)
                dve(tt(s5_fi, s5_a, s5_den, ALU.mult).then_inc(dve_done, 1), dve_done)
                for z in (bxr, bxi, cxr, cxi):
                    dve(eng.memset(z, 0.0).then_inc(dve_done, 1), dve_done)
                eng.wait_ge(*dve.latest)
                eng.wait_ge(s5_in, 16 * 6)
                fr, fi = col(s5_fr, P, 16, 16), col(s5_fi, P, 16, 16)
                for n, (f, bb) in enumerate(((fr, bre), (fi, bim), (fi, bre), (fr, bim))):
                    dve(tt(b_prod[:, n, :, :], bb, f, ALU.mult).then_inc(dve_done, 1), dve_done)
                eng.wait_ge(*dve.latest)
                for hf in range(2):
                    rows, cols = slice(64 * hf, 64 * hf + 64), slice(16 * hf, 16 * hf + 16)
                    dve(tt(bxr[rows, :, cols], b_prod[rows, 0, :, :], b_prod[rows, 1, :, :], ALU.subtract).then_inc(dve_done, 1), dve_done)
                    dve(tt(bxi[rows, :, cols], b_prod[rows, 2, :, :], b_prod[rows, 3, :, :], ALU.add).then_inc(s5_bx if hf else dve_done, 1),
                        s5_bx if hf else dve_done)
            elif kind == "ss":
                i, g, jp = a
                u = 4 * i + 2 * g + jp
                w = P if i == 0 else 2 * P
                k0 = 2 * P - w
                eng.wait_ge(dve_bank_full, V.nth(step))
                b = V.bank(step)
                if u == 0:
                    eng.wait_ge(alibi_in, 16)
                h0 = 4 * g + 2 * jp
                two = sS[:, u % 2, 0:2 * w].rearrange("p (j k) -> p j k", j=2)
                dve(tt(two, b[:, 0:2 * w].rearrange("p (j k) -> p j k", j=2), alibi[:, h0:h0 + 2, k0:], ALU.add).then_inc(dve_bank_copied, 1), dve_bank_copied)
                eng.wait_ge(*dve.latest)
                dve(eng.reduce_max(mx[:, u % 2, 0:2], two, AX.X).then_inc(dve_done, 1), dve_done)
                eng.wait_ge(*dve.latest)
                dve(tt(mx[:, u % 2, 0:2], mx[:, u % 2, 0:2], sinks[:, h0:h0 + 2], ALU.max).then_inc(dve_done, 1), dve_done)
                eng.wait_ge(*dve.latest)
                dve(tt(esink[:, u % 2, 0:2], sinks[:, h0:h0 + 2], mx[:, u % 2, 0:2], ALU.subtract).then_inc(dve_done, 1), dve_done)
                dve(ts(nmx[:, u % 2, 0:2], mx[:, u % 2, 0:2], -1.0, None, ALU.mult).then_inc(win_ready, 1), win_ready)
            elif kind == "sn":
                i, g, jp = a
                u = 4 * i + 2 * g + jp
                w = P if i == 0 else 2 * P
                eng.wait_ge(win_exp, u + 1)
                dve(tt(rsum[:, u % 2, 0:2], rsum[:, u % 2, 0:2], esink[:, u % 2, 0:2], ALU.add).then_inc(dve_done, 1), dve_done)
                eng.wait_ge(*dve.latest)
                dve(eng.reciprocal(rinv[:, u % 2, 0:2], rsum[:, u % 2, 0:2]).then_inc(dve_done, 1), dve_done)
                eng.wait_ge(*dve.latest)
                two = sP[:, u % 2, 0:2 * w].rearrange("p (j k) -> p j k", j=2)
                dve(tt(two, two, col(rinv[:, u % 2, 0:2], P, 2, w), ALU.mult).then_inc(win_probs, 1), win_probs)
            elif kind == "swa_end":
                eng.wait_ge(act_bank_copied, A.nth(("so", 3, 1, 1)))
                dve(eng.memset(mv, 0.0).then_inc(swa_done, 1), swa_done)
            elif kind == "bu":
                i = a[0]
                if i == 0:
                    eng.wait_ge(act_bank_copied, A.nth(("mat", 3, 3)))
                eng.wait_ge(s5_table, i + 1)
                c, s = er[:, i % 2, :], ei[:, i % 2, :]
                eng.wait_ge(dve_bank_full, V.nth(("bu", i, 0)))
                b0 = V.bank(("bu", i, 0))
                dve(tt(t1, b0[:, :], c, ALU.mult).then_inc(dve_done, 1), dve_done)
                dve(tt(t4, b0[:, :], s, ALU.mult).then_inc(dve_bank_copied, 1), dve_bank_copied)
                eng.wait_ge(dve_bank_full, V.nth(("bu", i, 1)))
                b1 = V.bank(("bu", i, 1))
                dve(tt(t2, b1[:, :], s, ALU.mult).then_inc(dve_done, 1), dve_done)
                dve(tt(t3, b1[:, :], c, ALU.mult).then_inc(dve_bank_copied, 1), dve_bank_copied)
                eng.wait_ge(*dve.latest)
                dve(tt(t1, t1, t2, ALU.add).then_inc(dve_done, 1), dve_done)
                dve(tt(t3, t3, t4, ALU.subtract).then_inc(dve_done, 1), dve_done)
                eng.wait_ge(*dve.latest)
                r = s5_r[:, i:i + 1].to_broadcast((P, 512))
                dve(eng.tensor_tensor_scan(zr, r, t1, 0.0, ALU.mult, ALU.add).then_inc(dve_done, 1), dve_done)
                dve(eng.tensor_tensor_scan(zi, r, t3, 0.0, ALU.mult, ALU.add).then_inc(dve_done, 1), dve_done)
                eng.wait_ge(*dve.latest)
                dve(tt(t1, zr, c, ALU.mult).then_inc(dve_done, 1), dve_done)
                dve(tt(t2, zi, s, ALU.mult).then_inc(dve_done, 1), dve_done)
                dve(tt(t3, zr, s, ALU.mult).then_inc(dve_done, 1), dve_done)
                dve(tt(t4, zi, c, ALU.mult).then_inc(s5_table_used, 1), s5_table_used)
                if i >= 2:
                    eng.wait_ge(y_step, i - 1)
                eng.wait_ge(*dve.latest)
                dve(tt(sr[:, i % 2, :], t1, t2, ALU.subtract).then_inc(dve_done, 1), dve_done)
                dve(tt(si[:, i % 2, :], t3, t4, ALU.add).then_inc(s5_state, 1), s5_state)
            elif kind == "y" and a[0] % 4 == 3:
                Tt = a[0] // 4
                eng.wait_ge(y_step, a[0] + 1)
                dve(stt(uT[:, Tt, :], uT[:, Tt, :], s5_d[:, Tt:Tt + 1], y_bank[:, :], ALU.mult, ALU.add).then_inc(y_taken, 1), y_taken)
            elif kind == "glu_end":
                eng.wait_ge(act_bank_copied, A.nth(("glu", 3)))
                dve(tt(uT[:, :, :], uT[:, :, :], glu_gate, ALU.mult).then_inc(glu_ready, 1), glu_ready)
            elif kind == "ln1":
                i = a[0]
                eng.wait_ge(act_bank_copied, A.nth(("wo", i, 1)))
                y = ln_y[:, i % 2, :]
                dve(stt(y, x[:, i, :], alpha, y, ALU.mult, ALU.add).then_inc(dve_done, 1), dve_done)
                if i == 0:
                    eng.wait_ge(ln_in, 32)
                layer_norm_tile(dve, eng, dve_done, ln_sd, ln_var, i, y, x[:, i, :], ln_g, ln_b, stats, mv, rstd, ln_done)

    @block.tensor
    def _(eng):
        mm = eng.matmul

        def chain(out, pairs):
            for n, (lhs, rhs) in enumerate(pairs):
                ins = mm(out, lhs, rhs, start=n == 0, stop=n == len(pairs) - 1)
            return ins

        def project(step, kind, c0, width, c, n=P):
            w = weights(eng, kind, c0, width)
            if A.reused(step):
                eng.wait_ge(act_bank_copied, A.last_user(step))
            b = A.bank(step)
            chain(b[0:n, :], [(w[:, k, c:c + n], xT[:, k, :]) for k in range(8)]).then_inc(act_bank_full, 1)

        def flip(out, src):
            return eng.transpose(out, src, ident[:, :])

        branch_in = {3: odT, 2: cgT, 1: qT, 0: uT}
        ukv = w_ukv.rearrange("p (h n) -> p h n", h=4)

        for step in plan:
            kind, a = step[0], step[1:]
            if kind == "xt":
                ring, full, copied = (A, act_bank_full, act_bank_copied) if step in A.number else (V, dve_bank_full, dve_bank_copied)
                if ring.reused(step):
                    eng.wait_ge(copied, ring.last_user(step))
                b = ring.bank(step)
                for i in range(4):
                    src = x[:, i, :].rearrange("p (m k) -> p k m", k=8)[:, a[0], :]
                    ins = flip(b[:, toks(i)], src)
                ins.then_inc(full, 1)
            elif kind == "lr":
                eng.wait_ge(act_bank_copied, A.nth(("xt", 7)))
                eng.wait_ge(dve_bank_copied, V.nth(("xt", 6)))
                project(step, "in", COL_LR, 272, 0, 16)
            elif kind == "qd":
                project(step, "in", COL_LR, 272, 16 + P * a[0])
            elif kind == "kvd":
                project(step, "in", COL_KVD, 256, 0)
            elif kind == "kr":
                project(step, "in", COL_KVD, 256, P)
            elif kind == "krs":
                if V.reused(step):
                    eng.wait_ge(dve_bank_copied, V.last_user(step))
                b = V.bank(step)
                eng.wait_ge(act_bank_copied, A.nth(("kr",)))
                chain(b[:, :], [(half_swap[:, :], kr)]).then_inc(dve_bank_full, 1)
            elif kind == "rq":
                if A.reused(step):
                    eng.wait_ge(act_bank_copied, A.last_user(step))
                b = A.bank(step)
                eng.wait_ge(act_bank_copied, A.nth(("qd", 1)))
                chain(b[:, :], [(ones[:, :], ml_t1[:, t, :]) for t in range(2)]).then_inc(act_bank_full, 1)
            elif kind == "rk":
                if A.reused(step):
                    eng.wait_ge(act_bank_copied, A.last_user(step))
                b = A.bank(step)
                eng.wait_ge(act_bank_copied, A.nth(("kvd",)))
                chain(b[:, :], [(ones[:, :], ml_t2)]).then_inc(act_bank_full, 1)
            elif kind == "mqn":
                if A.reused(step):
                    eng.wait_ge(act_bank_copied, A.last_user(step))
                b = A.bank(step)
                eng.wait_ge(normed, 1)
                eng.wait_ge(params_in, 16 * 16)
                chain(b[:, :], [(w_uq[:, k, toks(a[0])], qd[:, k, :]) for k in range(2)]).then_inc(act_bank_full, 1)
            elif kind == "mkn":
                if A.reused(step):
                    eng.wait_ge(act_bank_copied, A.last_user(step))
                b = A.bank(step)
                eng.wait_ge(normed, 2)
                chain(b[:, :], [(ukv[:, a[0], 0:P], kvd)]).then_inc(act_bank_full, 1)
            elif kind == "mqr":
                if A.reused(step):
                    eng.wait_ge(act_bank_copied, A.last_user(step))
                b = A.bank(step)
                t = a[0]
                chain(b[:, :], [(w_uq[:, k, 512 + P * t:640 + P * t], qd[:, k, :]) for k in range(2)]).then_inc(act_bank_full, 1)
            elif kind == "mqs":
                if V.reused(step):
                    eng.wait_ge(dve_bank_copied, V.last_user(step))
                b = V.bank(step)
                eng.wait_ge(act_bank_copied, A.nth(("mqr", a[0])))
                chain(b[:, :], [(half_swap[:, :], qr[:, a[0], :])]).then_inc(dve_bank_full, 1)
            elif kind == "mv":
                if A.reused(step):
                    eng.wait_ge(act_bank_copied, A.last_user(step))
                b = A.bank(step)
                chain(b[:, :], [(kvd[:, toks(a[0])], ukv[:, :, P:2 * P])]).then_inc(act_bank_full, 1)
            elif kind == "ms":
                i, h = a
                n, rows = P * (i + 1), slice(64 * (h % 2), 64 * (h % 2) + 64)
                if A.reused(step):
                    eng.wait_ge(act_bank_copied, A.last_user(step))
                b = A.bank(step)
                eng.wait_ge(act_bank_copied, A.nth(("mv", 3)))
                eng.wait_ge(rope_ready, 3)
                chain(b[:, 0:n], [(qn[:, h, toks(i)], kn[:, h, 0:n]), (qr[rows, h // 2, toks(i)], kr[rows, 0:n])]).then_inc(act_bank_full, 1)
            elif kind == "mp":
                i, h = a
                u = 4 * i + h
                if A.reused(step):
                    eng.wait_ge(act_bank_copied, A.last_user(step))
                b = A.bank(step)
                eng.wait_ge(probs_ready, u + 1)
                for kb in range(i + 1):
                    ins = flip(b[:, toks(kb)], mP[:, u % 2, toks(kb)])
                ins.then_inc(act_bank_full, 1)
            elif kind == "mo":
                i, h = a
                u = 4 * i + h
                if A.reused(step):
                    eng.wait_ge(act_bank_copied, A.last_user(step))
                b = A.bank(step)
                eng.wait_ge(act_bank_copied, A.nth(("mp", i, h)))
                chain(b[:, 0:P], [(vm[:, kb, toks(h)], mPT[:, u % 2, kb, :]) for kb in range(i + 1)]).then_inc(act_bank_full, 1)
            elif kind == "q":
                project(step, "in", COL_Q + a[0] // 2 * BLK, BLK, a[0] % 2 * P)
            elif kind == "k":
                project(step, "in", COL_K, BLK, 0)
            elif kind == "v":
                w = weights(eng, "in", COL_K, BLK)
                if A.reused(step):
                    eng.wait_ge(act_bank_copied, A.last_user(step))
                b = A.bank(step)
                for i in range(4):
                    ins = chain(b[:, toks(i)], [(xT[:, k, toks(i)], w[:, k, P:2 * P]) for k in range(8)])
                ins.then_inc(act_bank_full, 1)
            elif kind in ("u", "cg"):
                project(step, "in", {"u": COL_U, "cg": COL_CG}[kind] + a[0] // 2 * BLK, BLK, a[0] % 2 * P)
            elif kind in ("cq", "ck"):
                project(step, "in", COL_CQ + (BLK if kind == "ck" else 0), BLK, a[0] * P)
            elif kind == "cv":
                if A.reused(step):
                    eng.wait_ge(act_bank_copied, A.last_user(step))
                b = A.bank(step)
                for half in range(2):
                    w = weights(eng, "in", COL_CV + half * BLK, BLK)
                    ins = chain(b[:, half * BLK:(half + 1) * BLK], [(xT[:, k, toks(a[0])], w[:, k, :]) for k in range(8)])
                ins.then_inc(act_bank_full, 1)
            elif kind == "lg":
                for t in range(2):
                    if V.reused(("lg", t)):
                        eng.wait_ge(dve_bank_copied, V.last_user(("lg", t)))
                    b = V.bank(("lg", t))
                    eng.wait_ge(act_bank_copied, A.nth(("lr",)))
                    chain(b[:, :], [(w_lr2[:, t * P:(t + 1) * P], lrT[:, :])]).then_inc(dve_bank_full, 1)
            elif kind == "krt":
                eng.wait_ge(gdec_ready, 1)
                if A.reused(step):
                    eng.wait_ge(act_bank_copied, A.last_user(step))
                b = A.bank(step)
                for n in range(4):
                    i, t = 2 * a[0] + n // 2, n % 2
                    ins = flip(b[:, toks(n)], gtmp[:, t, toks(i)])
                ins.then_inc(act_bank_full, 1)
            elif kind == "kv":
                t = a[0]
                eng.wait_ge(act_bank_copied, A.nth(("krt", 1)))
                eng.wait_ge(act_bank_copied, A.nth(("cv", 3)))
                for par in (1, 0):
                    if V.reused(("kv", t, par)):
                        eng.wait_ge(dve_bank_copied, V.last_user(("kv", t, par)))
                    b = V.bank(("kv", t, par))
                    chunks = range(par, 7, 2)
                    rows = slice(64 * par, 64 * par + 64)
                    for c in chunks:
                        for hh in range(2):
                            out = b[64 * hh:64 * hh + 64, (c // 2) * P:(c // 2 + 1) * P]
                            h = 2 * t + hh
                            ins = chain(out, [(kremN[rows, c // 2, t, 64 * hh:64 * hh + 64], cv[rows, c // 2, toks(h)])])
                    ins.then_inc(dve_bank_full, 1)
            elif kind == "att":
                h = a[0]
                rows = slice(64 * (h % 2), 64 * (h % 2) + 64)
                if V.reused(step):
                    eng.wait_ge(dve_bank_copied, V.last_user(step))
                b = V.bank(step)
                eng.wait_ge(gdec_ready, 1)
                for i in range(4):
                    ins = chain(b[:, toks(i)], [(ck[rows, h // 2, toks(i)], cq[rows, h // 2, toks(i)])])
                ins.then_inc(dve_bank_full, 1)
            elif kind == "go":
                h = a[0]
                rows = slice(64 * (h % 2), 64 * (h % 2) + 64)
                if A.reused(step):
                    eng.wait_ge(act_bank_copied, A.last_user(step))
                b = A.bank(step)
                eng.wait_ge(dve_bank_copied, V.nth(("att", h)))
                for i in range(4):
                    mm(b[:, toks(i)], cv[:, i, toks(h)], attT[:, h % 2, toks(i)], start=True, stop=False,
                       skip_group_check=True)
                    for c in (2 * i, 2 * i + 1):
                        if c:
                            ins = mm(b[:, c * 64:c * 64 + 64], gstate[rows, h // 2, c - 1, :], cq[rows, h // 2, c * 64:c * 64 + 64],
                                     start=False, stop=c % 2 == 1, skip_group_check=True)
                ins.then_inc(act_bank_full, 1)
            elif kind == "gc":
                if A.reused(step):
                    eng.wait_ge(act_bank_copied, A.last_user(step))
                b = A.bank(step)
                eng.wait_ge(act_bank_copied, A.nth(("go", a[0])))
                chain(b[:, :], [(centre[:, :], oT[:, a[0] % 2, :])]).then_inc(act_bank_full, 1)
            elif kind == "gv":
                if A.reused(step):
                    eng.wait_ge(act_bank_copied, A.last_user(step))
                b = A.bank(step)
                eng.wait_ge(act_bank_copied, A.nth(("gc", a[0])))
                chain(b[:, :], [(ones[:, :], osq[:, a[0] % 2, :])]).then_inc(act_bank_full, 1)
            elif kind == "gate":
                n, dt = a
                w = weights(eng, "in", COL_GATE + n * 1024 + dt // 2 * BLK, BLK)
                if A.reused(step):
                    eng.wait_ge(act_bank_copied, A.last_user(step))
                b = A.bank(step)
                chain(b[:, :], [(w[:, k, dt % 2 * P:dt % 2 * P + P], xT[:, k, :]) for k in range(8)]).then_inc(act_bank_full, 1)
            elif kind == "mix":
                n, dt = a
                if n == 3:
                    eng.wait_ge(act_bank_copied, A.nth(("mo", 3, 3)))
                elif n == 2:
                    eng.wait_ge(gout_ready, 4)
                elif n == 1:
                    eng.wait_ge(act_bank_copied, A.nth(("so", 3, 1, 1)))
                else:
                    eng.wait_ge(glu_ready, 1)
                w = weights(eng, "branch", n, dt // 4 * 512)
                if V.reused(step):
                    eng.wait_ge(dve_bank_copied, V.last_user(step))
                b = V.bank(step)
                chain(b[:, :], [(w[:, k, dt % 4 * P:dt % 4 * P + P], branch_in[n][:, k, :]) for k in range(4)]).then_inc(dve_bank_full, 1)
            elif kind == "ss":
                i, g, jp = a
                w = P if i == 0 else 2 * P
                rows, k0 = slice(64 * g, 64 * g + 64), P * (i + 1) - w
                if V.reused(step):
                    eng.wait_ge(dve_bank_copied, V.last_user(step))
                b = V.bank(step)
                for j in range(2):
                    ins = chain(b[:, j * w:(j + 1) * w], [(qT[rows, 2 * jp + j, toks(i)], kT[rows, k0:k0 + w])])
                ins.then_inc(dve_bank_full, 1)
            elif kind == "sp":
                i, g, jp = a
                u = 4 * i + 2 * g + jp
                nb = 2 if i == 0 else 4
                if A.reused(step):
                    eng.wait_ge(act_bank_copied, A.last_user(step))
                b = A.bank(step)
                eng.wait_ge(win_probs, u + 1)
                for n in range(nb):
                    ins = flip(b[:, toks(n)], sP[:, u % 2, toks(n)])
                ins.then_inc(act_bank_full, 1)
            elif kind == "so":
                i, g, jp = a
                u = 4 * i + 2 * g + jp
                kb = [0] if i == 0 else [i - 1, i]
                if A.reused(step):
                    eng.wait_ge(act_bank_copied, A.last_user(step))
                b = A.bank(step)
                eng.wait_ge(act_bank_copied, A.nth(("sp", i, g, jp)))
                for j in range(2):
                    ins = chain(b[64 * g:64 * g + 64, toks(j)],
                          [(v_nat[:, blk, 64 * g:64 * g + 64], sPT[:, u % 2, j * len(kb) + n, :]) for n, blk in enumerate(kb)])
                ins.then_inc(act_bank_full, 1)
            elif kind == "s5_mats":
                Tt = a[0]
                eng.wait_ge(s5_bx, 1)
                eng.wait_ge(s5_in, 16 * 6)
                srcs = [bxr[:, 4 * Tt:4 * Tt + 4, :].rearrange("p a b -> p (a b)"),
                        bxi[:, 4 * Tt:4 * Tt + 4, :].rearrange("p a b -> p (a b)"), cre[:, Tt, :], cim[:, Tt, :]]
                for m, src in enumerate(srcs):
                    if A.reused(("mat", Tt, m)):
                        eng.wait_ge(act_bank_copied, A.last_user(("mat", Tt, m)))
                    b = A.bank(("mat", Tt, m))
                    flip(b[:, 0:P], src).then_inc(act_bank_full, 1)
            elif kind == "bu":
                i = a[0]
                rows = slice(32 * (i % 4), 32 * (i % 4) + 32)
                eng.wait_ge(act_bank_copied, A.nth(("mat", 3, 3)))
                for m, mat in enumerate((btr, bti)):
                    if V.reused(("bu", i, m)):
                        eng.wait_ge(dve_bank_copied, V.last_user(("bu", i, m)))
                    b = V.bank(("bu", i, m))
                    chain(b[:, :], [(mat[rows, i // 4, :], uT[rows, i // 4, :])]).then_inc(dve_bank_full, 1)
            elif kind == "y":
                i = a[0]
                rows = slice(32 * (i % 4), 32 * (i % 4) + 32)
                eng.wait_ge(s5_state, i + 1)
                if i % 4 == 0 and i:
                    eng.wait_ge(y_taken, i // 4)
                mm(y_bank[rows, :], cxr[:, i, :], sr[:, i % 2, :], start=True, stop=False)
                mm(y_bank[rows, :], cxi[:, i, :], si[:, i % 2, :], start=False, stop=True).then_inc(y_step, 1)
            elif kind == "glu":
                w = weights(eng, "glu", a[0] // 2 * BLK, BLK)
                if A.reused(step):
                    eng.wait_ge(act_bank_copied, A.last_user(step))
                b = A.bank(step)
                eng.wait_ge(gelu_done, 1)
                chain(b[:, :], [(w[:, k, a[0] % 2 * P:a[0] % 2 * P + P], uT[:, k, :]) for k in range(4)]).then_inc(act_bank_full, 1)
            elif kind == "wo":
                i, half = a
                if A.reused(step):
                    eng.wait_ge(act_bank_copied, A.last_user(step))
                b = A.bank(step)
                eng.wait_ge(mix_used, 32)
                for c in range(2):
                    w = weights(eng, "out", (2 * half + c) * BLK, BLK)
                    ins = chain(b[:, c * BLK:(c + 1) * BLK], [(mx_all[:, k, toks(i)], w[:, k, :]) for k in range(8)])
                ins.then_inc(act_bank_full, 1)


def layer_norm_tile(dve, eng, dve_done, act_sd, var_ready, n, y, out, g, b, stats, mv, rstd, done):
    if dve.latest:
        eng.wait_ge(*dve.latest)
    for half in range(2):
        dve(eng.bn_stats(stats[:, 6 * half:6 * half + 6], y[:, 512 * half:512 * half + 512]).then_inc(dve_done, 1), dve_done)
    eng.wait_ge(*dve.latest)
    dve(eng.bn_aggr(mv, stats).then_inc(var_ready, 1), var_ready)
    eng.wait_ge(act_sd, n + 1)
    dve(eng.reciprocal(rstd, rstd).then_inc(dve_done, 1), dve_done)
    eng.wait_ge(*dve.latest)
    dve(eng.tensor_scalar(y, y, mv[:, 0:1], rstd, ALU.subtract, ALU.mult).then_inc(dve_done, 1), dve_done)
    eng.wait_ge(*dve.latest)
    dve(eng.tensor_tensor(y, y, g, ALU.mult).then_inc(dve_done, 1), dve_done)
    eng.wait_ge(*dve.latest)
    dve(eng.tensor_tensor(out, y, b, ALU.add).then_inc(done, 1), done)


def routing_plan():
    steps = [("xt", k) for k in range(8)] + [("rt", i) for i in range(4)] + [("pt", 0), ("pt", 1), ("sg", 0)]
    steps += [("cnt", i) for i in range(4)] + [("tot",)]
    for i in range(4):
        if i:
            steps.append(("sg", i))
        steps += [("pg", i, 0), ("sh", i), ("pp", i, 0), ("pg", i, 1), ("sd", i, 0), ("sd", i, 1), ("pp", i, 1)]
    return steps


def build_routing(nc, ctx, T, layer, W, keep, sem):
    alpha, x, ident, ones = T["alpha"], keep["x"], keep["ident"], keep["ones"]
    plan = routing_plan()
    keys_act = [s for s in plan if s[0] in ("rt", "pt", "pg", "sh") or (s[0] == "xt" and s[1] % 2)]
    keys_dve = [s for s in plan if s[0] in ("cnt", "tot", "pp", "sg", "sd") or (s[0] == "xt" and not s[1] % 2)]

    def sb(name, shape, dt=F32):
        return ctx.enter_context(nc.sbuf_tensor("route_" + name, shape, dt))

    x1T = sb("x1T", [P, 8, 512])
    w_router, bias = sb("w_router", [P, 8, 64]), sb("bias", [P, 64])
    sh_gu, sh_dn = sb("sh_gu", [P, 8, 512]), sb("sh_dn", [P, 2, 1024])
    ple_w, ple_gate = sb("ple_w", [P, 2, 1024]), sb("ple_gate", [P, 8, 1024])
    p_nat, pT = sb("p_nat", [P, 4, 256]), sb("pT", [P, 2, 512])
    score, biased, left = sb("score", [P, 4, 64]), sb("biased", [P, 4, 64]), sb("left", [P, 4, 64])
    sel, wgt, code = sb("sel", [P, 4, 64]), sb("wgt", [P, 4, 64]), sb("code", [P, 4, 64])
    top, codes = sb("top", [P, 4, 8]), sb("codes", [P, 4, 8])
    wsum, most = sb("wsum", [P, 4]), sb("most_f", [P, 1])
    match = sb("match", [P, 8, 64])
    slot_id, expert_part = sb("slot_id", [P, 4, 8], I32), sb("expert_part", [P, 4, 8], I32)
    round_id = sb("round_id", [P, 4, 8], I32)
    before, expert_code, token_id = sb("before", [P, P]), sb("expert_code", [P, 64]), sb("token_id", [P, 4], I32)
    gate = sb("ple_sigmoid", [P, 2, 512])
    silu, h, hT = sb("silu", [P, 2, 256]), sb("h", [P, 2, 256]), sb("hT", [P, 2, 2, P])

    pa = [ctx.enter_context(nc.psum_tensor(f"route_act_bank{n}", [P, 512], F32)) for n in range(4)]
    pv = [ctx.enter_context(nc.psum_tensor(f"route_dve_bank{n}", [P, 512], F32)) for n in range(4)]
    A, V = Ring(pa, keys_act), Ring(pv, keys_dve)
    act_bank_full, act_bank_copied = sem("act_bank_full"), sem("act_bank_copied")
    dve_bank_full, dve_bank_copied = sem("dve_bank_full"), sem("dve_bank_copied")
    dve_done, act_done = sem("dve_done"), sem("act_done")
    router_in, shared_in, ple_in, tables_in = (sem(n) for n in ("router_in", "shared_in", "ple_in", "tables_in"))
    cleared, listed = sem("token_table_cleared"), sem("tokens_listed")
    chosen, slots_ready, silu_done, h_ready, summed = (
        sem(n) for n in ("experts_chosen", "slots_ready", "silu_done", "h_ready", "embedding_added"))

    def toks(i, n=P):
        return slice(i * n, i * n + n)

    block = ctx.enter_context(nc.Block())

    @block.sync
    def _(eng):
        def load(dst, src, done):
            eng.dma_start(dst, src).then_inc(done, 16)

        rows = "(p k) n -> p k n"
        load(w_router[:, :, :], W["router_w"][layer].rearrange(rows, p=P), router_in)
        load(bias[:, :], W["router_bias"][layer].partition_broadcast(P), router_in)
        load(before[:, :], T["before"], tables_in)
        load(expert_code[:, :], T["expert_code"], tables_in)
        load(token_id[:, :], T["token_id"], tables_in)
        load(p_nat[:, :, :], W["p"][layer, 0].rearrange("(i p) n -> p i n", p=P), tables_in)
        load(sh_gu[:, :, 0:256], W["sh_w_gate"][layer].rearrange(rows, p=P), shared_in)
        load(sh_gu[:, :, 256:512], W["sh_w_up"][layer].rearrange(rows, p=P), shared_in)
        load(sh_dn[:, :, :], W["sh_w_down"][layer].rearrange("(k p) n -> p k n", p=P), shared_in)
        load(ple_gate[:, :, :], W["ple_gate_w"][layer].rearrange(rows, p=P), ple_in)
        load(ple_w[:, :, :], W["ple_w"][layer].rearrange("(k p) n -> p k n", p=P), ple_in)

    @block.gpsimd
    def _(eng):
        eng.dma_start(T["token_table"].rearrange("(p n) o -> p (n o)", p=P), T["no_token"]).then_inc(cleared, 16)
        eng.wait_ge(cleared, 16)
        eng.wait_ge(tables_in, 64)
        for i in range(4):
            eng.wait_ge(slots_ready, i + 1)
            for k in range(TOP_K):
                eng.indirect_dma_start(T["token_table"], bass.IndirectOffsetOnAxis(slot_id[:, i, k:k + 1], 0),
                                       token_id[:, i:i + 1], None).then_inc(listed, 16)
        eng.wait_ge(listed, 16 * 4 * TOP_K)

    @block.scalar
    def _(eng):
        act = Count()
        n_gate = 0
        for step in plan:
            kind, a = step[0], step[1:]
            if kind == "xt" and step in A.number:
                eng.wait_ge(act_bank_full, A.nth(step))
                b = A.bank(step)
                act(eng.copy(x1T[:, a[0], :], b[:, :]).then_inc(act_bank_copied, 1), act_bank_copied)
            elif kind == "rt":
                eng.wait_ge(act_bank_full, A.nth(step))
                b = A.bank(step)
                act(eng.activation(score[:, a[0], :], b[:, 0:64], ACT.Sigmoid).then_inc(act_bank_copied, 1), act_bank_copied)
            elif kind == "pt":
                eng.wait_ge(act_bank_full, A.nth(step))
                b = A.bank(step)
                act(eng.copy(pT[:, a[0], :], b[:, :]).then_inc(act_bank_copied, 1), act_bank_copied)
            elif kind == "pg":
                if n_gate >= 2:
                    eng.wait_ge(summed, n_gate - 1)
                eng.wait_ge(act_bank_full, A.nth(step))
                b = A.bank(step)
                act(eng.activation(gate[:, n_gate % 2, :], b[:, :], ACT.Sigmoid).then_inc(act_bank_copied, 1), act_bank_copied)
                n_gate += 1
            elif kind == "sg":
                if a[0] >= 2:
                    eng.wait_ge(h_ready, a[0] - 1)
                eng.wait_ge(dve_bank_full, V.nth(step))
                b = V.bank(step)
                act(eng.activation(silu[:, a[0] % 2, :], b[:, 0:256], ACT.Silu).then_inc(silu_done, 1), silu_done)
            elif kind == "sh":
                eng.wait_ge(act_bank_full, A.nth(step))
                b = A.bank(step)
                act(eng.copy(hT[:, a[0] % 2, :, :].rearrange("p a b -> p (a b)"), b[:, 0:256]).then_inc(act_bank_copied, 1), act_bank_copied)

    @block.vector
    def _(eng):
        dve = Count()
        tt, ts, stt = eng.tensor_tensor, eng.tensor_scalar, eng.scalar_tensor_tensor
        n_gate = 0
        for step in plan:
            kind, a = step[0], step[1:]
            if dve.latest:
                eng.wait_ge(*dve.latest)
            if kind == "xt" and step in V.number:
                eng.wait_ge(dve_bank_full, V.nth(step))
                b = V.bank(step)
                dve(eng.tensor_copy(x1T[:, a[0], :], b[:, :]).then_inc(dve_bank_copied, 1), dve_bank_copied)
            elif kind == "rt":
                i = a[0]
                eng.wait_ge(router_in, 32)
                eng.wait_ge(act_bank_copied, A.nth(step))
                dve(tt(biased[:, i, :], score[:, i, :], bias[:, :], ALU.add).then_inc(dve_done, 1), dve_done)
                eng.wait_ge(*dve.latest)
                dve(eng.max(top[:, i, :], biased[:, i, :]).then_inc(dve_done, 1), dve_done)
                eng.wait_ge(*dve.latest)
                dve(eng.match_replace(left[:, i, :], top[:, i, :], biased[:, i, :], MASKED).then_inc(dve_done, 1), dve_done)
                eng.wait_ge(*dve.latest)
                dve(tt(sel[:, i, :], left[:, i, :], biased[:, i, :], ALU.not_equal).then_inc(chosen, 1), chosen)
                eng.wait_ge(*dve.latest)
                dve(tt(wgt[:, i, :], score[:, i, :], sel[:, i, :], ALU.mult).then_inc(dve_done, 1), dve_done)
                eng.wait_ge(*dve.latest)
                dve(eng.reduce_sum(wsum[:, i:i + 1], wgt[:, i, :], AX.X).then_inc(dve_done, 1), dve_done)
                eng.wait_ge(*dve.latest)
                dve(eng.reciprocal(wsum[:, i:i + 1], wsum[:, i:i + 1]).then_inc(dve_done, 1), dve_done)
                eng.wait_ge(*dve.latest)
                dve(ts(wgt[:, i, :], wgt[:, i, :], wsum[:, i:i + 1], ROUTED_SCALE, ALU.mult, ALU.mult).then_inc(dve_done, 1), dve_done)
            elif kind == "cnt":
                i = a[0]
                eng.wait_ge(dve_bank_full, V.nth(step))
                b = V.bank(step)
                if i == 0:
                    eng.wait_ge(tables_in, 64)
                dve(stt(code[:, i, :], b[:, 0:64], 64.0, expert_code[:, :], ALU.mult, ALU.add).then_inc(dve_bank_copied, 1), dve_bank_copied)
                eng.wait_ge(*dve.latest)
                dve(tt(code[:, i, :], code[:, i, :], sel[:, i, :], ALU.mult).then_inc(dve_done, 1), dve_done)
                eng.wait_ge(*dve.latest)
                dve(eng.max(codes[:, i, :], code[:, i, :]).then_inc(dve_done, 1), dve_done)
                eng.wait_ge(*dve.latest)
                dve(ts(slot_id[:, i, :], codes[:, i, :], -1.0, None, ALU.add).then_inc(slots_ready, 1), slots_ready)
                dve(tt(match[:, :, :], code[:, i, :].unsqueeze(1).to_broadcast((P, 8, 64)),
                       codes[:, i, :].unsqueeze(2).to_broadcast((P, 8, 64)), ALU.is_equal).then_inc(dve_done, 1), dve_done)
                eng.wait_ge(*dve.latest)
                dve(tt(match[:, :, :], match[:, :, :], wgt[:, i, :].unsqueeze(1).to_broadcast((P, 8, 64)), ALU.mult).then_inc(dve_done, 1), dve_done)
                eng.wait_ge(*dve.latest)
                dve(eng.reduce_sum(keep["pick_w"][:, i, :], match[:, :, :], AX.X).then_inc(dve_done, 1), dve_done)
                dve(ts(expert_part[:, i, :], slot_id[:, i, :], 63, 7, ALU.bitwise_and, ALU.logical_shift_left).then_inc(dve_done, 1), dve_done)
                dve(ts(keep["pick_row"][:, i, :], slot_id[:, i, :], 6, SLOTS - 1, ALU.logical_shift_right, ALU.bitwise_and).then_inc(dve_done, 1), dve_done)
                dve(ts(round_id[:, i, :], slot_id[:, i, :], 13, None, ALU.logical_shift_right).then_inc(dve_done, 1), dve_done)
                eng.wait_ge(*dve.latest)
                dve(tt(keep["pick_row"][:, i, :], keep["pick_row"][:, i, :], expert_part[:, i, :], ALU.bitwise_or).then_inc(dve_done, 1), dve_done)
                dve(eng.tensor_copy(keep["pick_round"][:, i, :], round_id[:, i, :]).then_inc(dve_done, 1), dve_done)
            elif kind == "tot":
                eng.wait_ge(dve_bank_full, V.nth(step))
                b = V.bank(step)
                dve(eng.reduce_max(most[:, :], b[:, 0:64], AX.X).then_inc(dve_bank_copied, 1), dve_bank_copied)
                eng.wait_ge(*dve.latest)
                dve(eng.tensor_copy(keep["most"][:, :], most[:, :]).then_inc(dve_done, 1), dve_done)
                dve(eng.memset(keep["round_now"][:, :], 0.0).then_inc(dve_done, 1), dve_done)
            elif kind == "pp":
                i, half = a
                eng.wait_ge(dve_bank_full, V.nth(step))
                b = V.bank(step)
                eng.wait_ge(act_bank_copied, A.nth(("pg", i, half)))
                g = gate[:, n_gate % 2, :]
                n_gate += 1
                dve(tt(g, g, b[:, :], ALU.mult).then_inc(dve_bank_copied, 1), dve_bank_copied)
                eng.wait_ge(*dve.latest)
                xs = x[:, i, 512 * half:512 * half + 512]
                dve(tt(xs, xs, g, ALU.add).then_inc(summed, 1), summed)
            elif kind == "sg":
                i = a[0]
                eng.wait_ge(dve_bank_full, V.nth(step))
                dve(ts(x[:, i, :], x[:, i, :], alpha, None, ALU.mult).then_inc(dve_done, 1), dve_done)
                eng.wait_ge(silu_done, i + 1)
                dve(tt(h[:, i % 2, :], silu[:, i % 2, :], V.bank(step)[:, 256:512], ALU.mult).then_inc(dve_bank_copied, 1), dve_bank_copied)
                eng.wait_ge(*dve.latest)
                dve(eng.memset(left[:, 0, 0:1], 0.0).then_inc(h_ready, 1), h_ready)
            elif kind == "sd":
                i, half = a
                eng.wait_ge(dve_bank_full, V.nth(step))
                b = V.bank(step)
                xs = x[:, i, 512 * half:512 * half + 512]
                dve(tt(xs, xs, b[:, :], ALU.add).then_inc(dve_bank_copied, 1), dve_bank_copied)

    @block.tensor
    def _(eng):
        mm = eng.matmul

        def chain(out, pairs):
            for n, (lhs, rhs) in enumerate(pairs):
                ins = mm(out, lhs, rhs, start=n == 0, stop=n == len(pairs) - 1)
            return ins

        def flip(out, src):
            return eng.transpose(out, src, ident[:, :])

        for step in plan:
            kind, a = step[0], step[1:]
            if kind == "xt":
                ring, full, copied = (A, act_bank_full, act_bank_copied) if step in A.number else (V, dve_bank_full, dve_bank_copied)
                if ring.reused(step):
                    eng.wait_ge(copied, ring.last_user(step))
                b = ring.bank(step)
                for i in range(4):
                    ins = flip(b[:, toks(i)], x[:, i, :].rearrange("p (m k) -> p k m", k=8)[:, a[0], :])
                ins.then_inc(full, 1)
            elif kind == "rt":
                eng.wait_ge(act_bank_copied, A.nth(("xt", 7)))
                eng.wait_ge(dve_bank_copied, V.nth(("xt", 6)))
                eng.wait_ge(router_in, 32)
                if A.reused(step):
                    eng.wait_ge(act_bank_copied, A.last_user(step))
                b = A.bank(step)
                chain(b[:, 0:64], [(x1T[:, k, toks(a[0])], w_router[:, k, :]) for k in range(8)]).then_inc(act_bank_full, 1)
            elif kind == "pt":
                eng.wait_ge(tables_in, 64)
                if A.reused(step):
                    eng.wait_ge(act_bank_copied, A.last_user(step))
                b = A.bank(step)
                for i in range(4):
                    ins = flip(b[:, toks(i)], p_nat[:, i, toks(a[0])])
                ins.then_inc(act_bank_full, 1)
            elif kind == "sg":
                eng.wait_ge(shared_in, 48)
                if V.reused(step):
                    eng.wait_ge(dve_bank_copied, V.last_user(step))
                b = V.bank(step)
                chain(b[:, :], [(x1T[:, k, toks(a[0])], sh_gu[:, k, :]) for k in range(8)]).then_inc(dve_bank_full, 1)
            elif kind == "cnt":
                i = a[0]
                if V.reused(step):
                    eng.wait_ge(dve_bank_copied, V.last_user(step))
                b = V.bank(step)
                eng.wait_ge(chosen, i + 1)
                chain(b[:, 0:64], [(ones[:, :], sel[:, j, :]) for j in range(i)] + [(before[:, :], sel[:, i, :])]).then_inc(dve_bank_full, 1)
            elif kind == "tot":
                if V.reused(step):
                    eng.wait_ge(dve_bank_copied, V.last_user(step))
                b = V.bank(step)
                chain(b[:, 0:64], [(ones[:, :], sel[:, j, :]) for j in range(4)]).then_inc(dve_bank_full, 1)
            elif kind == "pg":
                i, half = a
                eng.wait_ge(ple_in, 32)
                if A.reused(step):
                    eng.wait_ge(act_bank_copied, A.last_user(step))
                b = A.bank(step)
                chain(b[:, :], [(x1T[:, k, toks(i)], ple_gate[:, k, 512 * half:512 * half + 512]) for k in range(8)]).then_inc(act_bank_full, 1)
            elif kind == "pp":
                i, half = a
                eng.wait_ge(act_bank_copied, A.nth(("pt", 1)))
                if V.reused(step):
                    eng.wait_ge(dve_bank_copied, V.last_user(step))
                b = V.bank(step)
                chain(b[:, :], [(pT[:, k, toks(i)], ple_w[:, k, 512 * half:512 * half + 512]) for k in range(2)]).then_inc(dve_bank_full, 1)
            elif kind == "sh":
                i = a[0]
                if A.reused(step):
                    eng.wait_ge(act_bank_copied, A.last_user(step))
                b = A.bank(step)
                eng.wait_ge(h_ready, i + 1)
                for k in range(2):
                    ins = flip(b[:, toks(k)], h[:, i % 2, toks(k)])
                ins.then_inc(act_bank_full, 1)
            elif kind == "sd":
                i, half = a
                eng.wait_ge(act_bank_copied, A.nth(("sh", i)))
                if V.reused(step):
                    eng.wait_ge(dve_bank_copied, V.last_user(step))
                b = V.bank(step)
                chain(b[:, :], [(hT[:, i % 2, k, :], sh_dn[:, k, 512 * half:512 * half + 512]) for k in range(2)]).then_inc(dve_bank_full, 1)


def build_expert_rounds(nc, T, layer, W, keep):
    most = nc.values_load(keep["most"][0:1, 0:1], min_val=0, max_val=512)
    with nc.Fori(0, 512 // SLOTS) as r:
        with nc.If(most > r * SLOTS):
            phase(nc, build_experts, T, layer, W, keep, r)
            phase(nc, build_combination, T, keep)
        with nc.Else():
            for e in (nc.sync, nc.scalar, nc.vector, nc.gpsimd, nc.tensor):
                e.nop()
        nc.all_engine_barrier()


def build_experts(nc, ctx, T, layer, W, keep, r, sem):
    n_exp = W["exp_w_gate"].shape[1]
    R = EXPERT_RING
    ident = keep["ident"]

    def sb(name, shape, dt=F32):
        return ctx.enter_context(nc.sbuf_tensor("expert_" + name, shape, dt))

    w_gu, w_dn = sb("w_gu", [P, R, 2, 8, 256]), sb("w_dn", [P, R, 2, 1024])
    tokens, token_col = sb("tokens", [P, n_exp], I32), sb("token_col", [P, 2], I32)
    xg, xgT = sb("xg", [P, 2, 1024]), sb("xgT", [P, 2, 8, P])
    silu, h, hT = sb("silu", [P, 2, 256]), sb("h", [P, 2, 256]), sb("hT", [P, 2, P])
    y = sb("y", [P, 2, 1024])
    bx = [ctx.enter_context(nc.psum_tensor(f"expert_x_bank{n}", [P, 512], F32)) for n in range(2)]
    bg = [ctx.enter_context(nc.psum_tensor(f"expert_gu_bank{n}", [P, 512], F32)) for n in range(2)]
    bh = ctx.enter_context(nc.psum_tensor("expert_h_bank", [P, 512], F32))
    by = [ctx.enter_context(nc.psum_tensor(f"expert_y_bank{n}", [P, 512], F32)) for n in range(2)]

    tokens_in = sem("tokens_in")
    gu_in, dn_in = [sem(f"gate_up_in{n}") for n in range(R)], [sem(f"down_in{n}") for n in range(R)]
    col_ready, col_seen = sem("token_col_ready"), sem("token_col_seen")
    x_in = [sem(f"x_in{n}") for n in range(2)]
    x_full, x_copied = [sem(f"xT_full{n}") for n in range(2)], [sem(f"xT_copied{n}") for n in range(2)]
    gu_full, silu_done, h_ready, h_full, h_copied = (
        sem(n) for n in ("gate_up_full", "silu_done", "h_ready", "hT_full", "hT_copied"))
    y_full, y_copied = [sem(f"y_full{n}") for n in range(2)], [sem(f"y_copied{n}") for n in range(2)]
    y_stored = [sem(f"y_stored{n}") for n in range(2)]

    def expert_loop(eng, body, ahead):
        with eng.Fori(0, n_exp // R - 1) as i:
            for j in range(R):
                body(i * R + j, i, j, True)
        for j in range(R):
            body(n_exp - R + j, n_exp // R - 1, j, j + ahead < R)

    block = ctx.enter_context(nc.Block())

    @block.sync
    def _(sp):
        gate_w = W["exp_w_gate"][layer].rearrange("e (p k) n -> e p k n", p=P)
        up_w = W["exp_w_up"][layer].rearrange("e (p k) n -> e p k n", p=P)
        down_w = W["exp_w_down"][layer].rearrange("e (k p) n -> e p k n", p=P)

        def load_gu(e, j):
            sp.dma_start(w_gu[:, j, 0, :, :], gate_w[e]).then_inc(gu_in[j], 16)
            sp.dma_start(w_gu[:, j, 1, :, :], up_w[e]).then_inc(gu_in[j], 16)

        def load_dn(e, j):
            sp.dma_start(w_dn[:, j, :, :], down_w[e]).then_inc(dn_in[j], 16)

        table = T["token_table"].rearrange("(r s e) o -> r s (e o)", s=SLOTS, e=n_exp)
        sp.dma_start(tokens[:, :], table[r]).then_inc(tokens_in, 16)
        for n in range(2):
            sp.nop().then_inc(y_stored[n], 16)
        for j in range(R):
            load_gu(j, j)
            load_dn(j, j)

        def body(e, i, j, more):
            if more:
                sp.wait_ge(gu_full, e + 1)
                load_gu(e + R, j)
                sp.wait_ge(y_full[1], e + 1)
                load_dn(e + R, j)
            for n in range(2):
                sp.wait_ge(y_copied[n], e + 2)
            sp.dma_start(T["y_dram"][e], y[:, j % 2, :]).then_inc(y_stored[j % 2], 16)

        expert_loop(sp, body, R)
        for n in range(2):
            sp.wait_ge(y_stored[n], 16 * (n_exp // 2 + 1))

    @block.gpsimd
    def _(pool):
        def gather(e, b):
            pool.tensor_copy(token_col[:, b:b + 1], tokens[:, bass.ds(e, 1)]).then_inc(col_ready, 1)
            pool.wait_ge(col_ready, e + 1)
            pool.sem_inc(col_seen, 1)
            pool.indirect_dma_start(xg[:, b, :], None, T["x1_dram"],
                                    bass.IndirectOffsetOnAxis(token_col[:, b:b + 1], 0)).then_inc(x_in[b], 16)

        pool.wait_ge(tokens_in, 16)
        gather(0, 0)
        gather(1, 1)

        def body(e, i, j, more):
            if more:
                pool.wait_ge(x_full[1], e + 1)
                gather(e + 2, j % 2)

        expert_loop(pool, body, 2)

    @block.tensor
    def _(pe):
        def flip_x(e, i, j):
            b = j % 2
            pe.wait_ge(x_in[b], i * 16 * (R // 2) + 16 * (j // 2 + 1))
            for n in range(2):
                pe.wait_ge(x_copied[n], e + 1)
                for k in range(4):
                    src = xg[:, b, :].rearrange("p (m k) -> p k m", k=8)[:, 4 * n + k, :]
                    ins = pe.transpose(bx[n][:, k * P:(k + 1) * P], src, ident[:, :])
                ins.then_inc(x_full[n], 1)

        def gate_up(e, i, j):
            b = j % 2
            pe.wait_ge(gu_in[j], i * 32 + 32)
            pe.wait_ge(h_ready, e + 1)
            for k in range(8):
                if k % 4 == 0:
                    pe.wait_ge(x_copied[k // 4], e + 2)
                ins = pe.matmul(bg[b][:, :].rearrange("p (a n) -> p a n", a=2), xgT[:, b, k, :], w_gu[:, j, :, k, :],
                                start=k == 0, stop=k == 7)
            ins.then_inc(gu_full, 1)

        def body(e, i, j, more):
            b = j % 2
            nxt = (e + 1, i + 1 if j == R - 1 else i, (j + 1) % R)
            if more:
                flip_x(*nxt)
            pe.wait_ge(h_ready, e + 3)
            pe.wait_ge(h_copied, e + 1)
            for k in range(2):
                ins = pe.transpose(bh[:, k * P:(k + 1) * P], h[:, b, k * P:(k + 1) * P], ident[:, :])
            ins.then_inc(h_full, 1)
            if more:
                gate_up(*nxt)
            pe.wait_ge(h_copied, e + 2)
            pe.wait_ge(dn_in[j], i * 16 + 16)
            for n in range(2):
                pe.wait_ge(y_copied[n], e + 1)
                for k in range(2):
                    ins = pe.matmul(by[n][:, :], hT[:, k, :], w_dn[:, j, k, 512 * n:512 * n + 512], start=k == 0, stop=k == 1)
                ins.then_inc(y_full[n], 1)

        flip_x(0, 0, 0)
        gate_up(0, 0, 0)
        expert_loop(pe, body, 1)

    @block.scalar
    def _(act):
        for s in (x_copied[0], h_copied, y_copied[0]):
            act.nop().then_inc(s, 1)

        def take_x(e, j):
            act.wait_ge(x_full[0], e + 1)
            act.copy(xgT[:, j % 2, 0:4, :].rearrange("p a b -> p (a b)"), bx[0][:, :]).then_inc(x_copied[0], 1)

        def gate(e, j):
            act.wait_ge(gu_full, e + 1)
            act.activation(silu[:, j % 2, :], bg[j % 2][:, 0:256], ACT.Silu).then_inc(silu_done, 1)

        take_x(0, 0)
        gate(0, 0)

        def body(e, i, j, more):
            if more:
                take_x(e + 1, j + 1)
            act.wait_ge(h_full, e + 1)
            act.copy(hT[:, :, :].rearrange("p a b -> p (a b)"), bh[:, 0:256]).then_inc(h_copied, 1)
            if more:
                gate(e + 1, j + 1)
            act.wait_ge(y_full[0], e + 1)
            act.wait_ge(y_stored[j % 2], i * 16 * (R // 2) + 16 * (j // 2 + 1))
            act.copy(y[:, j % 2, 0:512], by[0][:, :]).then_inc(y_copied[0], 1)

        expert_loop(act, body, 1)

    @block.vector
    def _(dve):
        dve.nop().then_inc(h_ready, 2)
        for s in (x_copied[1], y_copied[1]):
            dve.nop().then_inc(s, 1)

        def take_x(e, j):
            dve.wait_ge(x_full[1], e + 1)
            dve.tensor_copy(xgT[:, j % 2, 4:8, :].rearrange("p a b -> p (a b)"), bx[1][:, :]).then_inc(x_copied[1], 1)

        def hidden(e, j):
            dve.wait_ge(silu_done, e + 1)
            dve.tensor_tensor(h[:, j % 2, :], silu[:, j % 2, :], bg[j % 2][:, 256:512], ALU.mult).then_inc(h_ready, 1)

        take_x(0, 0)
        hidden(0, 0)

        def body(e, i, j, more):
            if more:
                take_x(e + 1, j + 1)
                hidden(e + 1, j + 1)
            dve.wait_ge(y_full[1], e + 1)
            dve.wait_ge(y_stored[j % 2], i * 16 * (R // 2) + 16 * (j // 2 + 1))
            dve.tensor_copy(y[:, j % 2, 512:1024], by[1][:, :]).then_inc(y_copied[1], 1)

        expert_loop(dve, body, 1)


def build_combination(nc, ctx, T, keep, sem):
    x = keep["x"]
    NB = 8
    rows = ctx.enter_context(nc.sbuf_tensor("combine_rows", [P, NB, 1024], F32))
    w_now = ctx.enter_context(nc.sbuf_tensor("combine_w", [P, 4, 8], F32))
    row_in = [sem(f"row_in{n}") for n in range(NB)]
    added, dve_done = sem("row_added"), sem("dve_done")
    block = ctx.enter_context(nc.Block())
    y_rows = T["y_dram"].rearrange("e s d -> (e s) d")

    @block.gpsimd
    def _(pool):
        for i in range(4):
            for k in range(TOP_K):
                n = i * TOP_K + k
                if n >= NB:
                    pool.wait_ge(added, n - NB + 1)
                pool.indirect_dma_start(rows[:, n % NB, :], None, y_rows,
                                        bass.IndirectOffsetOnAxis(keep["pick_row"][:, i, k:k + 1], 0)).then_inc(row_in[n % NB], 16)

    @block.vector
    def _(eng):
        dve = Count()
        dve(eng.tensor_scalar(w_now[:, :, :], keep["pick_round"][:, :, :], keep["round_now"][:, :], None, ALU.is_equal).then_inc(dve_done, 1), dve_done)
        eng.wait_ge(*dve.latest)
        dve(eng.tensor_tensor(w_now[:, :, :], w_now[:, :, :], keep["pick_w"][:, :, :], ALU.mult).then_inc(dve_done, 1), dve_done)
        dve(eng.tensor_scalar(keep["round_now"][:, :], keep["round_now"][:, :], 1.0, None, ALU.add).then_inc(dve_done, 1), dve_done)
        for i in range(4):
            for k in range(TOP_K):
                n = i * TOP_K + k
                eng.wait_ge(row_in[n % NB], 16 * (n // NB + 1))
                eng.wait_ge(*dve.latest)
                dve(eng.scalar_tensor_tensor(x[:, i, :], rows[:, n % NB, :], w_now[:, i, k:k + 1], x[:, i, :],
                                             ALU.mult, ALU.add).then_inc(added, 1), added)


def build_last_norm(nc, ctx, T, layer, W, keep, sem):
    x, eps = keep["x"], keep["eps"]

    def sb(name, shape):
        return ctx.enter_context(nc.sbuf_tensor("norm_" + name, shape, F32))

    ln_g, ln_b = sb("ln_g", [P, 1024]), sb("ln_b", [P, 1024])
    stats, mv, rstd = sb("stats", [P, 12]), sb("mv", [P, 2]), sb("rstd", [P, 1])
    ln_in, dve_done = sem("ln_rows_in"), sem("dve_done")
    var_ready, sd_ready, tile_done, stored = (sem(n) for n in ("ln_var_ready", "ln_sd_ready", "ln2_tile_ready", "out_stored"))
    block = ctx.enter_context(nc.Block())

    @block.sync
    def _(sp):
        sp.dma_start(ln_g[:, :], W["ln2_g"][layer].partition_broadcast(P)).then_inc(ln_in, 16)
        sp.dma_start(ln_b[:, :], W["ln2_b"][layer].partition_broadcast(P)).then_inc(ln_in, 16)
        for i in range(4):
            sp.wait_ge(tile_done, i + 1)
            sp.dma_start(T["out"][0, i * P:(i + 1) * P, :], x[:, i, :]).then_inc(stored, 16)
        sp.wait_ge(stored, 64)

    @block.scalar
    def _(act):
        for i in range(4):
            act.wait_ge(var_ready, i + 1)
            act.activation(rstd[:, :], mv[:, 1:2], ACT.Sqrt, bias=eps[:, 0:1]).then_inc(sd_ready, 1)

    @block.vector
    def _(eng):
        dve = Count()
        eng.wait_ge(ln_in, 32)
        for i in range(4):
            layer_norm_tile(dve, eng, dve_done, sd_ready, var_ready, i, x[:, i, :], x[:, i, :], ln_g[:, :], ln_b[:, :],
                            stats[:, :], mv[:, :], rstd[:, :], tile_done)


def phase(nc, build, *args):
    with ExitStack() as ctx:
        sems = []

        def sem(name):
            sems.append(ctx.enter_context(nc.semaphore(name)))
            return sems[-1]

        with ExitStack() as inner:
            build(nc, inner, *args, sem)
        nc.gpsimd.dma_reset()
        nc.all_engine_barrier()
        for s in sems:
            nc.sync.sem_clear(s)
        nc.all_engine_barrier()


def build_constants(nc, ctx, T, keep, sem):
    loaded, made = sem("tables_loaded"), sem("constants_made")
    block = ctx.enter_context(nc.Block())
    names = [n for n in keep if n in T and n != "x"]

    @block.sync
    def _(eng):
        eng.dma_start(keep["x"][:, :, :], T["x"][0].rearrange("(i p) d -> p i d", p=P)).then_inc(loaded, 16)
        for n in names:
            dims = len(keep[n].shape)
            eng.dma_start(keep[n][(slice(None),) * dims], T[n]).then_inc(loaded, 16)
        eng.wait_ge(loaded, 16 * (len(names) + 1))
        eng.wait_ge(made, 4)

    @block.vector
    def _(eng):
        eng.memset(keep["ones"][:, :], 1.0).then_inc(made, 1)
        for n, v in enumerate((LN_EPS, RMS_EPS, TWO_PI / 4)):
            eng.memset(keep["eps"][:, n:n + 1], v).then_inc(made, 1)


def prog(nc, W, T, debug=None):
    depth = W["w_in"].shape[0]
    T["alpha"] = (2 * depth) ** 0.25
    with ExitStack() as ctx:
        def sb(name, shape, dt=F32):
            return ctx.enter_context(nc.sbuf_tensor(name, shape, dt))

        keep = {
            "x": sb("x_now", [P, 4, 1024]), "ident": sb("ident", [P, P]), "ones": sb("ones", [P, P]),
            "eps": sb("eps", [P, 3]), "centre": sb("centre", [P, P]), "half_swap": sb("half_swap", [P, P]),
            "rope_cos": sb("rope_cos", [P, 512]), "rope_sin": sb("rope_sin", [P, 512]),
            "chunk_keep": sb("chunk_keep", [P, 512]), "gla_causal": sb("gla_causal", [P, 4, P], I32),
            "pick_w": sb("pick_w", [P, 4, 8]), "pick_row": sb("pick_row", [P, 4, 8], I32), "most": sb("most", [P, 1], I32),
            "pick_round": sb("pick_round", [P, 4, 8]), "round_now": sb("round_now", [P, 1]),
        }
        T["x1_dram"] = nc.dram_tensor("x1_scratch", (512, 1024), F32, kind="Internal").ap()
        T["token_table"] = nc.dram_tensor("token_table", (512 * 64, 1), I32, kind="Internal").ap()
        T["y_dram"] = nc.dram_tensor("y_scratch", (64, SLOTS, 1024), F32, kind="Internal").ap()
        phase(nc, build_constants, T, keep)
        with nc.Fori(0, depth) as layer:
            phase(nc, build_mixers, T, layer, W, keep)
            if debug is None:
                phase(nc, build_routing, T, layer, W, keep)
                build_expert_rounds(nc, T, layer, W, keep)
                phase(nc, build_last_norm, T, layer, W, keep)


_INS = ['x', 'p', 'w_in', 's5_a_re', 's5_a_im', 's5_log_dt', 's5_b_re', 's5_b_im', 's5_c_re', 's5_c_im', 's5_d',
        's5_w_glu', 'swa_sinks', 'gla_w_lr2', 'gla_b_lr', 'gla_norm_g', 'mla_q_norm_g', 'mla_w_uq', 'mla_kv_norm_g',
        'mla_w_ukv', 'w_branch', 'w_out', 'ln1_g', 'ln1_b', 'router_w', 'router_bias', 'exp_w_gate', 'exp_w_up',
        'exp_w_down', 'sh_w_gate', 'sh_w_up', 'sh_w_down', 'ple_w', 'ple_gate_w', 'ln2_g', 'ln2_b']
_OUTS = [((1, 512, 1024), 'float32')]


def kernel(**inputs):
    import numpy as _np
    import concourse.bacc as _bacc
    from concourse import mybir as _mybir
    from concourse.bass_utils import run_bass_kernel_spmd as _run

    nc = _bacc.Bacc("TRN2", target_bir_lowering=False, num_devices=1)
    arrays, weights, tables = {}, {}, {}
    for name in _INS:
        a = _np.ascontiguousarray(inputs[name])
        arrays[f"in_{name}_dram"] = a
        weights[name] = nc.dram_tensor(f"in_{name}_dram", a.shape, _mybir.dt.from_np(a.dtype), kind="ExternalInput").ap()
    for name, a in shape_constants().items():
        a = _np.ascontiguousarray(a)
        arrays[f"const_{name}_dram"] = a
        tables[name] = nc.dram_tensor(f"const_{name}_dram", a.shape, _mybir.dt.from_np(a.dtype), kind="ExternalInput").ap()
    outs = []
    for i, (shape, dtype) in enumerate(_OUTS):
        dt = _mybir.dt.from_np(_np.dtype(dtype))
        outs.append(nc.dram_tensor(f"out_{i}_dram", shape, dt, kind="ExternalOutput").ap())
    tables["x"], tables["out"] = weights["x"], outs[0]
    prog(nc, weights, tables)
    r = _run(nc, [arrays], core_ids=[0])
    got = tuple(r.results[0][f"out_{i}_dram"] for i in range(len(_OUTS)))
    return got[0]
```

```python
from contextlib import ExitStack

import concourse.bass as bass
from concourse import mybir

F32 = mybir.dt.float32
I32 = mybir.dt.int32
ALU = mybir.AluOpType
ACT = mybir.ActivationFunctionType
AX = mybir.AxisListType

P = 128
CHUNK = 64
SWA_HEADS, SWA_DIM = 8, 64
GLA_DK = 64
GLA_TAU = 16.0
MLA_NOPE, MLA_ROPE = 128, 64
MLA_SCALE = (MLA_NOPE + MLA_ROPE) ** -0.5
ROPE_THETA = 10000.0
TOP_K = 8
ROUTED_SCALE = 2.5
LN_EPS, RMS_EPS = 1e-5, 1e-6
MASKED = -1e30
TWO_PI = 6.283185307179586
PI_CLIP = 3.1415925

COL_U, COL_Q, COL_K, COL_CQ, COL_CV, COL_CG, COL_LR, COL_KVD, COL_GATE = (
    0, 512, 1024, 1280, 1792, 2304, 2816, 3088, 3280)
WSLOTS, WCOLS = 5, 272
BLK = 256
EXPERT_RING = 4
SLOTS = 96
ROUNDS = -(-512 // SLOTS)


def shape_constants():
    import numpy as np
    f = np.float32
    seq, n_exp = 512, 64
    tok = np.arange(seq)
    p = np.arange(P)
    half = MLA_ROPE // 2
    inv = f(ROPE_THETA) ** (-np.arange(half, dtype=f) / f(half))
    ang = tok.astype(f)[None, :] * inv.astype(f)[p % half][:, None]
    sign = np.where(p % MLA_ROPE < half, -1.0, 1.0)[:, None]
    partner = np.where(p % MLA_ROPE < half, p + half, p - half)
    swap = np.zeros((P, P), f)
    swap[partner, p] = 1
    slopes = 2.0 ** (-8.0 * np.arange(1, SWA_HEADS + 1) / SWA_HEADS)
    kk = np.arange(2 * P)
    dist = np.abs(p[:, None] - (kk[None, :] - P))
    qc, kc = p // CHUNK, kk // CHUNK - 2
    seen = (kc[None, :] == qc[:, None]) | (kc[None, :] == qc[:, None] - 1)
    alibi = np.where(seen[:, None, :], -slopes[None, :, None] * dist[:, None, :], MASKED)
    causal = (p[:, None] <= p[None, :]) & (p[:, None] // CHUNK == p[None, :] // CHUNK)
    return {
        "ident": np.eye(P, dtype=f),
        "centre": (np.eye(P) - 1.0 / P).astype(f),
        "half_swap": swap,
        "rope_cos": np.cos(ang).astype(f),
        "rope_sin": (sign * np.sin(ang)).astype(f),
        "alibi": alibi.astype(f),
        "gla_causal": np.ascontiguousarray(np.broadcast_to(causal[:, None, :], (P, 4, P))).astype(np.int32),
        "chunk_keep": np.broadcast_to((tok % CHUNK != 0), (P, seq)).astype(f),
        "before": (p[:, None] < p[None, :]).astype(f),
        "expert_code": np.broadcast_to(np.arange(1, n_exp + 1), (P, n_exp)).astype(f),
        "token_id": (np.arange(4)[None, :] * P + p[:, None]).astype(np.int32),
        "no_token": np.zeros((P, ROUNDS * SLOTS * n_exp // P), np.int32),
    }


class Count:

    def __init__(self):
        self.counts, self.latest = {}, None

    def __call__(self, ins, sem):
        self.counts[sem.num] = self.counts.get(sem.num, 0) + 1
        self.latest = (sem, self.counts[sem.num])


class Ring:

    def __init__(self, banks, keys):
        self.banks = banks
        self.number = {k: n for n, k in enumerate(keys)}
        assert len(self.number) == len(keys)

    def bank(self, key):
        return self.banks[self.number[key] % len(self.banks)]

    def nth(self, key):
        return self.number[key] + 1

    def reused(self, key):
        return self.number[key] >= len(self.banks)

    def last_user(self, key):
        return self.number[key] - len(self.banks) + 1


class Region:

    def __init__(self, tensor, words, at=0):
        self.t, self.words, self.at = tensor, words, at

    def take(self, *dims):
        n = 1
        for d in dims:
            n *= d
        assert self.at + n <= self.words, (self.at, n, self.words)
        ap = self.t[:, self.at:self.at + n]
        self.at += n
        if len(dims) == 2:
            return ap.rearrange("p (a b) -> p a b", a=dims[0])
        if len(dims) == 3:
            return ap.rearrange("p (a b c) -> p a b c", a=dims[0], b=dims[1])
        if len(dims) == 4:
            return ap.rearrange("p (a b c d) -> p a b c d", a=dims[0], b=dims[1], c=dims[2])
        return ap


def col(ap, *shape):
    return ap.unsqueeze(len(ap.shape)).to_broadcast(shape)


BRANCH_ORDER = (3, 2, 1, 0)


def mixer_plan():
    steps = [("xt", k) for k in range(8)]
    steps += [("lr",), ("qd", 0), ("qd", 1), ("kvd",), ("rq",), ("kr",), ("rk",), ("krs",), ("q", 0)]
    steps += [("mqn", h) for h in range(4)] + [("mkn", h) for h in range(4)]
    steps += [("mqr", 0), ("mqr", 1), ("mv", 0), ("mqs", 0), ("mqs", 1)] + [("mv", i) for i in range(1, 4)]
    fill = [("q", j) for j in range(1, 4)] + [("k",), ("v",)] + [("u", t) for t in range(4)] + [("cg", t) for t in range(4)]
    fill += [("cq", 0), ("cq", 1)]
    units = [(i, h) for i in range(4) for h in range(4)]
    for n, u in enumerate(units):
        steps += [("ms", *u), ("mn", *u)]
        if n < 14:
            steps.append(fill.pop(0))
        if n:
            steps.append(("mp", *units[n - 1]))
        if n > 1:
            steps.append(("mo", *units[n - 2]))
    steps += [fill.pop(0), ("mp", *units[-1]), ("mo", *units[-2]), ("ck", 0), ("mo", *units[-1]), ("lg",), ("ck", 1)]
    steps += [("cv", i) for i in range(4)]
    halves = [s for n in BRANCH_ORDER for dt in range(8) for s in (("gate", n, dt), ("mix", n, dt))]
    last = BRANCH_ORDER[-1]
    halves[-16:] = [("gate", last, 0)] + [s for dt in range(7) for s in (("gate", last, dt + 1), ("mix", last, dt))] + [("mix", last, 7)]

    def mix(count):
        nonlocal halves
        taken, halves = halves[:count], halves[count:]
        return taken

    steps += [("ggate",)] + mix(3) + [("gdecay",)] + mix(2) + [("krt", 0), ("krt", 1)] + mix(1)
    steps += [("kv", 0), ("kv", 1), ("gstate", 0), ("gstate", 1), ("att", 0), ("att", 1)] + mix(1)
    for h in (0, 2):
        steps += [("go", h)] + mix(1) + [("go", h + 1), ("gc", h)] + mix(1) + [("gc", h + 1), ("gv", h)]
        if h == 0:
            steps += [("att", 2), ("att", 3)]
        steps += mix(1) + [("gv", h + 1), ("gout", h)] + mix(1) + [("gout", h + 1)]
    steps += mix(1)
    units = [(i, g, jp) for i in range(4) for g in range(2) for jp in range(2)]
    for n, u in enumerate(units):
        steps += [("ss", *u), ("sn", *u)]
        steps += mix(2 if n in (3, 7) else 0 if n in (5, 9, 11, 13, 15) else 1)
        if n:
            steps.append(("sp", *units[n - 1]))
        if n > 1:
            steps.append(("so", *units[n - 2]))
        if n == 2:
            steps.append(("s5_prep",))
        if n == 6:
            steps.append(("s5_mats_prep",))
    steps += mix(1) + [("sp", *units[-1]), ("so", *units[-2])] + [("s5_mats", 0), ("s5_mats", 1), ("so", *units[-1]), ("swa_end",)]
    steps += [("s5_mats", 2), ("s5_mats", 3)]
    for i in range(16):
        steps.append(("bu", i))
        steps += mix(2 if i == 8 else 1)
        if i:
            steps.append(("y", i - 1))
    steps += mix(1) + [("y", 15)] + mix(1) + [("gelu",), ("glu", 0), ("glu", 1), ("glu", 2), ("glu", 3)] + mix(1) + [("glu_end",)]
    steps += mix(len(halves)) + [("ln_load",)]
    steps += [s for i in range(4) for s in (("wo", i, 0), ("wo", i, 1), ("ln1", i))]
    return steps


def mixer_banks(steps):
    by_act, by_dve = [], []
    for s in steps:
        kind = s[0]
        if kind == "xt":
            (by_act if s[1] % 2 else by_dve).append(s)
        elif kind in ("lr", "qd", "kvd", "kr", "rq", "rk", "mqn", "mkn", "mv", "q", "k", "v", "u", "cg", "cq", "ck",
                      "cv", "ms", "mo", "krt", "go", "gc", "gv", "so", "glu", "wo", "mp", "sp", "mqr", "gate"):
            by_act.append(s)
        elif kind in ("krs", "mqs", "att", "ss", "mix"):
            by_dve.append(s)
        elif kind == "lg":
            by_dve += [("lg", 0), ("lg", 1)]
        elif kind == "kv":
            by_dve += [("kv", s[1], 1), ("kv", s[1], 0)]
        elif kind == "s5_mats":
            by_act += [("mat", s[1], m) for m in range(4)]
        elif kind == "bu":
            by_dve += [("bu", s[1], 0), ("bu", s[1], 1)]
    return by_act, by_dve


def step_blocks(step):
    kind, a = step[0], step[1:]
    if kind in ("lr", "qd"):
        return [("in", COL_LR, 272)]
    if kind in ("kvd", "kr"):
        return [("in", COL_KVD, 256)]
    if kind in ("q", "u", "cg", "cq", "ck"):
        start = {"q": COL_Q, "u": COL_U, "cg": COL_CG, "cq": COL_CQ, "ck": COL_CQ + BLK}[kind]
        return [("in", start + (a[0] // 2 * BLK if kind in ("q", "u", "cg") else 0), BLK)]
    if kind in ("k", "v"):
        return [("in", COL_K, BLK)]
    if kind == "cv":
        return [("in", COL_CV, BLK), ("in", COL_CV + BLK, BLK)]
    if kind == "gate":
        return [("in", COL_GATE + a[0] * 1024 + a[1] // 2 * BLK, BLK)]
    if kind == "mix":
        return [("branch", a[0], a[1] // 4 * 512)]
    if kind == "glu":
        return [("glu", a[0] // 2 * BLK, BLK)]
    if kind == "wo":
        return [("out", (2 * a[1] + c) * BLK, BLK) for c in range(2)]
    return []


def weight_blocks(plan):
    last = {}
    for step in plan:
        for b in step_blocks(step):
            last[b] = step
    return [(*b, step) for b, step in last.items()]




def build_mixers(nc, ctx, T, layer, W, keep, sem):
    alpha = T["alpha"]
    plan = mixer_plan()
    keys_act, keys_dve = mixer_banks(plan)
    blocks = weight_blocks(plan)
    last_block_use = [b[3] for b in blocks]

    def sb(name, shape, dt=F32):
        return ctx.enter_context(nc.sbuf_tensor(name, shape, dt))

    x, ident, ones, eps = keep["x"], keep["ident"], keep["ones"], keep["eps"]
    centre, half_swap = keep["centre"], keep["half_swap"]
    cos_t, sin_t = keep["rope_cos"], keep["rope_sin"]
    xT = sb("xT", [P, 8, 512])
    mixT = sb("mixT", [P, 8 * 512])
    wring = sb("wring", [P, WSLOTS, 8 * WCOLS])
    uT = sb("uT", [P, 4, 512])
    qT = sb("qT", [P, 4, 512])
    cgT = sb("cgT", [P, 4, 512])
    odT = sb("odT", [P, 4, 512])
    kT = sb("kT", [P, 512])
    v_nat = sb("v_nat", [P, 4, 128])
    lrT = sb("lrT", [16, 512])
    small = sb("small", [P, 384])
    s5keep = sb("s5keep", [P, 3 * 1024])
    work = sb("work", [P, 12032])
    thm = sb("thm", [P, 2, 512])

    sm = Region(small, 384)
    b_lr, gla_g, q_g, kv_g, s5_d = sm.take(2), sm.take(4), sm.take(2), sm.take(1), sm.take(4)
    sinks = sm.take(8)
    mx, nmx, rsum, rinv = sm.take(2, 8), sm.take(2, 8), sm.take(2, 8), sm.take(2, 8)
    esink = sm.take(2, 8)
    decay = sm.take(2, 8)
    stats, mv, rstd = sm.take(12), sm.take(2), sm.take(1)
    phase = sm.take(16)
    s5_are, s5_aim, s5_ldt, s5_th, s5_r = sm.take(16), sm.take(16), sm.take(16), sm.take(16), sm.take(16)
    s5_fr, s5_fi, s5_c, s5_s = sm.take(16), sm.take(16), sm.take(16), sm.take(16)
    s5_a, s5_b, s5_n, s5_m, s5_den = sm.take(16), sm.take(16), sm.take(16), sm.take(16), sm.take(16)
    s5_turns = sb("s5_turns", [P, 16], I32)
    rope_tmp = s5keep[:, 0:512]
    w_lr2 = sb("w_lr2", [16, 256])

    ml = Region(mixT, 4096)
    w_uq, w_ukv, ml_t1, ml_t2 = ml.take(2, 768), ml.take(1024), ml.take(2, 512), ml.take(512)
    mx_all = mixT[:, :].rearrange("p (a b) -> p a b", a=8)
    rm = Region(work, 12032)
    qd, kvd, kr = rm.take(2, 512), rm.take(512), rm.take(512)
    qn, qr, kn, vm = rm.take(4, 512), rm.take(2, 512), rm.take(4, 512), rm.take(4, 512)
    mP, mPT = rm.take(2, 512), rm.take(2, 4, 128)
    rg = Region(work, 12032)
    cq, ck, cv = rg.take(2, 512), rg.take(2, 512), rg.take(4, 512)
    bcum, gtmp = rg.take(2, 512), rg.take(2, 512)
    krem, kremN = rg.take(2, 512), rg.take(4, 2, 128)
    gstate = rg.take(2, 7, 128)
    attT = rg.take(2, 512)
    oT, osq = krem, gtmp
    rs = Region(work, 12032)
    alibi = rs.take(8, 256)
    sS, sP, sPT = rs.take(2, 512), rs.take(2, 512), rs.take(2, 4, 128)
    s5_at = rs.at
    rp = Region(work, 12032, s5_at)
    bre, bim, cre, cim = rp.take(16, 16), rp.take(16, 16), rp.take(4, 128), rp.take(4, 128)
    bxr, bxi = rp.take(16, 32), rp.take(16, 32)
    pt1, pt2 = rp.take(512), rp.take(512)
    rk = Region(work, 12032, s5_at + 2048 + 1024 + 512)
    phasor = rk.take(2, 2, 512)
    er, ei = phasor[:, :, 0, :], phasor[:, :, 1, :]
    rt = Region(work, s5_at)
    tu, tw = rt.take(2, 512), rt.take(2, 512)
    zr, zi = rt.take(512), rt.take(512)
    sr, si = rt.take(2, 512), rt.take(2, 512)
    e1, e2 = rk.take(512), rk.take(512)
    glu_gate = Region(work, 12032).take(4, 512)
    b_prod = phasor[:, 0, :, :].rearrange("p a b -> p (a b)").rearrange("p (a b c) -> p a b c", a=4, b=16)
    kp = Region(s5keep, 3072)
    btr, bti, cxr, cxi = kp.take(4, 128), kp.take(4, 128), kp.take(16, 32), kp.take(16, 32)
    jr, ji = kp.take(16, 32), kp.take(16, 32)
    kr_, ki_ = sb("s5_kr", [P, 16, 16]), sb("s5_ki", [P, 16, 16])
    rl = Region(work, 12032)
    ln_g, ln_b, ln_y = rl.take(1024), rl.take(1024), rl.take(2, 1024)

    pa = [ctx.enter_context(nc.psum_tensor(f"act_bank{n}", [P, 512], F32)) for n in range(3)]
    pv = [ctx.enter_context(nc.psum_tensor(f"dve_bank{n}", [P, 512], F32)) for n in range(4)]
    y_bank = ctx.enter_context(nc.psum_tensor("y_bank", [P, 512], F32))
    A, V = Ring(pa, keys_act), Ring(pv, keys_dve)
    act_bank_full, act_bank_copied = sem("act_bank_full"), sem("act_bank_copied")
    dve_bank_full, dve_bank_copied = sem("dve_bank_full"), sem("dve_bank_copied")

    slot_loaded = [sem(f"weights_in_slot{n}") for n in range(WSLOTS)]
    params_in, alibi_in, s5_in, ln_in = (
        sem(n) for n in ("params_in", "alibi_in", "s5_params_in", "ln_rows_in"))
    dve_done, act_done, pool_done = sem("dve_done"), sem("act_done"), sem("pool_done")
    max_ready, probs_ready = sem("mla_max_ready"), sem("mla_probs_ready")
    win_ready, win_exp, win_probs = sem("win_scores_ready"), sem("win_exp_done"), sem("win_probs_ready")
    normed = sem("latents_normed")
    rope_ready = sem("rope_ready")
    swa_done = sem("swa_done")
    gabs, gsoft, gcum, gexp, gdec_ready, gout_ready = (
        sem(n) for n in ("gla_abs_ready", "gla_softplus_ready", "gla_cum_ready", "gla_exps_ready",
                         "gla_decayed", "gla_out_ready"))
    s5_ang, s5_sin, s5_bx, s5_state, y_step, y_taken, gelu_done, glu_ready, mix_used = (
        sem(n) for n in ("s5_angle_ready", "s5_sincos_ready", "s5_bx_ready", "s5_state_ready",
                         "s5_y_step", "s5_y_taken", "s5_gelu_done", "s5_glu_ready", "gate_used"))
    s5_table, s5_table_used, s5_lam = sem("s5_table_ready"), sem("s5_table_used"), sem("s5_lam_ready")
    ln_var, ln_sd, ln_done = sem("ln_var_ready"), sem("ln_sd_ready"), sem("ln1_tile_ready")

    arrival, at = {}, [0] * WSLOTS
    for n, b in enumerate(blocks):
        loads = 4 if b[0] == "in" and COL_Q <= b[1] < COL_K else 2 if b[:2] in (("branch", 1), ("in", COL_KVD)) else 1
        at[n % WSLOTS] += 16 * loads
        arrival[b[:3]] = (n % WSLOTS, at[n % WSLOTS])

    def weights(eng, kind, c0, width):
        slot, value = arrival[kind, c0, width]
        eng.wait_ge(slot_loaded[slot], value)
        k = 8 if kind in ("in", "out") else 4
        w = 512 if kind == "branch" else width
        return wring[:, slot, 0:k * w].rearrange("p (k n) -> p k n", k=k)

    def toks(i, n=P):
        return slice(i * n, i * n + n)

    block = ctx.enter_context(nc.Block())

    @block.sync
    def _(eng):
        w_in = W["w_in"][layer].rearrange("(p k) n -> p k n", p=P)
        w_out = W["w_out"][layer].rearrange("(k p) n -> p k n", p=P)
        w_glu = W["s5_w_glu"][layer].rearrange("(k p) n -> p k n", p=P)
        for n, (kind, c0, width, _) in enumerate(blocks):
            slot = n % WSLOTS
            if n >= WSLOTS:
                user = last_block_use[n - WSLOTS]
                if user[0] == "mix":
                    eng.wait_ge(dve_bank_full, V.nth(user))
                else:
                    eng.wait_ge(act_bank_full, A.nth(user))
            k = 8 if kind in ("in", "out") else 4
            w = 512 if kind == "branch" else width
            dst = wring[:, slot, 0:k * w].rearrange("p (k n) -> p k n", k=k)
            done = slot_loaded[slot]
            if kind == "in" and COL_Q <= c0 < COL_K:
                for j in range(2):
                    for g in range(2):
                        c = COL_Q + g * 256 + (c0 - COL_Q) // 2 + j * 64
                        o = (2 * j + g) * 64
                        eng.dma_start(dst[:, :, o:o + 64], w_in[:, :, c:c + 64]).then_inc(done, 16)
            elif kind == "in" and c0 == COL_KVD:
                eng.dma_start(dst[:, :, 0:192], w_in[:, :, c0:c0 + 192]).then_inc(done, 16)
                eng.dma_start(dst[:, :, 192:256], w_in[:, :, c0 + P:c0 + 192]).then_inc(done, 16)
            elif kind == "in":
                eng.dma_start(dst, w_in[:, :, c0:c0 + width]).then_inc(done, 16)
            elif kind == "out":
                eng.dma_start(dst, w_out[:, :, c0:c0 + width]).then_inc(done, 16)
            elif kind == "glu":
                eng.dma_start(dst, w_glu[:, :, c0:c0 + width]).then_inc(done, 16)
            else:
                wb = W["w_branch"][layer, c0]
                cols = slice(width, width + 512)
                if c0 == 1:
                    rows = wb.rearrange("(g j d) n -> g d j n", g=2, j=4)
                    for g in range(2):
                        eng.dma_start(dst[64 * g:64 * g + 64], rows[g][:, :, cols]).then_inc(done, 16)
                else:
                    eng.dma_start(dst, wb.rearrange("(k p) n -> p k n", p=P)[:, :, cols]).then_inc(done, 16)

    @block.gpsimd
    def _(eng):
        pool = Count()

        def load(dst, src, done):
            eng.dma_start(dst, src, allow_slow_non_contiguous=True).then_inc(done, 16)

        load(w_lr2[:, :], W["gla_w_lr2"][layer], params_in)
        load(b_lr, W["gla_b_lr"][layer].rearrange("(t p) -> p t", p=P), params_in)
        load(gla_g, W["gla_norm_g"][layer].rearrange("(t p) -> p t", p=P), params_in)
        load(q_g, W["mla_q_norm_g"][layer].rearrange("(t p) -> p t", p=P), params_in)
        load(kv_g, W["mla_kv_norm_g"][layer].rearrange("(t p) -> p t", p=P), params_in)
        for k in range(2):
            src = W["mla_w_uq"][layer, k * P:(k + 1) * P, :].rearrange("p (h n) -> p h n", h=4)
            load(w_uq[:, k, 0:512].rearrange("p (h n) -> p h n", h=4), src[:, :, 0:P], params_in)
            load(w_uq[:, k, 512:768].rearrange("p (h n) -> p h n", h=4), src[:, :, P:P + 64], params_in)
        load(w_ukv, W["mla_w_ukv"][layer], params_in)
        load(s5_d, W["s5_d"][layer].rearrange("(t g) c -> (g c) t", t=4), params_in)
        load(sinks, W["swa_sinks"][layer].partition_broadcast(P), params_in)
        load(s5_are, W["s5_a_re"][layer].rearrange("(t g) p -> (g p) t", g=2), params_in)
        load(s5_aim, W["s5_a_im"][layer].rearrange("(t g) p -> (g p) t", g=2), params_in)
        for g in range(2):
            src = W["s5_log_dt"][layer].rearrange("(t g) -> g t", g=2)[g]
            load(s5_ldt[64 * g:64 * g + 64], src.partition_broadcast(64), params_in)

        def s5_prep():
            eng.wait_ge(gout_ready, 4)
            load(alibi, T["alibi"], alibi_in)
            for dst, name in ((bre, "s5_b_re"), (bim, "s5_b_im")):
                src = W[name][layer].rearrange("(t g) p c -> (g p) t c", g=2)
                load(dst, src, s5_in)
            for dst, name in ((cre, "s5_c_re"), (cim, "s5_c_im")):
                src = W[name][layer].rearrange("(t g) c p -> (g c) t p", t=4)
                for half in range(2):
                    load(dst[:, :, 64 * half:64 * half + 64], src, s5_in)
            eng.wait_ge(s5_sin, 2)
            eng.wait_ge(s5_lam, 1)
            g = eng
            pr, pi = s5_c, s5_s
            ta = pt1.rearrange("p (a b) -> p a b", a=16)
            tb = pt2.rearrange("p (a b) -> p a b", a=16)
            for tr, ti, size in ((jr, ji, 32), (kr_, ki_, 16)):
                pool(g.memset(tr[:, :, 0:1], 1.0).then_inc(pool_done, 1), pool_done)
                pool(g.memset(ti[:, :, 0:1], 0.0).then_inc(pool_done, 1), pool_done)
                m = 1
                while m < size:
                    eng.wait_ge(*pool.latest)
                    shape = (P, 16, m)
                    bpr, bpi = col(pr, *shape), col(pi, *shape)
                    pool(g.tensor_tensor(ta[:, :, 0:m], tr[:, :, 0:m], bpr, ALU.mult).then_inc(pool_done, 1), pool_done)
                    pool(g.tensor_tensor(tb[:, :, 0:m], ti[:, :, 0:m], bpi, ALU.mult).then_inc(pool_done, 1), pool_done)
                    eng.wait_ge(*pool.latest)
                    pool(g.tensor_tensor(tr[:, :, m:2 * m], ta[:, :, 0:m], tb[:, :, 0:m], ALU.subtract).then_inc(pool_done, 1), pool_done)
                    eng.wait_ge(*pool.latest)
                    pool(g.tensor_tensor(ta[:, :, 0:m], tr[:, :, 0:m], bpi, ALU.mult).then_inc(pool_done, 1), pool_done)
                    pool(g.tensor_tensor(tb[:, :, 0:m], ti[:, :, 0:m], bpr, ALU.mult).then_inc(pool_done, 1), pool_done)
                    eng.wait_ge(*pool.latest)
                    pool(g.tensor_tensor(ti[:, :, m:2 * m], ta[:, :, 0:m], tb[:, :, 0:m], ALU.add).then_inc(pool_done, 1), pool_done)
                    eng.wait_ge(*pool.latest)
                    pool(g.tensor_tensor(ta[:, :, 0], pr, pr, ALU.mult).then_inc(pool_done, 1), pool_done)
                    pool(g.tensor_tensor(tb[:, :, 0], pi, pi, ALU.mult).then_inc(pool_done, 1), pool_done)
                    pool(g.tensor_tensor(ta[:, :, 1], pr, pi, ALU.mult).then_inc(pool_done, 1), pool_done)
                    eng.wait_ge(*pool.latest)
                    pool(g.tensor_tensor(pr, ta[:, :, 0], tb[:, :, 0], ALU.subtract).then_inc(pool_done, 1), pool_done)
                    pool(g.tensor_tensor(pi, ta[:, :, 1], ta[:, :, 1], ALU.add).then_inc(pool_done, 1), pool_done)
                    m *= 2
            eng.wait_ge(*pool.latest)

        def s5_time(i):
            if i == 0:
                eng.wait_ge(swa_done, 1)
                eng.wait_ge(s5_bx, 1)
            if i >= 2:
                eng.wait_ge(s5_table_used, i - 1)
            shape = (P, 16, 32)
            k_r, k_i = kr_[:, i, :].unsqueeze(2).to_broadcast(shape), ki_[:, i, :].unsqueeze(2).to_broadcast(shape)
            j_r, j_i = jr[:, i, :].unsqueeze(1).to_broadcast(shape), ji[:, i, :].unsqueeze(1).to_broadcast(shape)
            e_r, e_i = (e[:, i % 2, :].rearrange("p (c j) -> p c j", c=16) for e in (er, ei))
            a, b = (e.rearrange("p (c j) -> p c j", c=16) for e in (e1, e2))
            for x1, y1, x2, y2, op, out in ((k_r, j_r, k_i, j_i, ALU.subtract, e_r), (k_r, j_i, k_i, j_r, ALU.add, e_i)):
                if pool.latest:
                    eng.wait_ge(*pool.latest)
                pool(eng.tensor_tensor(a, x1, y1, ALU.mult).then_inc(pool_done, 1), pool_done)
                pool(eng.tensor_tensor(b, x2, y2, ALU.mult).then_inc(pool_done, 1), pool_done)
                eng.wait_ge(*pool.latest)
                pool(eng.tensor_tensor(out, a, b, op).then_inc(s5_table if op == ALU.add else pool_done, 1), s5_table if op == ALU.add else pool_done)

        for step in plan:
            if step[0] == "s5_prep":
                s5_prep()
            elif step[0] == "bu":
                s5_time(step[1])
            elif step[0] == "ln_load":
                eng.wait_ge(glu_ready, 1)
                load(ln_g, W["ln1_g"][layer].partition_broadcast(P), ln_in)
                load(ln_b, W["ln1_b"][layer].partition_broadcast(P), ln_in)

    @block.scalar
    def _(eng):
        act = Count()
        mix_no = [0]

        def copy_out(step, dst, scale=None):
            eng.wait_ge(act_bank_full, A.nth(step))
            b = A.bank(step)
            src = b[0:dst.shape[0], :]
            if len(dst.shape) == 3:
                src = src.rearrange("p (a b) -> p a b", a=dst.shape[1])
            if scale is None:
                act(eng.copy(dst, src).then_inc(act_bank_copied, 1), act_bank_copied)
            else:
                act(eng.mul(dst, src, scale).then_inc(act_bank_copied, 1), act_bank_copied)

        def squares(step, dst, sq):
            eng.wait_ge(act_bank_full, A.nth(step))
            b = A.bank(step)
            act(eng.activation(sq, b[:, :], ACT.Square).then_inc(act_done, 1), act_done)
            act(eng.copy(dst, b[:, :]).then_inc(act_bank_copied, 1), act_bank_copied)

        def root(step, dst, n, e):
            eng.wait_ge(act_bank_full, A.nth(step))
            b = A.bank(step)
            act(eng.activation(dst, b[:, :], ACT.Sqrt, bias=eps[:, e:e + 1], scale=1.0 / n).then_inc(act_bank_copied, 1), act_bank_copied)

        for step in plan:
            kind, a = step[0], step[1:]
            if kind == "xt" and step in A.number:
                copy_out(step, xT[:, a[0], :])
            elif kind == "lr":
                copy_out(step, lrT[:, :])
            elif kind == "qd":
                squares(step, qd[:, a[0], :], ml_t1[:, a[0], :])
            elif kind == "kvd":
                squares(step, kvd, ml_t2)
            elif kind == "kr":
                copy_out(step, kr)
            elif kind == "rq":
                root(step, thm[:, 0, :], 256, 1)
            elif kind == "rk":
                root(step, thm[:, 1, :], 128, 1)
            elif kind == "mqn":
                copy_out(step, qn[:, a[0], :])
            elif kind == "mkn":
                copy_out(step, kn[:, a[0], :])
            elif kind == "mqr":
                copy_out(step, qr[:, a[0], :])
            elif kind == "mv":
                copy_out(step, vm[:, a[0], :])
            elif kind == "q":
                copy_out(step, qT[:, a[0], :], SWA_DIM ** -0.5)
            elif kind == "k":
                copy_out(step, kT[:, :])
            elif kind == "v":
                copy_out(step, v_nat[:, :, :])
            elif kind == "u":
                copy_out(step, uT[:, a[0], :])
            elif kind == "cg":
                eng.wait_ge(act_bank_full, A.nth(step))
                b = A.bank(step)
                act(eng.activation(cgT[:, a[0], :], b[:, :], ACT.Silu).then_inc(act_bank_copied, 1), act_bank_copied)
            elif kind == "cq":
                copy_out(step, cq[:, a[0], :], GLA_DK ** -0.5)
            elif kind == "ck":
                copy_out(step, ck[:, a[0], :])
            elif kind == "cv":
                copy_out(step, cv[:, a[0], :])
            elif kind == "ms":
                i, h = a
                u, n = 4 * i + h, P * (i + 1)
                eng.wait_ge(max_ready, u + 1)
                b = A.bank(step)
                act(eng.activation(mP[:, u % 2, 0:n], b[:, 0:n], ACT.Exp, bias=nmx[:, u % 2, 0:1], scale=MLA_SCALE,
                                   accum_out=rsum[:, u % 2, 0:1]).then_inc(act_bank_copied, 1), act_bank_copied)
            elif kind == "mp":
                i, h = a
                u, n = 4 * i + h, P * (i + 1)
                eng.wait_ge(act_bank_full, A.nth(step))
                b = A.bank(step)
                act(eng.copy(mPT[:, u % 2, 0:i + 1, :], b[:, 0:n].rearrange("p (a b) -> p a b", b=P)).then_inc(act_bank_copied, 1), act_bank_copied)
            elif kind == "mo":
                i, h = a
                eng.wait_ge(act_bank_full, A.nth(step))
                b = A.bank(step)
                act(eng.copy(odT[:, h, toks(i)], b[:, 0:P]).then_inc(act_bank_copied, 1), act_bank_copied)
            elif kind == "ggate":
                eng.wait_ge(gabs, 1)
                act(eng.activation(bcum, bcum, ACT.Exp, scale=-1.0).then_inc(act_done, 1), act_done)
                eng.wait_ge(*act.latest)
                act(eng.activation(krem, bcum, ACT.Ln, bias=1.0).then_inc(gsoft, 1), gsoft)
            elif kind == "gdecay":
                eng.wait_ge(gcum, 1)
                act(eng.activation(krem, bcum, ACT.Exp, scale=1.0 / GLA_TAU).then_inc(act_done, 1), act_done)
                act(eng.activation(kremN, bcum, ACT.Exp, scale=-1.0 / GLA_TAU).then_inc(act_done, 1), act_done)
                last = bcum.rearrange("p t (c s) -> p t c s", s=CHUNK)[:, :, :, CHUNK - 1]
                act(eng.activation(decay, last, ACT.Exp, scale=1.0 / GLA_TAU).then_inc(act_done, 1), act_done)
                act(eng.activation(gtmp, gtmp, ACT.Exp, scale=1.0 / GLA_TAU).then_inc(gexp, 1), gexp)
            elif kind == "krt":
                eng.wait_ge(act_bank_full, A.nth(step))
                b = A.bank(step)
                act(eng.copy(kremN[:, 2 * a[0]:2 * a[0] + 2, :, :].rearrange("p a b c -> p (a b c)"), b[:, :]).then_inc(act_bank_copied, 1), act_bank_copied)
            elif kind == "go":
                h = a[0]
                if h >= 2:
                    eng.wait_ge(gout_ready, h - 1)
                copy_out(step, oT[:, h % 2, :])
            elif kind == "gc":
                squares(step, oT[:, a[0] % 2, :], osq[:, a[0] % 2, :])
            elif kind == "gv":
                root(step, osq[:, a[0] % 2, :], P, 0)
            elif kind == "gate":
                m = mix_no[0]
                mix_no[0] += 1
                if m >= 2:
                    eng.wait_ge(mix_used, m - 1)
                eng.wait_ge(act_bank_full, A.nth(step))
                b = A.bank(step)
                act(eng.activation(thm[:, m % 2, :], b[:, :], ACT.Tanh, scale=0.5).then_inc(act_bank_copied, 1), act_bank_copied)
            elif kind == "s5_prep":
                eng.wait_ge(params_in, 16 * 16)
                act(eng.activation(s5_ldt, s5_ldt, ACT.Exp).then_inc(s5_sin, 1), s5_sin)
                eng.wait_ge(s5_ang, 1)
                act(eng.activation(s5_r, s5_a, ACT.Exp).then_inc(act_done, 1), act_done)
                eng.wait_ge(s5_ang, 2)
                act(eng.activation(s5_s, phase, ACT.Sin).then_inc(act_done, 1), act_done)
                act(eng.activation(s5_c, s5_b, ACT.Sin, bias=eps[:, 2:3], scale=-1.0).then_inc(s5_sin, 1), s5_sin)
            elif kind == "ss":
                i, g, jp = a
                u = 4 * i + 2 * g + jp
                w = P if i == 0 else 2 * P
                eng.wait_ge(win_ready, u + 1)
                for j in range(2):
                    act(eng.activation(sP[:, u % 2, j * w:(j + 1) * w], sS[:, u % 2, j * w:(j + 1) * w], ACT.Exp,
                                       bias=nmx[:, u % 2, j:j + 1], accum_out=rsum[:, u % 2, j:j + 1]).then_inc(act_done, 1), act_done)
                act(eng.activation(esink[:, u % 2, 0:2], esink[:, u % 2, 0:2], ACT.Exp).then_inc(win_exp, 1), win_exp)
            elif kind == "sp":
                i, g, jp = a
                u = 4 * i + 2 * g + jp
                w = 2 * P if i == 0 else 4 * P
                eng.wait_ge(act_bank_full, A.nth(step))
                b = A.bank(step)
                act(eng.copy(sPT[:, u % 2, 0:w // P, :], b[:, 0:w].rearrange("p (a b) -> p a b", b=P)).then_inc(act_bank_copied, 1), act_bank_copied)
            elif kind == "so":
                i, g, jp = a
                eng.wait_ge(act_bank_full, A.nth(step))
                b = A.bank(step)
                rows = slice(64 * g, 64 * g + 64)
                act(eng.copy(qT[rows, 2 * jp:2 * jp + 2, toks(i)], b[rows, 0:2 * P].rearrange("p (a b) -> p a b", b=P)).then_inc(act_bank_copied, 1),
                    act_bank_copied)
            elif kind == "s5_mats":
                Tt = a[0]
                for m, dst in ((0, btr), (1, bti)):
                    eng.wait_ge(act_bank_full, A.nth(("mat", Tt, m)))
                    b = A.bank(("mat", Tt, m))
                    act(eng.copy(dst[:, Tt, :], b[:, 0:P]).then_inc(act_bank_copied, 1), act_bank_copied)
                for m, dst, sign in ((2, cxr, 1.0), (3, cxi, -1.0)):
                    eng.wait_ge(act_bank_full, A.nth(("mat", Tt, m)))
                    b = A.bank(("mat", Tt, m))
                    for hf in range(2):
                        rows, cols = slice(64 * hf, 64 * hf + 64), slice(16 * hf, 16 * hf + 16)
                        act(eng.mul(dst[rows, 4 * Tt:4 * Tt + 4, cols],
                                    b[rows, 0:P].rearrange("p (i n) -> p i n", n=32)[:, :, cols], sign).then_inc(act_bank_copied if hf else act_done, 1),
                            act_bank_copied if hf else act_done)
            elif kind == "gelu":
                eng.wait_ge(y_taken, 4)
                act(eng.activation(uT[:, :, :], uT[:, :, :], ACT.Gelu_apprx_tanh).then_inc(gelu_done, 1), gelu_done)
            elif kind == "glu":
                eng.wait_ge(act_bank_full, A.nth(step))
                b = A.bank(step)
                act(eng.activation(glu_gate[:, a[0], :], b[:, :], ACT.Sigmoid).then_inc(act_bank_copied, 1), act_bank_copied)
            elif kind == "wo":
                i, half = a
                if i >= 2:
                    eng.wait_ge(ln_done, i - 1)
                elif half == 0 and i == 0:
                    eng.wait_ge(glu_ready, 1)
                eng.wait_ge(act_bank_full, A.nth(step))
                b = A.bank(step)
                act(eng.mul(ln_y[:, i % 2, 512 * half:512 * half + 512], b[:, :], 0.5).then_inc(act_bank_copied, 1), act_bank_copied)
            elif kind == "ln1":
                eng.wait_ge(ln_var, a[0] + 1)
                act(eng.activation(rstd, mv[:, 1:2], ACT.Sqrt, bias=eps[:, 0:1]).then_inc(ln_sd, 1), ln_sd)

    @block.vector
    def _(eng):
        dve = Count()
        mix_no = [0]
        tt, ts, stt = eng.tensor_tensor, eng.tensor_scalar, eng.scalar_tensor_tensor

        def norm_latent(parts, rms, gains):
            dve(eng.reciprocal(rms, rms).then_inc(dve_done, 1), dve_done)
            eng.wait_ge(*dve.latest)
            for n, (t, g) in enumerate(zip(parts, gains)):
                dve(stt(t, t, g, rms, ALU.mult, ALU.mult).then_inc(normed if n == len(parts) - 1 else dve_done, 1), normed if n == len(parts) - 1 else dve_done)

        def rope(step, t, tmp):
            eng.wait_ge(dve_bank_full, V.nth(step))
            b = V.bank(step)
            dve(tt(tmp, b[:, :], sin_t[:, :], ALU.mult).then_inc(dve_bank_copied, 1), dve_bank_copied)
            dve(tt(t, t, cos_t[:, :], ALU.mult).then_inc(dve_done, 1), dve_done)
            eng.wait_ge(*dve.latest)
            dve(tt(t, t, tmp, ALU.add).then_inc(rope_ready, 1), rope_ready)

        for step in plan:
            kind, a = step[0], step[1:]
            if dve.latest:
                eng.wait_ge(*dve.latest)
            if kind == "xt" and step in V.number:
                eng.wait_ge(dve_bank_full, V.nth(step))
                b = V.bank(step)
                dve(eng.tensor_copy(xT[:, a[0], :], b[:, :]).then_inc(dve_bank_copied, 1), dve_bank_copied)
            elif kind == "krs":
                rope(step, kr, rope_tmp)
            elif kind == "rq":
                eng.wait_ge(params_in, 16 * 16)
                eng.wait_ge(act_bank_copied, A.nth(step))
                norm_latent([qd[:, 0, :], qd[:, 1, :]], thm[:, 0, :], [q_g[:, 0:1], q_g[:, 1:2]])
            elif kind == "rk":
                eng.wait_ge(act_bank_copied, A.nth(step))
                norm_latent([kvd], thm[:, 1, :], [kv_g[:, 0:1]])
            elif kind == "mqs":
                rope(step, qr[:, a[0], :], rope_tmp)
            elif kind == "ms":
                i, h = a
                u, n = 4 * i + h, P * (i + 1)
                eng.wait_ge(act_bank_full, A.nth(step))
                b = A.bank(step)
                dve(eng.memset(b[0:64, n - 64:n], MASKED).then_inc(dve_done, 1), dve_done)
                eng.wait_ge(*dve.latest)
                dve(eng.reduce_max(mx[:, u % 2, 0:1], b[:, 0:n], AX.X).then_inc(dve_done, 1), dve_done)
                eng.wait_ge(*dve.latest)
                dve(ts(nmx[:, u % 2, 0:1], mx[:, u % 2, 0:1], -MLA_SCALE, None, ALU.mult).then_inc(max_ready, 1), max_ready)
            elif kind == "mn":
                i, h = a
                u, n = 4 * i + h, P * (i + 1)
                eng.wait_ge(act_bank_copied, A.nth(("ms", i, h)))
                dve(eng.reciprocal(rinv[:, u % 2, 0:1], rsum[:, u % 2, 0:1]).then_inc(dve_done, 1), dve_done)
                eng.wait_ge(*dve.latest)
                dve(ts(mP[:, u % 2, 0:n], mP[:, u % 2, 0:n], rinv[:, u % 2, 0:1], None, ALU.mult).then_inc(probs_ready, 1), probs_ready)
            elif kind == "lg":
                for t in range(2):
                    eng.wait_ge(dve_bank_full, V.nth(("lg", t)))
                    b = V.bank(("lg", t))
                    dve(ts(gtmp[:, t, :], b[:, :], b_lr[:, t:t + 1], None, ALU.add).then_inc(dve_bank_copied, 1), dve_bank_copied)
                eng.wait_ge(*dve.latest)
                dve(stt(bcum, gtmp, -1.0, gtmp, ALU.mult, ALU.max).then_inc(gabs, 1), gabs)
                dve(eng.memset(attT, 0.0).then_inc(dve_done, 1), dve_done)
            elif kind == "ggate":
                eng.wait_ge(gsoft, 1)
                dve(stt(gtmp, gtmp, 0.0, krem, ALU.min, ALU.subtract).then_inc(dve_done, 1), dve_done)
                eng.wait_ge(*dve.latest)
                for t in range(2):
                    dve(eng.tensor_tensor_scan(bcum[:, t, :], keep["chunk_keep"][:, :], gtmp[:, t, :], 0.0, ALU.mult, ALU.add).then_inc(dve_done, 1), dve_done)
                eng.wait_ge(*dve.latest)
                bc = bcum.rearrange("p t (c s) -> p (t c) s", s=CHUNK)
                last = bc[:, :, CHUNK - 1:CHUNK].to_broadcast((P, 16, CHUNK))
                dve(tt(gtmp.rearrange("p t (c s) -> p (t c) s", s=CHUNK), last, bc, ALU.subtract).then_inc(gcum, 1), gcum)
            elif kind == "gdecay":
                eng.wait_ge(gexp, 1)
                eng.wait_ge(act_bank_copied, A.nth(("ck", 1)))
                dve(tt(gtmp, gtmp, ck, ALU.mult).then_inc(dve_done, 1), dve_done)
                dve(tt(cq, cq, krem, ALU.mult).then_inc(dve_done, 1), dve_done)
                eng.wait_ge(*dve.latest)
                dve(tt(ck, ck, kremN.rearrange("p a b c -> p (a b) c").rearrange("p (t a) c -> p t (a c)", t=2), ALU.mult).then_inc(gdec_ready, 1), gdec_ready)
            elif kind == "gstate":
                t = a[0]
                eng.wait_ge(dve_bank_full, V.nth(("kv", t, 0)))
                for c in range(7):
                    kv = V.bank(("kv", t, c % 2))[:, (c // 2) * P:(c // 2 + 1) * P]
                    if c == 0:
                        dve(eng.tensor_copy(gstate[:, t, 0, :], kv).then_inc(dve_done, 1), dve_done)
                    else:
                        eng.wait_ge(*dve.latest)
                        dve(stt(gstate[:, t, c, :], gstate[:, t, c - 1, :], decay[:, t, c:c + 1], kv, ALU.mult, ALU.add).then_inc(dve_bank_copied if c >= 5 else dve_done, 1), dve_bank_copied if c >= 5 else dve_done)
            elif kind == "att":
                h = a[0]
                if h >= 2:
                    eng.wait_ge(act_bank_full, A.nth(("go", h - 2)))
                eng.wait_ge(dve_bank_full, V.nth(step))
                b = V.bank(step)
                dve(eng.copy_predicated(attT[:, h % 2, :].rearrange("p (a b) -> p a b", a=4), keep["gla_causal"][:, :, :],
                                        b[:, :].rearrange("p (a b) -> p a b", a=4)).then_inc(dve_bank_copied, 1), dve_bank_copied)
            elif kind == "gout":
                h = a[0]
                eng.wait_ge(act_bank_copied, A.nth(("gv", h)))
                o, sd = oT[:, h % 2, :], osq[:, h % 2, :]
                dve(eng.reciprocal(sd, sd).then_inc(dve_done, 1), dve_done)
                eng.wait_ge(*dve.latest)
                dve(stt(o, o, gla_g[:, h:h + 1], sd, ALU.mult, ALU.mult).then_inc(dve_done, 1), dve_done)
                eng.wait_ge(*dve.latest)
                dve(tt(cgT[:, h, :], cgT[:, h, :], o, ALU.mult).then_inc(gout_ready, 1), gout_ready)
            elif kind == "mix":
                m = mix_no[0]
                mix_no[0] += 1
                n, dt = a
                eng.wait_ge(dve_bank_full, V.nth(step))
                b = V.bank(step)
                eng.wait_ge(act_bank_copied, A.nth(("gate", n, dt)))
                dve(stt(thm[:, m % 2, :], thm[:, m % 2, :], 1.0, b[:, :], ALU.add, ALU.mult).then_inc(dve_bank_copied, 1), dve_bank_copied)
                eng.wait_ge(*dve.latest)
                if m < 8:
                    dve(eng.tensor_copy(mx_all[:, dt, :], thm[:, m % 2, :]).then_inc(mix_used, 1), mix_used)
                else:
                    dve(tt(mx_all[:, dt, :], mx_all[:, dt, :], thm[:, m % 2, :], ALU.add).then_inc(mix_used, 1), mix_used)
            elif kind == "s5_prep":
                eng.wait_ge(s5_sin, 1)
                dve(tt(s5_a, s5_are, s5_ldt, ALU.mult).then_inc(s5_ang, 1), s5_ang)
                dve(tt(s5_th, s5_aim, s5_ldt, ALU.mult).then_inc(dve_done, 1), dve_done)
                eng.wait_ge(*dve.latest)
                dve(ts(s5_turns[:, :], s5_th, 1.0 / TWO_PI, None, ALU.mult).then_inc(dve_done, 1), dve_done)
                eng.wait_ge(*dve.latest)
                dve(eng.tensor_copy(s5_m, s5_turns[:, :]).then_inc(dve_done, 1), dve_done)
                eng.wait_ge(*dve.latest)
                dve(stt(s5_th, s5_m, -6.28125, s5_th, ALU.mult, ALU.add).then_inc(dve_done, 1), dve_done)
                eng.wait_ge(*dve.latest)
                dve(stt(s5_th, s5_m, -(TWO_PI - 6.28125), s5_th, ALU.mult, ALU.add).then_inc(dve_done, 1), dve_done)
                eng.wait_ge(*dve.latest)
                dve(ts(phase, s5_th, PI_CLIP, -PI_CLIP, ALU.min, ALU.max).then_inc(dve_done, 1), dve_done)
                eng.wait_ge(*dve.latest)
                dve(stt(s5_b, phase, -1.0, phase, ALU.mult, ALU.max).then_inc(s5_ang, 1), s5_ang)
            elif kind == "s5_mats_prep":
                dve(tt(s5_n, s5_are, s5_are, ALU.mult).then_inc(dve_done, 1), dve_done)
                dve(tt(s5_m, s5_aim, s5_aim, ALU.mult).then_inc(dve_done, 1), dve_done)
                eng.wait_ge(*dve.latest)
                dve(tt(s5_n, s5_n, s5_m, ALU.add).then_inc(dve_done, 1), dve_done)
                eng.wait_ge(*dve.latest)
                dve(eng.reciprocal(s5_den, s5_n).then_inc(dve_done, 1), dve_done)
                eng.wait_ge(s5_sin, 2)
                dve(tt(s5_fr, s5_r, s5_c, ALU.mult).then_inc(dve_done, 1), dve_done)
                dve(tt(s5_fi, s5_r, s5_s, ALU.mult).then_inc(s5_lam, 1), s5_lam)
                eng.wait_ge(*dve.latest)
                dve(ts(s5_fr, s5_fr, -1.0, None, ALU.add).then_inc(dve_done, 1), dve_done)
                eng.wait_ge(*dve.latest)
                dve(tt(s5_m, s5_fr, s5_are, ALU.mult).then_inc(dve_done, 1), dve_done)
                dve(tt(s5_n, s5_fi, s5_aim, ALU.mult).then_inc(dve_done, 1), dve_done)
                dve(tt(s5_a, s5_fi, s5_are, ALU.mult).then_inc(dve_done, 1), dve_done)
                dve(tt(s5_b, s5_fr, s5_aim, ALU.mult).then_inc(dve_done, 1), dve_done)
                eng.wait_ge(*dve.latest)
                dve(tt(s5_m, s5_m, s5_n, ALU.add).then_inc(dve_done, 1), dve_done)
                dve(tt(s5_a, s5_a, s5_b, ALU.subtract).then_inc(dve_done, 1), dve_done)
                eng.wait_ge(*dve.latest)
                dve(tt(s5_fr, s5_m, s5_den, ALU.mult).then_inc(dve_done, 1), dve_done)
                dve(tt(s5_fi, s5_a, s5_den, ALU.mult).then_inc(dve_done, 1), dve_done)
                for z in (bxr, bxi, cxr, cxi):
                    dve(eng.memset(z, 0.0).then_inc(dve_done, 1), dve_done)
                eng.wait_ge(*dve.latest)
                eng.wait_ge(s5_in, 16 * 6)
                fr, fi = col(s5_fr, P, 16, 16), col(s5_fi, P, 16, 16)
                for n, (f, bb) in enumerate(((fr, bre), (fi, bim), (fi, bre), (fr, bim))):
                    dve(tt(b_prod[:, n, :, :], bb, f, ALU.mult).then_inc(dve_done, 1), dve_done)
                eng.wait_ge(*dve.latest)
                for hf in range(2):
                    rows, cols = slice(64 * hf, 64 * hf + 64), slice(16 * hf, 16 * hf + 16)
                    dve(tt(bxr[rows, :, cols], b_prod[rows, 0, :, :], b_prod[rows, 1, :, :], ALU.subtract).then_inc(dve_done, 1), dve_done)
                    dve(tt(bxi[rows, :, cols], b_prod[rows, 2, :, :], b_prod[rows, 3, :, :], ALU.add).then_inc(s5_bx if hf else dve_done, 1),
                        s5_bx if hf else dve_done)
            elif kind == "ss":
                i, g, jp = a
                u = 4 * i + 2 * g + jp
                w = P if i == 0 else 2 * P
                k0 = 2 * P - w
                eng.wait_ge(dve_bank_full, V.nth(step))
                b = V.bank(step)
                if u == 0:
                    eng.wait_ge(alibi_in, 16)
                h0 = 4 * g + 2 * jp
                two = sS[:, u % 2, 0:2 * w].rearrange("p (j k) -> p j k", j=2)
                dve(tt(two, b[:, 0:2 * w].rearrange("p (j k) -> p j k", j=2), alibi[:, h0:h0 + 2, k0:], ALU.add).then_inc(dve_bank_copied, 1), dve_bank_copied)
                eng.wait_ge(*dve.latest)
                dve(eng.reduce_max(mx[:, u % 2, 0:2], two, AX.X).then_inc(dve_done, 1), dve_done)
                eng.wait_ge(*dve.latest)
                dve(tt(mx[:, u % 2, 0:2], mx[:, u % 2, 0:2], sinks[:, h0:h0 + 2], ALU.max).then_inc(dve_done, 1), dve_done)
                eng.wait_ge(*dve.latest)
                dve(tt(esink[:, u % 2, 0:2], sinks[:, h0:h0 + 2], mx[:, u % 2, 0:2], ALU.subtract).then_inc(dve_done, 1), dve_done)
                dve(ts(nmx[:, u % 2, 0:2], mx[:, u % 2, 0:2], -1.0, None, ALU.mult).then_inc(win_ready, 1), win_ready)
            elif kind == "sn":
                i, g, jp = a
                u = 4 * i + 2 * g + jp
                w = P if i == 0 else 2 * P
                eng.wait_ge(win_exp, u + 1)
                dve(tt(rsum[:, u % 2, 0:2], rsum[:, u % 2, 0:2], esink[:, u % 2, 0:2], ALU.add).then_inc(dve_done, 1), dve_done)
                eng.wait_ge(*dve.latest)
                dve(eng.reciprocal(rinv[:, u % 2, 0:2], rsum[:, u % 2, 0:2]).then_inc(dve_done, 1), dve_done)
                eng.wait_ge(*dve.latest)
                two = sP[:, u % 2, 0:2 * w].rearrange("p (j k) -> p j k", j=2)
                dve(tt(two, two, col(rinv[:, u % 2, 0:2], P, 2, w), ALU.mult).then_inc(win_probs, 1), win_probs)
            elif kind == "swa_end":
                eng.wait_ge(act_bank_copied, A.nth(("so", 3, 1, 1)))
                dve(eng.memset(mv, 0.0).then_inc(swa_done, 1), swa_done)
            elif kind == "bu":
                i = a[0]
                if i == 0:
                    eng.wait_ge(act_bank_copied, A.nth(("mat", 3, 3)))
                eng.wait_ge(s5_table, i + 1)
                turn = phasor[:, i % 2, :, :]
                b0, b1 = V.bank(("bu", i, 0)), V.bank(("bu", i, 1))
                wide = (P, 2, 512)
                eng.wait_ge(dve_bank_full, V.nth(("bu", i, 0)))
                dve(tt(tu, b0[:, :].unsqueeze(1).to_broadcast(wide), turn, ALU.mult).then_inc(dve_bank_copied, 1), dve_bank_copied)
                eng.wait_ge(dve_bank_full, V.nth(("bu", i, 1)))
                dve(tt(tw, b1[:, :].unsqueeze(1).to_broadcast(wide), turn, ALU.mult).then_inc(dve_bank_copied, 1), dve_bank_copied)
                eng.wait_ge(*dve.latest)
                dve(tt(tu[:, 0, :], tu[:, 0, :], tw[:, 1, :], ALU.add).then_inc(dve_done, 1), dve_done)
                dve(tt(tw[:, 0, :], tw[:, 0, :], tu[:, 1, :], ALU.subtract).then_inc(dve_done, 1), dve_done)
                eng.wait_ge(*dve.latest)
                r = s5_r[:, i:i + 1].to_broadcast((P, 512))
                dve(eng.tensor_tensor_scan(zr, r, tu[:, 0, :], 0.0, ALU.mult, ALU.add).then_inc(dve_done, 1), dve_done)
                dve(eng.tensor_tensor_scan(zi, r, tw[:, 0, :], 0.0, ALU.mult, ALU.add).then_inc(dve_done, 1), dve_done)
                eng.wait_ge(*dve.latest)
                dve(tt(tu, zr.unsqueeze(1).to_broadcast(wide), turn, ALU.mult).then_inc(dve_done, 1), dve_done)
                dve(tt(tw, zi.unsqueeze(1).to_broadcast(wide), turn, ALU.mult).then_inc(s5_table_used, 1), s5_table_used)
                if i >= 2:
                    eng.wait_ge(y_step, i - 1)
                eng.wait_ge(*dve.latest)
                dve(tt(sr[:, i % 2, :], tu[:, 0, :], tw[:, 1, :], ALU.subtract).then_inc(dve_done, 1), dve_done)
                dve(tt(si[:, i % 2, :], tu[:, 1, :], tw[:, 0, :], ALU.add).then_inc(s5_state, 1), s5_state)
            elif kind == "y" and a[0] % 4 == 3:
                Tt = a[0] // 4
                eng.wait_ge(y_step, a[0] + 1)
                dve(stt(uT[:, Tt, :], uT[:, Tt, :], s5_d[:, Tt:Tt + 1], y_bank[:, :], ALU.mult, ALU.add).then_inc(y_taken, 1), y_taken)
            elif kind == "glu_end":
                eng.wait_ge(act_bank_copied, A.nth(("glu", 3)))
                dve(tt(uT[:, :, :], uT[:, :, :], glu_gate, ALU.mult).then_inc(glu_ready, 1), glu_ready)
            elif kind == "ln1":
                i = a[0]
                eng.wait_ge(act_bank_copied, A.nth(("wo", i, 1)))
                y = ln_y[:, i % 2, :]
                dve(stt(y, x[:, i, :], alpha, y, ALU.mult, ALU.add).then_inc(dve_done, 1), dve_done)
                if i == 0:
                    eng.wait_ge(ln_in, 32)
                layer_norm_tile(dve, eng, dve_done, ln_sd, ln_var, i, y, x[:, i, :], ln_g, ln_b, stats, mv, rstd, ln_done)

    @block.tensor
    def _(eng):
        mm = eng.matmul

        def chain(out, pairs):
            for n, (lhs, rhs) in enumerate(pairs):
                ins = mm(out, lhs, rhs, start=n == 0, stop=n == len(pairs) - 1)
            return ins

        def project(step, kind, c0, width, c, n=P):
            w = weights(eng, kind, c0, width)
            if A.reused(step):
                eng.wait_ge(act_bank_copied, A.last_user(step))
            b = A.bank(step)
            chain(b[0:n, :], [(w[:, k, c:c + n], xT[:, k, :]) for k in range(8)]).then_inc(act_bank_full, 1)

        def flip(out, src):
            return eng.transpose(out, src, ident[:, :])

        branch_in = {3: odT, 2: cgT, 1: qT, 0: uT}
        ukv = w_ukv.rearrange("p (h n) -> p h n", h=4)

        for step in plan:
            kind, a = step[0], step[1:]
            if kind == "xt":
                ring, full, copied = (A, act_bank_full, act_bank_copied) if step in A.number else (V, dve_bank_full, dve_bank_copied)
                if ring.reused(step):
                    eng.wait_ge(copied, ring.last_user(step))
                b = ring.bank(step)
                for i in range(4):
                    src = x[:, i, :].rearrange("p (m k) -> p k m", k=8)[:, a[0], :]
                    ins = flip(b[:, toks(i)], src)
                ins.then_inc(full, 1)
            elif kind == "lr":
                eng.wait_ge(act_bank_copied, A.nth(("xt", 7)))
                eng.wait_ge(dve_bank_copied, V.nth(("xt", 6)))
                project(step, "in", COL_LR, 272, 0, 16)
            elif kind == "qd":
                project(step, "in", COL_LR, 272, 16 + P * a[0])
            elif kind == "kvd":
                project(step, "in", COL_KVD, 256, 0)
            elif kind == "kr":
                project(step, "in", COL_KVD, 256, P)
            elif kind == "krs":
                if V.reused(step):
                    eng.wait_ge(dve_bank_copied, V.last_user(step))
                b = V.bank(step)
                eng.wait_ge(act_bank_copied, A.nth(("kr",)))
                chain(b[:, :], [(half_swap[:, :], kr)]).then_inc(dve_bank_full, 1)
            elif kind == "rq":
                if A.reused(step):
                    eng.wait_ge(act_bank_copied, A.last_user(step))
                b = A.bank(step)
                eng.wait_ge(act_bank_copied, A.nth(("qd", 1)))
                chain(b[:, :], [(ones[:, :], ml_t1[:, t, :]) for t in range(2)]).then_inc(act_bank_full, 1)
            elif kind == "rk":
                if A.reused(step):
                    eng.wait_ge(act_bank_copied, A.last_user(step))
                b = A.bank(step)
                eng.wait_ge(act_bank_copied, A.nth(("kvd",)))
                chain(b[:, :], [(ones[:, :], ml_t2)]).then_inc(act_bank_full, 1)
            elif kind == "mqn":
                if A.reused(step):
                    eng.wait_ge(act_bank_copied, A.last_user(step))
                b = A.bank(step)
                eng.wait_ge(normed, 1)
                eng.wait_ge(params_in, 16 * 16)
                chain(b[:, :], [(w_uq[:, k, toks(a[0])], qd[:, k, :]) for k in range(2)]).then_inc(act_bank_full, 1)
            elif kind == "mkn":
                if A.reused(step):
                    eng.wait_ge(act_bank_copied, A.last_user(step))
                b = A.bank(step)
                eng.wait_ge(normed, 2)
                chain(b[:, :], [(ukv[:, a[0], 0:P], kvd)]).then_inc(act_bank_full, 1)
            elif kind == "mqr":
                if A.reused(step):
                    eng.wait_ge(act_bank_copied, A.last_user(step))
                b = A.bank(step)
                t = a[0]
                chain(b[:, :], [(w_uq[:, k, 512 + P * t:640 + P * t], qd[:, k, :]) for k in range(2)]).then_inc(act_bank_full, 1)
            elif kind == "mqs":
                if V.reused(step):
                    eng.wait_ge(dve_bank_copied, V.last_user(step))
                b = V.bank(step)
                eng.wait_ge(act_bank_copied, A.nth(("mqr", a[0])))
                chain(b[:, :], [(half_swap[:, :], qr[:, a[0], :])]).then_inc(dve_bank_full, 1)
            elif kind == "mv":
                if A.reused(step):
                    eng.wait_ge(act_bank_copied, A.last_user(step))
                b = A.bank(step)
                chain(b[:, :], [(kvd[:, toks(a[0])], ukv[:, :, P:2 * P])]).then_inc(act_bank_full, 1)
            elif kind == "ms":
                i, h = a
                n, rows = P * (i + 1), slice(64 * (h % 2), 64 * (h % 2) + 64)
                if A.reused(step):
                    eng.wait_ge(act_bank_copied, A.last_user(step))
                b = A.bank(step)
                eng.wait_ge(act_bank_copied, A.nth(("mv", 3)))
                eng.wait_ge(rope_ready, 3)
                chain(b[:, 0:n], [(qn[:, h, toks(i)], kn[:, h, 0:n]), (qr[rows, h // 2, toks(i)], kr[rows, 0:n])]).then_inc(act_bank_full, 1)
            elif kind == "mp":
                i, h = a
                u = 4 * i + h
                if A.reused(step):
                    eng.wait_ge(act_bank_copied, A.last_user(step))
                b = A.bank(step)
                eng.wait_ge(probs_ready, u + 1)
                for kb in range(i + 1):
                    ins = flip(b[:, toks(kb)], mP[:, u % 2, toks(kb)])
                ins.then_inc(act_bank_full, 1)
            elif kind == "mo":
                i, h = a
                u = 4 * i + h
                if A.reused(step):
                    eng.wait_ge(act_bank_copied, A.last_user(step))
                b = A.bank(step)
                eng.wait_ge(act_bank_copied, A.nth(("mp", i, h)))
                chain(b[:, 0:P], [(vm[:, kb, toks(h)], mPT[:, u % 2, kb, :]) for kb in range(i + 1)]).then_inc(act_bank_full, 1)
            elif kind == "q":
                project(step, "in", COL_Q + a[0] // 2 * BLK, BLK, a[0] % 2 * P)
            elif kind == "k":
                project(step, "in", COL_K, BLK, 0)
            elif kind == "v":
                w = weights(eng, "in", COL_K, BLK)
                if A.reused(step):
                    eng.wait_ge(act_bank_copied, A.last_user(step))
                b = A.bank(step)
                for i in range(4):
                    ins = chain(b[:, toks(i)], [(xT[:, k, toks(i)], w[:, k, P:2 * P]) for k in range(8)])
                ins.then_inc(act_bank_full, 1)
            elif kind in ("u", "cg"):
                project(step, "in", {"u": COL_U, "cg": COL_CG}[kind] + a[0] // 2 * BLK, BLK, a[0] % 2 * P)
            elif kind in ("cq", "ck"):
                project(step, "in", COL_CQ + (BLK if kind == "ck" else 0), BLK, a[0] * P)
            elif kind == "cv":
                if A.reused(step):
                    eng.wait_ge(act_bank_copied, A.last_user(step))
                b = A.bank(step)
                for half in range(2):
                    w = weights(eng, "in", COL_CV + half * BLK, BLK)
                    ins = chain(b[:, half * BLK:(half + 1) * BLK], [(xT[:, k, toks(a[0])], w[:, k, :]) for k in range(8)])
                ins.then_inc(act_bank_full, 1)
            elif kind == "lg":
                for t in range(2):
                    if V.reused(("lg", t)):
                        eng.wait_ge(dve_bank_copied, V.last_user(("lg", t)))
                    b = V.bank(("lg", t))
                    eng.wait_ge(act_bank_copied, A.nth(("lr",)))
                    chain(b[:, :], [(w_lr2[:, t * P:(t + 1) * P], lrT[:, :])]).then_inc(dve_bank_full, 1)
            elif kind == "krt":
                eng.wait_ge(gdec_ready, 1)
                if A.reused(step):
                    eng.wait_ge(act_bank_copied, A.last_user(step))
                b = A.bank(step)
                for n in range(4):
                    i, t = 2 * a[0] + n // 2, n % 2
                    ins = flip(b[:, toks(n)], gtmp[:, t, toks(i)])
                ins.then_inc(act_bank_full, 1)
            elif kind == "kv":
                t = a[0]
                eng.wait_ge(act_bank_copied, A.nth(("krt", 1)))
                eng.wait_ge(act_bank_copied, A.nth(("cv", 3)))
                for par in (1, 0):
                    if V.reused(("kv", t, par)):
                        eng.wait_ge(dve_bank_copied, V.last_user(("kv", t, par)))
                    b = V.bank(("kv", t, par))
                    chunks = range(par, 7, 2)
                    rows = slice(64 * par, 64 * par + 64)
                    for c in chunks:
                        for hh in range(2):
                            out = b[64 * hh:64 * hh + 64, (c // 2) * P:(c // 2 + 1) * P]
                            h = 2 * t + hh
                            ins = chain(out, [(kremN[rows, c // 2, t, 64 * hh:64 * hh + 64], cv[rows, c // 2, toks(h)])])
                    ins.then_inc(dve_bank_full, 1)
            elif kind == "att":
                h = a[0]
                rows = slice(64 * (h % 2), 64 * (h % 2) + 64)
                if V.reused(step):
                    eng.wait_ge(dve_bank_copied, V.last_user(step))
                b = V.bank(step)
                eng.wait_ge(gdec_ready, 1)
                for i in range(4):
                    ins = chain(b[:, toks(i)], [(ck[rows, h // 2, toks(i)], cq[rows, h // 2, toks(i)])])
                ins.then_inc(dve_bank_full, 1)
            elif kind == "go":
                h = a[0]
                rows = slice(64 * (h % 2), 64 * (h % 2) + 64)
                if A.reused(step):
                    eng.wait_ge(act_bank_copied, A.last_user(step))
                b = A.bank(step)
                eng.wait_ge(dve_bank_copied, V.nth(("att", h)))
                for i in range(4):
                    mm(b[:, toks(i)], cv[:, i, toks(h)], attT[:, h % 2, toks(i)], start=True, stop=False,
                       skip_group_check=True)
                    for c in (2 * i, 2 * i + 1):
                        if c:
                            ins = mm(b[:, c * 64:c * 64 + 64], gstate[rows, h // 2, c - 1, :], cq[rows, h // 2, c * 64:c * 64 + 64],
                                     start=False, stop=c % 2 == 1, skip_group_check=True)
                ins.then_inc(act_bank_full, 1)
            elif kind == "gc":
                if A.reused(step):
                    eng.wait_ge(act_bank_copied, A.last_user(step))
                b = A.bank(step)
                eng.wait_ge(act_bank_copied, A.nth(("go", a[0])))
                chain(b[:, :], [(centre[:, :], oT[:, a[0] % 2, :])]).then_inc(act_bank_full, 1)
            elif kind == "gv":
                if A.reused(step):
                    eng.wait_ge(act_bank_copied, A.last_user(step))
                b = A.bank(step)
                eng.wait_ge(act_bank_copied, A.nth(("gc", a[0])))
                chain(b[:, :], [(ones[:, :], osq[:, a[0] % 2, :])]).then_inc(act_bank_full, 1)
            elif kind == "gate":
                n, dt = a
                w = weights(eng, "in", COL_GATE + n * 1024 + dt // 2 * BLK, BLK)
                if A.reused(step):
                    eng.wait_ge(act_bank_copied, A.last_user(step))
                b = A.bank(step)
                chain(b[:, :], [(w[:, k, dt % 2 * P:dt % 2 * P + P], xT[:, k, :]) for k in range(8)]).then_inc(act_bank_full, 1)
            elif kind == "mix":
                n, dt = a
                if n == 3:
                    eng.wait_ge(act_bank_copied, A.nth(("mo", 3, 3)))
                elif n == 2:
                    eng.wait_ge(gout_ready, 4)
                elif n == 1:
                    eng.wait_ge(act_bank_copied, A.nth(("so", 3, 1, 1)))
                else:
                    eng.wait_ge(glu_ready, 1)
                w = weights(eng, "branch", n, dt // 4 * 512)
                if V.reused(step):
                    eng.wait_ge(dve_bank_copied, V.last_user(step))
                b = V.bank(step)
                chain(b[:, :], [(w[:, k, dt % 4 * P:dt % 4 * P + P], branch_in[n][:, k, :]) for k in range(4)]).then_inc(dve_bank_full, 1)
            elif kind == "ss":
                i, g, jp = a
                w = P if i == 0 else 2 * P
                rows, k0 = slice(64 * g, 64 * g + 64), P * (i + 1) - w
                if V.reused(step):
                    eng.wait_ge(dve_bank_copied, V.last_user(step))
                b = V.bank(step)
                for j in range(2):
                    ins = chain(b[:, j * w:(j + 1) * w], [(qT[rows, 2 * jp + j, toks(i)], kT[rows, k0:k0 + w])])
                ins.then_inc(dve_bank_full, 1)
            elif kind == "sp":
                i, g, jp = a
                u = 4 * i + 2 * g + jp
                nb = 2 if i == 0 else 4
                if A.reused(step):
                    eng.wait_ge(act_bank_copied, A.last_user(step))
                b = A.bank(step)
                eng.wait_ge(win_probs, u + 1)
                for n in range(nb):
                    ins = flip(b[:, toks(n)], sP[:, u % 2, toks(n)])
                ins.then_inc(act_bank_full, 1)
            elif kind == "so":
                i, g, jp = a
                u = 4 * i + 2 * g + jp
                kb = [0] if i == 0 else [i - 1, i]
                if A.reused(step):
                    eng.wait_ge(act_bank_copied, A.last_user(step))
                b = A.bank(step)
                eng.wait_ge(act_bank_copied, A.nth(("sp", i, g, jp)))
                for j in range(2):
                    ins = chain(b[64 * g:64 * g + 64, toks(j)],
                          [(v_nat[:, blk, 64 * g:64 * g + 64], sPT[:, u % 2, j * len(kb) + n, :]) for n, blk in enumerate(kb)])
                ins.then_inc(act_bank_full, 1)
            elif kind == "s5_mats":
                Tt = a[0]
                eng.wait_ge(s5_bx, 1)
                eng.wait_ge(s5_in, 16 * 6)
                srcs = [bxr[:, 4 * Tt:4 * Tt + 4, :].rearrange("p a b -> p (a b)"),
                        bxi[:, 4 * Tt:4 * Tt + 4, :].rearrange("p a b -> p (a b)"), cre[:, Tt, :], cim[:, Tt, :]]
                for m, src in enumerate(srcs):
                    if A.reused(("mat", Tt, m)):
                        eng.wait_ge(act_bank_copied, A.last_user(("mat", Tt, m)))
                    b = A.bank(("mat", Tt, m))
                    flip(b[:, 0:P], src).then_inc(act_bank_full, 1)
            elif kind == "bu":
                i = a[0]
                rows = slice(32 * (i % 4), 32 * (i % 4) + 32)
                eng.wait_ge(act_bank_copied, A.nth(("mat", 3, 3)))
                for m, mat in enumerate((btr, bti)):
                    if V.reused(("bu", i, m)):
                        eng.wait_ge(dve_bank_copied, V.last_user(("bu", i, m)))
                    b = V.bank(("bu", i, m))
                    chain(b[:, :], [(mat[rows, i // 4, :], uT[rows, i // 4, :])]).then_inc(dve_bank_full, 1)
            elif kind == "y":
                i = a[0]
                rows = slice(32 * (i % 4), 32 * (i % 4) + 32)
                eng.wait_ge(s5_state, i + 1)
                if i % 4 == 0 and i:
                    eng.wait_ge(y_taken, i // 4)
                mm(y_bank[rows, :], cxr[:, i, :], sr[:, i % 2, :], start=True, stop=False)
                mm(y_bank[rows, :], cxi[:, i, :], si[:, i % 2, :], start=False, stop=True).then_inc(y_step, 1)
            elif kind == "glu":
                w = weights(eng, "glu", a[0] // 2 * BLK, BLK)
                if A.reused(step):
                    eng.wait_ge(act_bank_copied, A.last_user(step))
                b = A.bank(step)
                eng.wait_ge(gelu_done, 1)
                chain(b[:, :], [(w[:, k, a[0] % 2 * P:a[0] % 2 * P + P], uT[:, k, :]) for k in range(4)]).then_inc(act_bank_full, 1)
            elif kind == "wo":
                i, half = a
                if A.reused(step):
                    eng.wait_ge(act_bank_copied, A.last_user(step))
                b = A.bank(step)
                eng.wait_ge(mix_used, 32)
                for c in range(2):
                    w = weights(eng, "out", (2 * half + c) * BLK, BLK)
                    ins = chain(b[:, c * BLK:(c + 1) * BLK], [(mx_all[:, k, toks(i)], w[:, k, :]) for k in range(8)])
                ins.then_inc(act_bank_full, 1)


def layer_norm_tile(dve, eng, dve_done, act_sd, var_ready, n, y, out, g, b, stats, mv, rstd, done):
    if dve.latest:
        eng.wait_ge(*dve.latest)
    for half in range(2):
        dve(eng.bn_stats(stats[:, 6 * half:6 * half + 6], y[:, 512 * half:512 * half + 512]).then_inc(dve_done, 1), dve_done)
    eng.wait_ge(*dve.latest)
    dve(eng.bn_aggr(mv, stats).then_inc(var_ready, 1), var_ready)
    eng.wait_ge(act_sd, n + 1)
    dve(eng.reciprocal(rstd, rstd).then_inc(dve_done, 1), dve_done)
    eng.wait_ge(*dve.latest)
    dve(eng.tensor_scalar(y, y, mv[:, 0:1], rstd, ALU.subtract, ALU.mult).then_inc(dve_done, 1), dve_done)
    eng.wait_ge(*dve.latest)
    dve(eng.tensor_tensor(y, y, g, ALU.mult).then_inc(dve_done, 1), dve_done)
    eng.wait_ge(*dve.latest)
    dve(eng.tensor_tensor(out, y, b, ALU.add).then_inc(done, 1), done)


def routing_plan():
    steps = [("xt", k) for k in range(8)] + [("rt", i) for i in range(4)] + [("scale",)]
    for i in range(4):
        steps += [("cnt", i), ("sg", i)] + ([("sd", i - 1, 0), ("sd", i - 1, 1)] if i else []) + [("sh", i)]
        if i == 3:
            steps += [("tot",), ("places",)]
    return steps + [("sd", 3, 0), ("sd", 3, 1)]


def build_routing(nc, ctx, T, layer, W, keep, sem):
    alpha, x, ident, ones = T["alpha"], keep["x"], keep["ident"], keep["ones"]
    x1T = keep["x1T"]
    plan = routing_plan()
    keys_act = [s for s in plan if s[0] in ("rt", "sh") or (s[0] == "xt" and s[1] % 2)]
    keys_dve = [s for s in plan if s[0] in ("cnt", "tot", "sg", "sd") or (s[0] == "xt" and not s[1] % 2)]

    def sb(name, shape, dt=F32):
        return ctx.enter_context(nc.sbuf_tensor("route_" + name, shape, dt))

    sh_gu, sh_dn = sb("sh_gu", [P, 8, 512]), sb("sh_dn", [P, 2, 1024])
    silu, h, hT, flag = sb("silu", [P, 2, 256]), sb("h", [P, 2, 256]), sb("hT", [P, 2, 2, P]), sb("flag", [P, 1])
    w_router, bias = sb("w_router", [P, 8, 64]), sb("bias", [P, 64])
    score, biased, left = sb("score", [P, 4, 64]), sb("biased", [P, 4, 64]), sb("left", [P, 4, 64])
    sel, wgt, code = sb("sel", [P, 4, 64]), sb("wgt", [P, 4, 64]), sb("code", [P, 4, 64])
    top, codes = sb("top", [P, 4, 8]), sb("codes", [P, 4, 8])
    wsum, most = sb("wsum", [P, 4]), sb("most_f", [P, 1])
    match = sb("match", [P, 8, 64])
    slot_id, expert_id, place_id = (sb(n, [P, 4, 8], I32) for n in ("slot_id", "expert_id", "place_id"))
    row, place = sb("row", [P, 4, 8]), sb("place", [P, 4, 8])
    before, expert_code, token_id = sb("before", [P, P]), sb("expert_code", [P, 64]), sb("token_id", [P, 4], I32)

    pa = [ctx.enter_context(nc.psum_tensor(f"route_act_bank{n}", [P, 512], F32)) for n in range(4)]
    pv = [ctx.enter_context(nc.psum_tensor(f"route_dve_bank{n}", [P, 512], F32)) for n in range(4)]
    A, V = Ring(pa, keys_act), Ring(pv, keys_dve)
    act_bank_full, act_bank_copied = sem("act_bank_full"), sem("act_bank_copied")
    dve_bank_full, dve_bank_copied = sem("dve_bank_full"), sem("dve_bank_copied")
    dve_done, scaled = sem("dve_done"), sem("x_scaled")
    x1_stored = sem("x1_stored")
    router_in, tables_in, weights_in = sem("router_in"), sem("tables_in"), sem("first_experts_in")
    cleared, listed = sem("token_table_cleared"), sem("tokens_listed")
    chosen, slots_ready = sem("experts_chosen"), sem("slots_ready")
    shared_gu_in, shared_dn_in, silu_done, h_ready = (
        sem(n) for n in ("shared_gate_up_in", "shared_down_in", "silu_done", "h_ready"))

    def toks(i, n=P):
        return slice(i * n, i * n + n)

    block = ctx.enter_context(nc.Block())

    @block.sync
    def _(eng):
        def load(dst, src, done):
            eng.dma_start(dst, src).then_inc(done, 16)

        rows = "(p k) n -> p k n"
        load(w_router[:, :, :], W["router_w"][layer].rearrange(rows, p=P), router_in)
        load(bias[:, :], W["router_bias"][layer].partition_broadcast(P), router_in)
        load(before[:, :], T["before"], tables_in)
        load(expert_code[:, :], T["expert_code"], tables_in)
        load(token_id[:, :], T["token_id"], tables_in)
        load(sh_gu[:, :, 0:256], W["sh_w_gate"][layer].rearrange(rows, p=P), shared_gu_in)
        load(sh_gu[:, :, 256:512], W["sh_w_up"][layer].rearrange(rows, p=P), shared_gu_in)
        load(T["x1_dram"].rearrange("(i p) d -> p i d", p=P), x[:, :, :], x1_stored)
        load(sh_dn[:, :, :], W["sh_w_down"][layer].rearrange("(k p) n -> p k n", p=P), shared_dn_in)
        for j in range(EXPERT_RING):
            for dst, src in expert_weights(W, layer, keep, j, j):
                load(dst, src, weights_in)
        eng.wait_ge(weights_in, 16 * 3 * EXPERT_RING)

    @block.gpsimd
    def _(eng):
        eng.dma_start(T["token_table"].rearrange("(p n) o -> p (n o)", p=P), T["no_token"]).then_inc(cleared, 16)
        eng.wait_ge(cleared, 16)
        eng.wait_ge(tables_in, 48)
        for i in range(4):
            eng.wait_ge(slots_ready, i + 1)
            for k in range(TOP_K):
                eng.indirect_dma_start(T["token_table"], bass.IndirectOffsetOnAxis(slot_id[:, i, k:k + 1], 0),
                                       token_id[:, i:i + 1], None).then_inc(listed, 16)
        eng.wait_ge(listed, 16 * 4 * TOP_K)

    @block.scalar
    def _(eng):
        act = Count()
        for step in plan:
            kind, a = step[0], step[1:]
            if kind == "xt" and step in A.number:
                eng.wait_ge(act_bank_full, A.nth(step))
                b = A.bank(step)
                act(eng.copy(x1T[:, a[0], :], b[:, :]).then_inc(act_bank_copied, 1), act_bank_copied)
            elif kind == "rt":
                eng.wait_ge(act_bank_full, A.nth(step))
                b = A.bank(step)
                act(eng.activation(score[:, a[0], :], b[:, 0:64], ACT.Sigmoid).then_inc(act_bank_copied, 1), act_bank_copied)
            elif kind == "scale":
                eng.wait_ge(x1_stored, 16)
                eng.wait_ge(act_bank_full, A.nth(("xt", 7)))
                eng.wait_ge(dve_bank_full, V.nth(("xt", 6)))
                act(eng.mul(x[:, :, :], x[:, :, :], alpha).then_inc(scaled, 1), scaled)
            elif kind == "sg":
                if a[0] >= 2:
                    eng.wait_ge(h_ready, a[0] - 1)
                eng.wait_ge(dve_bank_full, V.nth(step))
                b = V.bank(step)
                act(eng.activation(silu[:, a[0] % 2, :], b[:, 0:256], ACT.Silu).then_inc(silu_done, 1), silu_done)
            elif kind == "sh":
                eng.wait_ge(act_bank_full, A.nth(step))
                b = A.bank(step)
                act(eng.copy(hT[:, a[0] % 2, :, :].rearrange("p a b -> p (a b)"), b[:, 0:256]).then_inc(act_bank_copied, 1), act_bank_copied)

    @block.vector
    def _(eng):
        dve = Count()
        tt, ts, stt = eng.tensor_tensor, eng.tensor_scalar, eng.scalar_tensor_tensor
        for step in plan:
            kind, a = step[0], step[1:]
            if dve.latest:
                eng.wait_ge(*dve.latest)
            if kind == "xt" and step in V.number:
                eng.wait_ge(dve_bank_full, V.nth(step))
                b = V.bank(step)
                dve(eng.tensor_copy(x1T[:, a[0], :], b[:, :]).then_inc(dve_bank_copied, 1), dve_bank_copied)
            elif kind == "rt":
                i = a[0]
                eng.wait_ge(router_in, 32)
                eng.wait_ge(act_bank_copied, A.nth(step))
                dve(tt(biased[:, i, :], score[:, i, :], bias[:, :], ALU.add).then_inc(dve_done, 1), dve_done)
                eng.wait_ge(*dve.latest)
                dve(eng.max(top[:, i, :], biased[:, i, :]).then_inc(dve_done, 1), dve_done)
                eng.wait_ge(*dve.latest)
                dve(eng.match_replace(left[:, i, :], top[:, i, :], biased[:, i, :], MASKED).then_inc(dve_done, 1), dve_done)
                eng.wait_ge(*dve.latest)
                dve(tt(sel[:, i, :], left[:, i, :], biased[:, i, :], ALU.not_equal).then_inc(chosen, 1), chosen)
                eng.wait_ge(*dve.latest)
                dve(tt(wgt[:, i, :], score[:, i, :], sel[:, i, :], ALU.mult).then_inc(dve_done, 1), dve_done)
                eng.wait_ge(*dve.latest)
                dve(eng.reduce_sum(wsum[:, i:i + 1], wgt[:, i, :], AX.X).then_inc(dve_done, 1), dve_done)
                eng.wait_ge(*dve.latest)
                dve(eng.reciprocal(wsum[:, i:i + 1], wsum[:, i:i + 1]).then_inc(dve_done, 1), dve_done)
                eng.wait_ge(*dve.latest)
                dve(ts(wgt[:, i, :], wgt[:, i, :], wsum[:, i:i + 1], ROUTED_SCALE, ALU.mult, ALU.mult).then_inc(dve_done, 1), dve_done)
            elif kind == "cnt":
                i = a[0]
                eng.wait_ge(dve_bank_full, V.nth(step))
                b = V.bank(step)
                if i == 0:
                    eng.wait_ge(tables_in, 48)
                dve(stt(code[:, i, :], b[:, 0:64], 64.0, expert_code[:, :], ALU.mult, ALU.add).then_inc(dve_bank_copied, 1), dve_bank_copied)
                eng.wait_ge(*dve.latest)
                dve(tt(code[:, i, :], code[:, i, :], sel[:, i, :], ALU.mult).then_inc(dve_done, 1), dve_done)
                eng.wait_ge(*dve.latest)
                dve(eng.max(codes[:, i, :], code[:, i, :]).then_inc(dve_done, 1), dve_done)
                eng.wait_ge(*dve.latest)
                dve(ts(slot_id[:, i, :], codes[:, i, :], -1.0, None, ALU.add).then_inc(slots_ready, 1), slots_ready)
                dve(tt(match[:, :, :], code[:, i, :].unsqueeze(1).to_broadcast((P, 8, 64)),
                       codes[:, i, :].unsqueeze(2).to_broadcast((P, 8, 64)), ALU.is_equal).then_inc(dve_done, 1), dve_done)
                eng.wait_ge(*dve.latest)
                dve(tt(match[:, :, :], match[:, :, :], wgt[:, i, :].unsqueeze(1).to_broadcast((P, 8, 64)), ALU.mult).then_inc(dve_done, 1), dve_done)
                eng.wait_ge(*dve.latest)
                dve(eng.reduce_sum(keep["pick_w"][:, i, :], match[:, :, :], AX.X).then_inc(dve_done, 1), dve_done)
            elif kind == "tot":
                eng.wait_ge(dve_bank_full, V.nth(step))
                b = V.bank(step)
                dve(eng.reduce_max(most[:, :], b[:, 0:64], AX.X).then_inc(dve_bank_copied, 1), dve_bank_copied)
                eng.wait_ge(*dve.latest)
                dve(eng.tensor_copy(keep["most"][:, :], most[:, :]).then_inc(dve_done, 1), dve_done)
                dve(eng.memset(keep["round_now"][:, :], 1.0).then_inc(dve_done, 1), dve_done)
            elif kind == "places":
                dve(ts(expert_id[:, :, :], slot_id[:, :, :], 63, None, ALU.bitwise_and).then_inc(dve_done, 1), dve_done)
                dve(ts(place_id[:, :, :], slot_id[:, :, :], 6, None, ALU.logical_shift_right).then_inc(dve_done, 1), dve_done)
                eng.wait_ge(*dve.latest)
                dve(eng.tensor_copy(row[:, :, :], expert_id[:, :, :]).then_inc(dve_done, 1), dve_done)
                dve(eng.tensor_copy(place[:, :, :], place_id[:, :, :]).then_inc(dve_done, 1), dve_done)
                eng.wait_ge(*dve.latest)
                dve(ts(keep["pick_round"][:, :, :], place[:, :, :], float(SLOTS), None, ALU.is_ge).then_inc(dve_done, 1), dve_done)
                for later in range(2, ROUNDS):
                    eng.wait_ge(*dve.latest)
                    dve(stt(keep["pick_round"][:, :, :], place[:, :, :], float(SLOTS * later), keep["pick_round"][:, :, :],
                            ALU.is_ge, ALU.add).then_inc(dve_done, 1), dve_done)
                eng.wait_ge(*dve.latest)
                dve(stt(row[:, :, :], row[:, :, :], float(SLOTS), place[:, :, :], ALU.mult, ALU.add).then_inc(dve_done, 1), dve_done)
                eng.wait_ge(*dve.latest)
                dve(stt(row[:, :, :], keep["pick_round"][:, :, :], -float(SLOTS), row[:, :, :], ALU.mult, ALU.add).then_inc(dve_done, 1), dve_done)
                eng.wait_ge(*dve.latest)
                dve(eng.tensor_copy(keep["pick_row"][:, :, :], row[:, :, :]).then_inc(dve_done, 1), dve_done)
            elif kind == "sg":
                i = a[0]
                eng.wait_ge(dve_bank_full, V.nth(step))
                eng.wait_ge(silu_done, i + 1)
                dve(tt(h[:, i % 2, :], silu[:, i % 2, :], V.bank(step)[:, 256:512], ALU.mult).then_inc(dve_bank_copied, 1), dve_bank_copied)
                eng.wait_ge(*dve.latest)
                dve(eng.memset(flag[:, :], 0.0).then_inc(h_ready, 1), h_ready)
            elif kind == "sd":
                i, half = a
                eng.wait_ge(dve_bank_full, V.nth(step))
                b = V.bank(step)
                eng.wait_ge(scaled, 1)
                xs = x[:, i, 512 * half:512 * half + 512]
                dve(tt(xs, xs, b[:, :], ALU.add).then_inc(dve_bank_copied, 1), dve_bank_copied)

    @block.tensor
    def _(eng):
        mm = eng.matmul

        def chain(out, pairs):
            for n, (lhs, rhs) in enumerate(pairs):
                ins = mm(out, lhs, rhs, start=n == 0, stop=n == len(pairs) - 1)
            return ins

        def flip(out, src):
            return eng.transpose(out, src, ident[:, :])

        for step in plan:
            kind, a = step[0], step[1:]
            if kind == "xt":
                ring, full, copied = (A, act_bank_full, act_bank_copied) if step in A.number else (V, dve_bank_full, dve_bank_copied)
                if ring.reused(step):
                    eng.wait_ge(copied, ring.last_user(step))
                b = ring.bank(step)
                for i in range(4):
                    ins = flip(b[:, toks(i)], x[:, i, :].rearrange("p (m k) -> p k m", k=8)[:, a[0], :])
                ins.then_inc(full, 1)
            elif kind == "rt":
                eng.wait_ge(act_bank_copied, A.nth(("xt", 7)))
                eng.wait_ge(dve_bank_copied, V.nth(("xt", 6)))
                eng.wait_ge(router_in, 32)
                if A.reused(step):
                    eng.wait_ge(act_bank_copied, A.last_user(step))
                b = A.bank(step)
                chain(b[:, 0:64], [(x1T[:, k, toks(a[0])], w_router[:, k, :]) for k in range(8)]).then_inc(act_bank_full, 1)
            elif kind == "sg":
                eng.wait_ge(shared_gu_in, 32)
                if V.reused(step):
                    eng.wait_ge(dve_bank_copied, V.last_user(step))
                b = V.bank(step)
                chain(b[:, :], [(x1T[:, k, toks(a[0])], sh_gu[:, k, :]) for k in range(8)]).then_inc(dve_bank_full, 1)
            elif kind == "sh":
                i = a[0]
                if A.reused(step):
                    eng.wait_ge(act_bank_copied, A.last_user(step))
                b = A.bank(step)
                eng.wait_ge(h_ready, i + 1)
                for k in range(2):
                    ins = flip(b[:, toks(k)], h[:, i % 2, toks(k)])
                ins.then_inc(act_bank_full, 1)
            elif kind == "sd":
                i, half = a
                eng.wait_ge(act_bank_copied, A.nth(("sh", i)))
                eng.wait_ge(shared_dn_in, 16)
                if V.reused(step):
                    eng.wait_ge(dve_bank_copied, V.last_user(step))
                b = V.bank(step)
                chain(b[:, :], [(hT[:, i % 2, k, :], sh_dn[:, k, 512 * half:512 * half + 512]) for k in range(2)]).then_inc(dve_bank_full, 1)
            elif kind == "cnt":
                i = a[0]
                if V.reused(step):
                    eng.wait_ge(dve_bank_copied, V.last_user(step))
                b = V.bank(step)
                eng.wait_ge(chosen, i + 1)
                eng.wait_ge(tables_in, 48)
                chain(b[:, 0:64], [(ones[:, :], sel[:, j, :]) for j in range(i)] + [(before[:, :], sel[:, i, :])]).then_inc(dve_bank_full, 1)
            elif kind == "tot":
                if V.reused(step):
                    eng.wait_ge(dve_bank_copied, V.last_user(step))
                b = V.bank(step)
                chain(b[:, 0:64], [(ones[:, :], sel[:, j, :]) for j in range(4)]).then_inc(dve_bank_full, 1)


def build_more_rounds(nc, T, layer, W, keep):
    most = nc.values_load(keep["most"][0:1, 0:1], min_val=0, max_val=512)
    engines = (nc.sync, nc.scalar, nc.vector, nc.gpsimd, nc.tensor)
    with nc.If(most > SLOTS):
        with nc.Fori(1, ROUNDS) as r:
            with nc.If(most > r * SLOTS):
                phase(nc, build_experts, T, layer, W, keep, r)
                phase(nc, build_combination, T, keep)
            with nc.Else():
                for e in engines:
                    e.nop()
            nc.all_engine_barrier()
    with nc.Else():
        for e in engines:
            e.nop()
    nc.all_engine_barrier()


def expert_weights(W, layer, keep, e, j):
    return [(keep["w_gu"][:, j, 0, :, :], W["exp_w_gate"][layer].rearrange("e (p k) n -> e p k n", p=P)[e]),
            (keep["w_gu"][:, j, 1, :, :], W["exp_w_up"][layer].rearrange("e (p k) n -> e p k n", p=P)[e]),
            (keep["w_dn"][:, j, :, :], W["exp_w_down"][layer].rearrange("e (k p) n -> e p k n", p=P)[e])]


def build_experts(nc, ctx, T, layer, W, keep, r, sem):
    n_exp = W["exp_w_gate"].shape[1]
    R = EXPERT_RING
    first_round = isinstance(r, int)
    prefix = "expert_" if first_round else "more_expert_"
    ident = keep["ident"]

    def sb(name, shape, dt=F32):
        return ctx.enter_context(nc.sbuf_tensor(prefix + name, shape, dt))

    w_gu, w_dn = keep["w_gu"], keep["w_dn"]
    tokens, token_col = sb("tokens", [SLOTS, n_exp], I32), sb("token_col", [SLOTS, 2], I32)
    xg, xgT = sb("xg", [SLOTS, 2, 1024]), sb("xgT", [P, 2, 8, SLOTS])
    silu, h, hT = sb("silu", [SLOTS, 2, 256]), sb("h", [SLOTS, 2, 256]), sb("hT", [P, 2, SLOTS])
    y = sb("y", [SLOTS, 2, 1024])
    bx = [ctx.enter_context(nc.psum_tensor(prefix + f"x_bank{n}", [P, 4 * SLOTS], F32)) for n in range(2)]
    bg = [ctx.enter_context(nc.psum_tensor(prefix + f"gu_bank{n}", [SLOTS, 512], F32)) for n in range(2)]
    bh = ctx.enter_context(nc.psum_tensor(prefix + "h_bank", [P, 2 * SLOTS], F32))
    by = [ctx.enter_context(nc.psum_tensor(prefix + f"y_bank{n}", [SLOTS, 512], F32)) for n in range(2)]

    tokens_in, ple_in = sem("tokens_in"), sem("ple_gate_half_in")
    gu_in, dn_in = [sem(f"gate_up_in{n}") for n in range(R)], [sem(f"down_in{n}") for n in range(R)]
    col_ready, col_seen = sem("token_col_ready"), sem("token_col_seen")
    x_in = [sem(f"x_in{n}") for n in range(2)]
    x_full, x_copied = [sem(f"xT_full{n}") for n in range(2)], [sem(f"xT_copied{n}") for n in range(2)]
    gu_full, silu_done, h_ready, h_full, h_copied = (
        sem(n) for n in ("gate_up_full", "silu_done", "h_ready", "hT_full", "hT_copied"))
    y_full, y_copied = [sem(f"y_full{n}") for n in range(2)], [sem(f"y_copied{n}") for n in range(2)]
    y_stored = [sem(f"y_stored{n}") for n in range(2)]

    def expert_loop(eng, body):
        with eng.Fori(0, n_exp // R - 1) as i:
            for j in range(R):
                body(i * R + j, i, j, R)
        for j in range(R):
            body(n_exp - R + j, n_exp // R - 1, j, R - 1 - j)

    block = ctx.enter_context(nc.Block())

    @block.sync
    def _(sp):
        def load_gu(e, j):
            for dst, src in expert_weights(W, layer, keep, e, j)[0:2]:
                sp.dma_start(dst, src).then_inc(gu_in[j], 16)

        def load_dn(e, j):
            dst, src = expert_weights(W, layer, keep, e, j)[2]
            sp.dma_start(dst, src).then_inc(dn_in[j], 16)

        table = T["token_table"].rearrange("(r s e) o -> r s (e o)", s=SLOTS, e=n_exp)
        sp.dma_start(tokens[:, :], table[r]).then_inc(tokens_in, 16)
        for n in range(2):
            sp.nop().then_inc(y_stored[n], 16)
        for j in range(R):
            sp.nop().then_inc(gu_in[j], 32)
            sp.nop().then_inc(dn_in[j], 16)

        def body(e, i, j, left):
            more = left == R
            if more or not first_round:
                sp.wait_ge(gu_full, e + 1)
                load_gu(e + R if more else j, j)
                sp.wait_ge(y_full[1], e + 1)
                load_dn(e + R if more else j, j)
            if first_round and not more and j == 0:
                sp.dma_start(keep["ple_gate_half"][:, :, :],
                             W["ple_gate_w"][layer].rearrange("(p k) n -> p k n", p=P)[:, :, 0:512]).then_inc(ple_in, 16)
            for n in range(2):
                sp.wait_ge(y_copied[n], e + 2)
            sp.dma_start(T["y_dram"][e], y[:, j % 2, :]).then_inc(y_stored[j % 2], 16)

        expert_loop(sp, body)
        for n in range(2):
            sp.wait_ge(y_stored[n], 16 * (n_exp // 2 + 1))
        if first_round:
            sp.wait_ge(ple_in, 16)
        else:
            for j in range(R):
                sp.wait_ge(gu_in[j], 32 * (n_exp // R + 1))
                sp.wait_ge(dn_in[j], 16 * (n_exp // R + 1))

    @block.gpsimd
    def _(pool):
        def gather(e, b):
            pool.tensor_copy(token_col[:, b:b + 1], tokens[:, bass.ds(e, 1)]).then_inc(col_ready, 1)
            pool.wait_ge(col_ready, e + 1)
            pool.sem_inc(col_seen, 1)
            pool.indirect_dma_start(xg[:, b, :], None, T["x1_dram"],
                                    bass.IndirectOffsetOnAxis(token_col[:, b:b + 1], 0)).then_inc(x_in[b], 16)

        pool.wait_ge(tokens_in, 16)
        gather(0, 0)
        gather(1, 1)

        def body(e, i, j, left):
            if left >= 2:
                pool.wait_ge(x_full[1], e + 1)
                gather(e + 2, j % 2)

        expert_loop(pool, body)

    @block.tensor
    def _(pe):
        def flip_x(e, i, j):
            b = j % 2
            pe.wait_ge(x_in[b], i * 16 * (R // 2) + 16 * (j // 2 + 1))
            for n in range(2):
                pe.wait_ge(x_copied[n], e + 1)
                for k in range(4):
                    src = xg[:, b, :].rearrange("p (m k) -> p k m", k=8)[:, 4 * n + k, :]
                    ins = pe.transpose(bx[n][:, k * SLOTS:(k + 1) * SLOTS], src, ident[0:SLOTS, 0:SLOTS])
                ins.then_inc(x_full[n], 1)

        def gate_up(e, i, j):
            b = j % 2
            pe.wait_ge(gu_in[j], i * 32 + 32)
            pe.wait_ge(h_ready, e + 1)
            for k in range(8):
                if k % 4 == 0:
                    pe.wait_ge(x_copied[k // 4], e + 2)
                ins = pe.matmul(bg[b][:, :].rearrange("p (a n) -> p a n", a=2), xgT[:, b, k, :], w_gu[:, j, :, k, :],
                                start=k == 0, stop=k == 7)
            ins.then_inc(gu_full, 1)

        def body(e, i, j, left):
            b = j % 2
            pe.wait_ge(h_ready, e + 3)
            pe.wait_ge(h_copied, e + 1)
            for k in range(2):
                ins = pe.transpose(bh[:, k * SLOTS:(k + 1) * SLOTS], h[:, b, k * P:(k + 1) * P], ident[0:SLOTS, 0:SLOTS])
            ins.then_inc(h_full, 1)
            if left >= 1:
                gate_up(e + 1, i + (j + 1) // R, (j + 1) % R)
            if left >= 2:
                flip_x(e + 2, i + (j + 2) // R, (j + 2) % R)
            pe.wait_ge(h_copied, e + 2)
            pe.wait_ge(dn_in[j], i * 16 + 16)
            for n in range(2):
                pe.wait_ge(y_copied[n], e + 1)
                for k in range(2):
                    ins = pe.matmul(by[n][:, :], hT[:, k, :], w_dn[:, j, k, 512 * n:512 * n + 512], start=k == 0, stop=k == 1)
                ins.then_inc(y_full[n], 1)

        flip_x(0, 0, 0)
        gate_up(0, 0, 0)
        flip_x(1, 0, 1)
        expert_loop(pe, body)

    @block.scalar
    def _(act):
        for s in (x_copied[0], h_copied, y_copied[0]):
            act.nop().then_inc(s, 1)

        def take_x(e, j):
            act.wait_ge(x_full[0], e + 1)
            act.copy(xgT[:, j % 2, 0:4, :].rearrange("p a b -> p (a b)"), bx[0][:, :]).then_inc(x_copied[0], 1)

        def gate(e, j):
            act.wait_ge(gu_full, e + 1)
            act.activation(silu[:, j % 2, :], bg[j % 2][:, 0:256], ACT.Silu).then_inc(silu_done, 1)

        take_x(0, 0)
        gate(0, 0)
        take_x(1, 1)

        def body(e, i, j, left):
            act.wait_ge(h_full, e + 1)
            act.copy(hT[:, :, :].rearrange("p a b -> p (a b)"), bh[:, :]).then_inc(h_copied, 1)
            if left >= 1:
                gate(e + 1, j + 1)
            if left >= 2:
                take_x(e + 2, j)
            act.wait_ge(y_full[0], e + 1)
            act.wait_ge(y_stored[j % 2], i * 16 * (R // 2) + 16 * (j // 2 + 1))
            act.copy(y[:, j % 2, 0:512], by[0][:, :]).then_inc(y_copied[0], 1)

        expert_loop(act, body)

    @block.vector
    def _(dve):
        dve.nop().then_inc(h_ready, 2)
        for s in (x_copied[1], y_copied[1]):
            dve.nop().then_inc(s, 1)

        def take_x(e, j):
            dve.wait_ge(x_full[1], e + 1)
            dve.tensor_copy(xgT[:, j % 2, 4:8, :].rearrange("p a b -> p (a b)"), bx[1][:, :]).then_inc(x_copied[1], 1)

        def hidden(e, j):
            dve.wait_ge(silu_done, e + 1)
            dve.tensor_tensor(h[:, j % 2, :], silu[:, j % 2, :], bg[j % 2][:, 256:512], ALU.mult).then_inc(h_ready, 1)

        take_x(0, 0)
        hidden(0, 0)
        take_x(1, 1)

        def body(e, i, j, left):
            if left >= 1:
                hidden(e + 1, j + 1)
            if left >= 2:
                take_x(e + 2, j)
            dve.wait_ge(y_full[1], e + 1)
            dve.wait_ge(y_stored[j % 2], i * 16 * (R // 2) + 16 * (j // 2 + 1))
            dve.tensor_copy(y[:, j % 2, 512:1024], by[1][:, :]).then_inc(y_copied[1], 1)

        expert_loop(dve, body)


def build_combination(nc, ctx, T, keep, sem):
    x = keep["x"]
    NB = 8
    rows = ctx.enter_context(nc.sbuf_tensor("combine_rows", [P, NB, 1024], F32))
    w_now = ctx.enter_context(nc.sbuf_tensor("combine_w", [P, 4, 8], F32))
    row_in = [sem(f"row_in{n}") for n in range(NB)]
    added, dve_done = sem("row_added"), sem("dve_done")
    block = ctx.enter_context(nc.Block())
    y_rows = T["y_dram"].rearrange("e s d -> (e s) d")

    @block.gpsimd
    def _(pool):
        for i in range(4):
            for k in range(TOP_K):
                n = i * TOP_K + k
                if n >= NB:
                    pool.wait_ge(added, n - NB + 1)
                pool.indirect_dma_start(rows[:, n % NB, :], None, y_rows,
                                        bass.IndirectOffsetOnAxis(keep["pick_row"][:, i, k:k + 1], 0)).then_inc(row_in[n % NB], 16)

    @block.vector
    def _(eng):
        dve = Count()
        dve(eng.tensor_scalar(w_now[:, :, :], keep["pick_round"][:, :, :], keep["round_now"][:, :], None, ALU.is_equal).then_inc(dve_done, 1), dve_done)
        eng.wait_ge(*dve.latest)
        dve(eng.tensor_tensor(w_now[:, :, :], w_now[:, :, :], keep["pick_w"][:, :, :], ALU.mult).then_inc(dve_done, 1), dve_done)
        dve(eng.tensor_scalar(keep["round_now"][:, :], keep["round_now"][:, :], 1.0, None, ALU.add).then_inc(dve_done, 1), dve_done)
        for i in range(4):
            for k in range(TOP_K):
                n = i * TOP_K + k
                eng.wait_ge(row_in[n % NB], 16 * (n // NB + 1))
                eng.wait_ge(*dve.latest)
                dve(eng.scalar_tensor_tensor(x[:, i, :], rows[:, n % NB, :], w_now[:, i, k:k + 1], x[:, i, :],
                                             ALU.mult, ALU.add).then_inc(added, 1), added)


def finish_plan():
    ple = [[("pg", i, 0), ("pp", i, 0), ("pg", i, 1), ("pp", i, 1)] for i in range(4)]
    return (ple[0][0:1] + [("pt", 0), ("pt", 1)] + ple[0][1:] + [("rows", 0)] + ple[1] + [("rows", 1), ("ln2", 0)] + ple[2]
            + [("rows", 2), ("ln2", 1)] + ple[3] + [("ln2", 2), ("row_sums", 3), ("ln2", 3)])


def build_finish(nc, ctx, T, layer, W, keep, sem):
    x, x1T, ident, eps = keep["x"], keep["x1T"], keep["ident"], keep["eps"]
    plan = finish_plan()
    keys_act = [s for s in plan if s[0] in ("pt", "pg")]
    keys_dve = [s for s in plan if s[0] == "pp"]
    NB = 12

    def sb(name, shape, dt=F32):
        return ctx.enter_context(nc.sbuf_tensor("finish_" + name, shape, dt))

    ple_w, ple_gate = sb("ple_w", [P, 2, 1024]), [keep["ple_gate_half"], sb("ple_gate_half", [P, 8, 512])]
    p_nat, pT = sb("p_nat", [P, 4, 256]), sb("pT", [P, 2, 512])
    gate = sb("ple_sigmoid", [P, 4, 512])
    diag = sb("diag", [P, TOP_K, P])
    rows, w_now = sb("rows", [P, NB, 1024]), sb("w_now", [P, 4, 8])
    ln_g, ln_b = sb("ln_g", [P, 1024]), sb("ln_b", [P, 1024])
    stats, mv, rstd = sb("stats", [P, 12]), sb("mv", [P, 2]), sb("rstd", [P, 1])

    pa = [ctx.enter_context(nc.psum_tensor(f"finish_act_bank{n}", [P, 512], F32)) for n in range(2)]
    sums = [ctx.enter_context(nc.psum_tensor(f"finish_row_sums{n}", [P, 512], F32)) for n in range(2)]
    pv = [ctx.enter_context(nc.psum_tensor(f"finish_dve_bank{n}", [P, 512], F32)) for n in range(4)]
    A, V = Ring(pa, keys_act), Ring(pv, keys_dve)
    act_bank_full, act_bank_copied = sem("act_bank_full"), sem("act_bank_copied")
    dve_bank_full, dve_bank_copied = sem("dve_bank_full"), sem("dve_bank_copied")
    dve_done = sem("dve_done")
    ple_gate_in = sem("ple_gate_in")
    ple_w_in, p_in, ln_in = (sem(n) for n in ("ple_w_in", "p_in", "ln_rows_in"))
    summed, added = sem("embedding_added"), sem("row_added")
    w_ready, diag_ready, rows_summed = (sem(n) for n in ("round_weights_ready", "diagonals_ready", "rows_summed"))
    var_ready, sd_ready, tile_done, stored = (sem(n) for n in ("ln_var_ready", "ln_sd_ready", "ln2_tile_ready", "out_stored"))
    row_in = [sem(f"row_in{n}") for n in range(NB)]

    def toks(i, n=P):
        return slice(i * n, i * n + n)

    block = ctx.enter_context(nc.Block())

    @block.sync
    def _(eng):
        def load(dst, src, done):
            eng.dma_start(dst, src).then_inc(done, 16)

        load(p_nat[:, :, :], W["p"][layer, 0].rearrange("(i p) n -> p i n", p=P), p_in)
        load(ple_w[:, :, :], W["ple_w"][layer].rearrange("(k p) n -> p k n", p=P), ple_w_in)
        load(ple_gate[1][:, :, :], W["ple_gate_w"][layer].rearrange("(p k) n -> p k n", p=P)[:, :, 512:1024], ple_gate_in)
        load(ln_g[:, :], W["ln2_g"][layer].partition_broadcast(P), ln_in)
        load(ln_b[:, :], W["ln2_b"][layer].partition_broadcast(P), ln_in)
        for i in range(4):
            eng.wait_ge(tile_done, i + 1)
            load(T["out"][0, toks(i), :], x[:, i, :], stored)
        eng.wait_ge(stored, 64)

    @block.gpsimd
    def _(pool):
        y_rows = T["y_dram"].rearrange("e s d -> (e s) d")
        for i in range(4):
            for k in range(TOP_K):
                n = i * TOP_K + k
                if n >= NB:
                    pool.wait_ge(added, n - NB + 1)
                pool.indirect_dma_start(rows[:, n % NB, :], None, y_rows,
                                        bass.IndirectOffsetOnAxis(keep["pick_row"][:, i, k:k + 1], 0)).then_inc(row_in[n % NB], 16)

    @block.scalar
    def _(eng):
        act = Count()
        n_gate = 0
        eng.wait_ge(w_ready, 1)
        for k in range(TOP_K):
            act(eng.mul(diag[:, k, :], ident[:, :], w_now[:, 3, k:k + 1]).then_inc(diag_ready, 1), diag_ready)
        for step in plan:
            kind, a = step[0], step[1:]
            if kind == "pt":
                eng.wait_ge(act_bank_full, A.nth(step))
                b = A.bank(step)
                act(eng.copy(pT[:, a[0], :], b[:, :]).then_inc(act_bank_copied, 1), act_bank_copied)
            elif kind == "pg":
                if n_gate >= 4:
                    eng.wait_ge(summed, n_gate - 3)
                eng.wait_ge(act_bank_full, A.nth(step))
                b = A.bank(step)
                act(eng.activation(gate[:, n_gate % 4, :], b[:, :], ACT.Sigmoid).then_inc(act_bank_copied, 1), act_bank_copied)
                n_gate += 1
            elif kind == "ln2":
                eng.wait_ge(var_ready, a[0] + 1)
                act(eng.activation(rstd[:, :], mv[:, 1:2], ACT.Sqrt, bias=eps[:, 0:1]).then_inc(sd_ready, 1), sd_ready)

    @block.vector
    def _(eng):
        dve = Count()
        tt, ts, stt = eng.tensor_tensor, eng.tensor_scalar, eng.scalar_tensor_tensor
        n_gate = 0
        dve(ts(w_now[:, :, :], keep["pick_round"][:, :, :], 0.0, None, ALU.is_equal).then_inc(dve_done, 1), dve_done)
        eng.wait_ge(*dve.latest)
        dve(tt(w_now[:, :, :], w_now[:, :, :], keep["pick_w"][:, :, :], ALU.mult).then_inc(w_ready, 1), w_ready)
        for step in plan:
            kind, a = step[0], step[1:]
            eng.wait_ge(*dve.latest)
            if kind == "pp":
                i, half = a
                eng.wait_ge(dve_bank_full, V.nth(step))
                b = V.bank(step)
                eng.wait_ge(act_bank_copied, A.nth(("pg", i, half)))
                g = gate[:, n_gate % 4, :]
                n_gate += 1
                dve(tt(g, g, b[:, :], ALU.mult).then_inc(dve_bank_copied, 1), dve_bank_copied)
                eng.wait_ge(*dve.latest)
                xs = x[:, i, 512 * half:512 * half + 512]
                dve(tt(xs, xs, g, ALU.add).then_inc(summed, 1), summed)
            elif kind == "rows":
                i = a[0]
                for k in range(TOP_K):
                    n = i * TOP_K + k
                    eng.wait_ge(row_in[n % NB], 16 * (n // NB + 1))
                    eng.wait_ge(*dve.latest)
                    dve(stt(x[:, i, :], rows[:, n % NB, :], w_now[:, i, k:k + 1], x[:, i, :], ALU.mult, ALU.add).then_inc(added, 1), added)
            elif kind == "row_sums":
                i = a[0]
                eng.wait_ge(rows_summed, 1)
                dve(tt(x[:, i, 0:512], x[:, i, 0:512], sums[0][:, :], ALU.add).then_inc(dve_done, 1), dve_done)
                dve(tt(x[:, i, 512:1024], x[:, i, 512:1024], sums[1][:, :], ALU.add).then_inc(dve_done, 1), dve_done)
            elif kind == "ln2":
                i = a[0]
                if i == 0:
                    eng.wait_ge(ln_in, 32)
                layer_norm_tile(dve, eng, dve_done, sd_ready, var_ready, i, x[:, i, :], x[:, i, :], ln_g[:, :], ln_b[:, :],
                                stats[:, :], mv[:, :], rstd[:, :], tile_done)

    @block.tensor
    def _(eng):
        mm = eng.matmul

        def chain(out, pairs):
            for n, (lhs, rhs) in enumerate(pairs):
                ins = mm(out, lhs, rhs, start=n == 0, stop=n == len(pairs) - 1)
            return ins

        def flip(out, src):
            return eng.transpose(out, src, ident[:, :])

        for step in plan:
            kind, a = step[0], step[1:]
            if kind == "pt":
                eng.wait_ge(p_in, 16)
                if A.reused(step):
                    eng.wait_ge(act_bank_copied, A.last_user(step))
                b = A.bank(step)
                for i in range(4):
                    ins = flip(b[:, toks(i)], p_nat[:, i, toks(a[0])])
                ins.then_inc(act_bank_full, 1)
            elif kind == "pg":
                i, half = a
                if half:
                    eng.wait_ge(ple_gate_in, 16)
                if A.reused(step):
                    eng.wait_ge(act_bank_copied, A.last_user(step))
                b = A.bank(step)
                chain(b[:, :], [(x1T[:, k, toks(i)], ple_gate[half][:, k, :]) for k in range(8)]).then_inc(act_bank_full, 1)
            elif kind == "pp":
                i, half = a
                eng.wait_ge(act_bank_copied, A.nth(("pt", 1)))
                eng.wait_ge(ple_w_in, 16)
                if V.reused(step):
                    eng.wait_ge(dve_bank_copied, V.last_user(step))
                b = V.bank(step)
                chain(b[:, :], [(pT[:, k, toks(i)], ple_w[:, k, 512 * half:512 * half + 512]) for k in range(2)]).then_inc(dve_bank_full, 1)
            elif kind == "row_sums":
                i = a[0]
                eng.wait_ge(diag_ready, TOP_K)
                for k in range(TOP_K):
                    n = i * TOP_K + k
                    eng.wait_ge(row_in[n % NB], 16 * (n // NB + 1))
                    for half in range(2):
                        ins = mm(sums[half][:, :], diag[:, k, :], rows[:, n % NB, 512 * half:512 * half + 512],
                                 start=k == 0, stop=k == TOP_K - 1)
                ins.then_inc(rows_summed, 1)


def phase(nc, build, *args):
    with ExitStack() as ctx:
        sems = []

        def sem(name):
            sems.append(ctx.enter_context(nc.semaphore(name)))
            return sems[-1]

        with ExitStack() as inner:
            build(nc, inner, *args, sem)
        nc.gpsimd.dma_reset()
        nc.all_engine_barrier()
        engines = (nc.sync, nc.scalar, nc.vector, nc.tensor)
        for n, s in enumerate(sems):
            engines[n % 4].sem_clear(s)
        nc.all_engine_barrier()


def build_constants(nc, ctx, T, keep, sem):
    loaded, made = sem("tables_loaded"), sem("constants_made")
    block = ctx.enter_context(nc.Block())
    names = [n for n in keep if n in T and n != "x"]

    @block.sync
    def _(eng):
        eng.dma_start(keep["x"][:, :, :], T["x"][0].rearrange("(i p) d -> p i d", p=P)).then_inc(loaded, 16)
        for n in names:
            dims = len(keep[n].shape)
            eng.dma_start(keep[n][(slice(None),) * dims], T[n]).then_inc(loaded, 16)
        eng.wait_ge(loaded, 16 * (len(names) + 1))
        eng.wait_ge(made, 4)

    @block.vector
    def _(eng):
        eng.memset(keep["ones"][:, :], 1.0).then_inc(made, 1)
        for n, v in enumerate((LN_EPS, RMS_EPS, TWO_PI / 4)):
            eng.memset(keep["eps"][:, n:n + 1], v).then_inc(made, 1)


def prog(nc, W, T):
    depth = W["w_in"].shape[0]
    T["alpha"] = (2 * depth) ** 0.25
    with ExitStack() as ctx:
        def sb(name, shape, dt=F32):
            return ctx.enter_context(nc.sbuf_tensor(name, shape, dt))

        keep = {
            "x": sb("x_now", [P, 4, 1024]), "ident": sb("ident", [P, P]), "ones": sb("ones", [P, P]),
            "eps": sb("eps", [P, 3]), "centre": sb("centre", [P, P]), "half_swap": sb("half_swap", [P, P]),
            "rope_cos": sb("rope_cos", [P, 512]), "rope_sin": sb("rope_sin", [P, 512]),
            "chunk_keep": sb("chunk_keep", [P, 512]), "gla_causal": sb("gla_causal", [P, 4, P], I32),
            "pick_w": sb("pick_w", [P, 4, 8]), "pick_row": sb("pick_row", [P, 4, 8], I32), "most": sb("most", [P, 1], I32),
            "pick_round": sb("pick_round", [P, 4, 8]), "round_now": sb("round_now", [P, 1]),
        }
        T["x1_dram"] = nc.dram_tensor("x1_scratch", (512, 1024), F32, kind="Internal").ap()
        T["token_table"] = nc.dram_tensor("token_table", (ROUNDS * SLOTS * 64, 1), I32, kind="Internal").ap()
        T["y_dram"] = nc.dram_tensor("y_scratch", (64, SLOTS, 1024), F32, kind="Internal").ap()
        phase(nc, build_constants, T, keep)
        with nc.Fori(0, depth) as layer:
            phase(nc, build_mixers, T, layer, W, keep)
            with ExitStack() as shared:
                keep["x1T"] = shared.enter_context(nc.sbuf_tensor("x1T", [P, 8, 512], F32))
                keep["ple_gate_half"] = shared.enter_context(nc.sbuf_tensor("ple_gate_half", [P, 8, 512], F32))
                with ExitStack() as ring:
                    keep["w_gu"] = ring.enter_context(nc.sbuf_tensor("expert_w_gu", [P, EXPERT_RING, 2, 8, 256], F32))
                    keep["w_dn"] = ring.enter_context(nc.sbuf_tensor("expert_w_dn", [P, EXPERT_RING, 2, 1024], F32))
                    phase(nc, build_routing, T, layer, W, keep)
                    build_more_rounds(nc, T, layer, W, keep)
                    phase(nc, build_experts, T, layer, W, keep, 0)
                phase(nc, build_finish, T, layer, W, keep)


_INS = ['x', 'p', 'w_in', 's5_a_re', 's5_a_im', 's5_log_dt', 's5_b_re', 's5_b_im', 's5_c_re', 's5_c_im', 's5_d',
        's5_w_glu', 'swa_sinks', 'gla_w_lr2', 'gla_b_lr', 'gla_norm_g', 'mla_q_norm_g', 'mla_w_uq', 'mla_kv_norm_g',
        'mla_w_ukv', 'w_branch', 'w_out', 'ln1_g', 'ln1_b', 'router_w', 'router_bias', 'exp_w_gate', 'exp_w_up',
        'exp_w_down', 'sh_w_gate', 'sh_w_up', 'sh_w_down', 'ple_w', 'ple_gate_w', 'ln2_g', 'ln2_b']
_OUTS = [((1, 512, 1024), 'float32')]


def kernel(**inputs):
    import numpy as _np
    import concourse.bacc as _bacc
    from concourse import mybir as _mybir
    from concourse.bass_utils import run_bass_kernel_spmd as _run

    nc = _bacc.Bacc("TRN2", target_bir_lowering=False, num_devices=1)
    arrays, weights, tables = {}, {}, {}
    for name in _INS:
        a = _np.ascontiguousarray(inputs[name])
        arrays[f"in_{name}_dram"] = a
        weights[name] = nc.dram_tensor(f"in_{name}_dram", a.shape, _mybir.dt.from_np(a.dtype), kind="ExternalInput").ap()
    for name, a in shape_constants().items():
        a = _np.ascontiguousarray(a)
        arrays[f"const_{name}_dram"] = a
        tables[name] = nc.dram_tensor(f"const_{name}_dram", a.shape, _mybir.dt.from_np(a.dtype), kind="ExternalInput").ap()
    outs = []
    for i, (shape, dtype) in enumerate(_OUTS):
        dt = _mybir.dt.from_np(_np.dtype(dtype))
        outs.append(nc.dram_tensor(f"out_{i}_dram", shape, dt, kind="ExternalOutput").ap())
    tables["x"], tables["out"] = weights["x"], outs[0]
    prog(nc, weights, tables)
    r = _run(nc, [arrays], core_ids=[0])
    got = tuple(r.results[0][f"out_{i}_dram"] for i in range(len(_OUTS)))
    return got[0]
```
